# Optimizing a Trainium2 kernel written in Bass

```python
import math
import jax, jax.numpy as jnp
from jax import lax
import numpy as np

D_MODEL = 1024
BATCH = 1
SEQ = 1024
DEPTH = 1

POOL_GROUPS = 4
POOL_GROUP_CH = D_MODEL // 8
POOL_WIDTH = POOL_GROUPS * POOL_GROUP_CH
POOL_WINDOWS = (2, 4, 8, 16)
N_Q_HEADS = 8
N_KV_HEADS = 2
GQA_GROUP = N_Q_HEADS // N_KV_HEADS
HEAD_DIM = 64
Q_WIDTH = N_Q_HEADS * HEAD_DIM
KV_WIDTH = N_KV_HEADS * HEAD_DIM
WINDOW = 128
ATT_BLOCK = 128
D_IN = POOL_WIDTH + Q_WIDTH + 2 * KV_WIDTH + 2 * D_MODEL
V_START = POOL_WIDTH + Q_WIDTH + KV_WIDTH
V_END = V_START + KV_WIDTH
SPLIT_POINTS = (POOL_WIDTH, POOL_WIDTH + Q_WIDTH, POOL_WIDTH + Q_WIDTH + KV_WIDTH, V_END, V_END + D_MODEL)
N_EXPERTS = 64
EXPERT_FF = D_MODEL // 4
TOP_K = 8
N_EXPERT_GROUPS = 8
EXPERTS_PER_GROUP = N_EXPERTS // N_EXPERT_GROUPS
TOPK_GROUPS = 4
ROUTED_SCALE = 2.5
MOE_BLOCK = 256
ALPHA = (2.0 * DEPTH) ** 0.25
BETA = (8.0 * DEPTH) ** -0.25
LN_EPS = 1e-5

kernel_name = 'hybrid_pool_swa_moe_deepnorm'

def _layer_norm(x, g, b):
    xf = x.astype(jnp.float32)
    mu = xf.mean(-1, keepdims=True)
    var = jnp.square(xf - mu).mean(-1, keepdims=True)
    y = (xf - mu) * lax.rsqrt(var + LN_EPS)
    return (y * g.astype(jnp.float32) + b.astype(jnp.float32)).astype(x.dtype)

def _alibi_slopes():
    return jnp.asarray(2.0 ** (-8.0 * np.arange(1, N_Q_HEADS + 1) / N_Q_HEADS), dtype=jnp.float32)

def _pool_mixer(u, w_pool, pool_scale):
    B, S, _ = u.shape
    c = jnp.cumsum(u.astype(jnp.float32), axis=1)
    c = jnp.concatenate([jnp.zeros((B, 1, POOL_WIDTH), jnp.float32), c], axis=1)
    t1 = jnp.arange(1, S + 1, dtype=jnp.float32)[:, None]
    means = []
    for gi, w in enumerate(POOL_WINDOWS):
        cg = c[:, :, gi * POOL_GROUP_CH:(gi + 1) * POOL_GROUP_CH]
        lo = jnp.concatenate([jnp.zeros((B, w - 1, POOL_GROUP_CH), jnp.float32), cg[:, :S + 1 - w]], axis=1)
        means.append((cg[:, 1:] - lo) / jnp.minimum(t1, float(w)))
    pooled = jnp.stack(means, axis=2)
    ug = u.reshape(B, S, POOL_GROUPS, POOL_GROUP_CH).astype(jnp.float32)
    mixed = jnp.einsum('bsgc,gcd->bsgd', (pooled - ug).astype(u.dtype), w_pool)
    return mixed.reshape(B, S, POOL_WIDTH) * pool_scale

def _sliding_window_attention(q, k, v, sinks):
    B, S = q.shape[0], q.shape[1]
    nb = S // ATT_BLOCK
    qb = q.reshape(B, nb, ATT_BLOCK, N_KV_HEADS, GQA_GROUP, HEAD_DIM)

    def banded(t):
        cur = t.reshape(B, nb, ATT_BLOCK, N_KV_HEADS, HEAD_DIM)
        prev = jnp.concatenate([jnp.zeros_like(cur[:, :1]), cur[:, :-1]], axis=1)
        return jnp.concatenate([prev, cur], axis=2)

    kb, vb = banded(k), banded(v)
    s = jnp.einsum('bnqhgd,bnkhd->bnhgqk', qb, kb).astype(jnp.float32) * (HEAD_DIM ** -0.5)
    qi = jnp.arange(ATT_BLOCK)[:, None]
    kj = jnp.arange(2 * ATT_BLOCK)[None, :]
    dist = ATT_BLOCK + qi - kj
    key_pos = jnp.arange(nb)[:, None, None] * ATT_BLOCK - ATT_BLOCK + kj[None]
    valid = (dist >= 0) & (dist < WINDOW) & (key_pos >= 0)
    slopes = _alibi_slopes().reshape(N_KV_HEADS, GQA_GROUP, 1, 1)
    s = s - slopes * dist.astype(jnp.float32)
    s = jnp.where(valid[None, :, None, None], s, -jnp.inf)
    sink = sinks.astype(jnp.float32).reshape(1, 1, N_KV_HEADS, GQA_GROUP, 1, 1)
    m = jnp.maximum(s.max(-1, keepdims=True), sink)
    p = jnp.exp(s - m)
    denom = p.sum(-1, keepdims=True) + jnp.exp(sink - m)
    o = jnp.einsum('bnhgqk,bnkhd->bnqhgd', (p / denom).astype(v.dtype), vb)
    return o.reshape(B, S, Q_WIDTH)

def _mixer(x, w_in, b_in, w_pool, pool_scale, sinks, w_br_pool, w_br_attn, w_out):
    B, S, _ = x.shape
    h = jnp.einsum('bsd,de->bse', x, w_in) + b_in
    u, q, k, v, g_pool, g_attn = jnp.split(h, list(SPLIT_POINTS), axis=-1)
    y_pool = jnp.einsum('bsp,pd->bsd', _pool_mixer(u, w_pool, pool_scale), w_br_pool)
    o = _sliding_window_attention(q.reshape(B, S, N_Q_HEADS, HEAD_DIM),
                                  k.reshape(B, S, N_KV_HEADS, HEAD_DIM),
                                  v.reshape(B, S, N_KV_HEADS, HEAD_DIM), sinks)
    y_attn = jnp.einsum('bse,ed->bsd', o, w_br_attn)
    merged = jax.nn.sigmoid(g_pool) * y_pool + jax.nn.sigmoid(g_attn) * y_attn
    return jnp.einsum('bsd,de->bse', merged, w_out)

def _swiglu(x, wg, wu, wd):
    return jnp.dot(jax.nn.silu(jnp.dot(x, wg)) * jnp.dot(x, wu), wd)

def _moe(x, w_router, router_bias, w_eg, w_eu, w_ed, w_sg, w_su, w_sd):
    B, S, D = x.shape
    T = B * S
    xt = x.reshape(T, D)
    scores = jax.nn.sigmoid(jnp.dot(xt, w_router).astype(jnp.float32))
    biased = scores + router_bias.astype(jnp.float32)
    grp_score = lax.top_k(biased.reshape(T, N_EXPERT_GROUPS, EXPERTS_PER_GROUP), 2)[0].sum(-1)
    _, top_groups = lax.top_k(grp_score, TOPK_GROUPS)
    grp_keep = jax.nn.one_hot(top_groups, N_EXPERT_GROUPS, dtype=jnp.float32).sum(1) > 0
    expert_keep = jnp.repeat(grp_keep, EXPERTS_PER_GROUP, axis=1)
    _, top_e = lax.top_k(jnp.where(expert_keep, biased, -jnp.inf), TOP_K)
    sel = jnp.take_along_axis(scores, top_e, axis=1)
    gates = sel / sel.sum(-1, keepdims=True) * ROUTED_SCALE
    A = T * TOP_K
    e_flat = top_e.reshape(A).astype(jnp.int32)
    tok_flat = jnp.repeat(jnp.arange(T, dtype=jnp.int32), TOP_K)
    g_flat = gates.reshape(A)
    order = jnp.argsort(e_flat, stable=True)
    e_s, tok_s, g_s = e_flat[order], tok_flat[order], g_flat[order]
    counts = jnp.bincount(e_flat, length=N_EXPERTS)
    starts = jnp.cumsum(counts) - counts
    pcounts = (counts + MOE_BLOCK - 1) // MOE_BLOCK * MOE_BLOCK
    pends = jnp.cumsum(pcounts)
    pstarts = pends - pcounts
    dest = pstarts[e_s] + (jnp.arange(A, dtype=jnp.int32) - starts[e_s])
    n_pad = -(-A // MOE_BLOCK) * MOE_BLOCK + N_EXPERTS * MOE_BLOCK
    n_blocks = n_pad // MOE_BLOCK
    buf_tok = jnp.full((n_pad,), T, jnp.int32).at[dest].set(tok_s)
    buf_gate = jnp.zeros((n_pad,), jnp.float32).at[dest].set(g_s)
    blk_expert = jnp.minimum(jnp.searchsorted(pends, jnp.arange(n_blocks, dtype=jnp.int32) * MOE_BLOCK, side='right'),
                             N_EXPERTS - 1).astype(jnp.int32)
    x_pad = jnp.concatenate([xt, jnp.zeros((1, D), xt.dtype)], axis=0)

    def expert_block(acc, blk):
        tok_b, gate_b, e = blk
        xb = x_pad[tok_b]
        yb = _swiglu(xb, w_eg[e], w_eu[e], w_ed[e]) * gate_b[:, None].astype(xb.dtype)
        return acc.at[tok_b].add(yb), None

    acc, _ = lax.scan(expert_block, jnp.zeros((T + 1, D), x.dtype),
                      (buf_tok.reshape(n_blocks, MOE_BLOCK), buf_gate.reshape(n_blocks, MOE_BLOCK), blk_expert))
    y = acc[:T] + _swiglu(xt, w_sg, w_su, w_sd)
    return y.reshape(B, S, D)

def setup_inputs(seed: int = 0) -> dict:
    key = jax.random.key(seed)
    ks = jax.random.split(key, 24)

    def nrm(k, shape, scale):
        return jax.random.normal(k, shape, jnp.float32) * scale

    col_scale = np.ones((D_IN,), np.float32)
    col_scale[V_START:V_END] = BETA
    return {
        'x': nrm(ks[0], (BATCH, SEQ, D_MODEL), 1.0),
        'ln0_g': 1.0 + nrm(ks[1], (D_MODEL,), 0.02),
        'ln0_b': nrm(ks[2], (D_MODEL,), 0.02),
        'w_in': nrm(ks[3], (DEPTH, D_MODEL, D_IN), D_MODEL ** -0.5) * jnp.asarray(col_scale),
        'b_in': nrm(ks[4], (DEPTH, D_IN), 0.02),
        'w_pool': nrm(ks[5], (DEPTH, POOL_GROUPS, POOL_GROUP_CH, POOL_GROUP_CH), POOL_GROUP_CH ** -0.5),
        'pool_scale': 1.0 + nrm(ks[6], (DEPTH, POOL_WIDTH), 0.02),
        'attn_sinks': nrm(ks[7], (DEPTH, N_Q_HEADS), 0.5),
        'w_br_pool': nrm(ks[8], (DEPTH, POOL_WIDTH, D_MODEL), POOL_WIDTH ** -0.5),
        'w_br_attn': nrm(ks[9], (DEPTH, Q_WIDTH, D_MODEL), Q_WIDTH ** -0.5),
        'w_out': nrm(ks[10], (DEPTH, D_MODEL, D_MODEL), D_MODEL ** -0.5 * BETA),
        'ln1_g': 1.0 + nrm(ks[11], (DEPTH, D_MODEL), 0.02),
        'ln1_b': nrm(ks[12], (DEPTH, D_MODEL), 0.02),
        'w_router': nrm(ks[13], (DEPTH, D_MODEL, N_EXPERTS), D_MODEL ** -0.5),
        'router_bias': nrm(ks[14], (DEPTH, N_EXPERTS), 0.01),
        'w_exp_gate': nrm(ks[15], (DEPTH, N_EXPERTS, D_MODEL, EXPERT_FF), D_MODEL ** -0.5),
        'w_exp_up': nrm(ks[16], (DEPTH, N_EXPERTS, D_MODEL, EXPERT_FF), D_MODEL ** -0.5),
        'w_exp_down': nrm(ks[17], (DEPTH, N_EXPERTS, EXPERT_FF, D_MODEL), EXPERT_FF ** -0.5 * BETA),
        'w_sh_gate': nrm(ks[18], (DEPTH, D_MODEL, EXPERT_FF), D_MODEL ** -0.5),
        'w_sh_up': nrm(ks[19], (DEPTH, D_MODEL, EXPERT_FF), D_MODEL ** -0.5),
        'w_sh_down': nrm(ks[20], (DEPTH, EXPERT_FF, D_MODEL), EXPERT_FF ** -0.5 * BETA),
        'ln2_g': 1.0 + nrm(ks[21], (DEPTH, D_MODEL), 0.02),
        'ln2_b': nrm(ks[22], (DEPTH, D_MODEL), 0.02),
    }

def reference(x, ln0_g, ln0_b, w_in, b_in, w_pool, pool_scale, attn_sinks, w_br_pool, w_br_attn, w_out,
              ln1_g, ln1_b, w_router, router_bias, w_exp_gate, w_exp_up, w_exp_down,
              w_sh_gate, w_sh_up, w_sh_down, ln2_g, ln2_b):
    x = _layer_norm(x, ln0_g, ln0_b)
    for l in range(DEPTH):
        mix = _mixer(x, w_in[l], b_in[l], w_pool[l], pool_scale[l], attn_sinks[l],
                     w_br_pool[l], w_br_attn[l], w_out[l])
        x = _layer_norm(ALPHA * x + mix, ln1_g[l], ln1_b[l])
        ffn = _moe(x, w_router[l], router_bias[l], w_exp_gate[l], w_exp_up[l], w_exp_down[l],
                   w_sh_gate[l], w_sh_up[l], w_sh_down[l])
        x = _layer_norm(ALPHA * x + ffn, ln2_g[l], ln2_b[l])
    return x


_drawn_inputs = setup_inputs


def setup_inputs(seed=0):
    import zlib

    import numpy as np

    out = dict(_drawn_inputs(seed))
    spreads = {}
    factors = {'pool_scale': 2.881, 'attn_sinks': 23.079, 'ln2_g': 7.566, 'ln2_b': 7.778, 'b_in': 2.723}
    for name, (base, spread) in spreads.items():
        noise = np.random.default_rng([zlib.crc32(name.encode()), seed]).standard_normal(out[name].shape)
        drawn = base * np.exp(spread * noise) if base else spread * noise
        out[name] = __import__('jax').numpy.asarray(drawn.astype(out[name].dtype))
    for name, factor in factors.items():
        out[name] = (out[name] * factor).astype(out[name].dtype)
    return out
```

```python
import concourse.bass as bass
from concourse import mybir
from contextlib import ExitStack

T, D, P = 1024, 1024, 128
NT = T // P
ND = D // P
POOL_G = 4
HEADS, HD = 8, 64
QC = HEADS * HD // P
D_IN = 3328
K_COL, V_COL, GP_COL, GA_COL = 1024, 1152, 1280, 2304
NE, FF = 64, 256
NF = FF // P
TOPK = 8
GROUPS, PER_GROUP, KEEP_GROUPS = 8, 8, 4
ROUTED_SCALE = 2.5
ALPHA = 2.0 ** 0.25
EPS = 1e-5
HALF = 512

CS = 80
NC = 2
SLOTS = CS * NC
MAX_OVER = T * TOPK // SLOTS
MAX_OVER += MAX_OVER % 2
NTAB = NE + MAX_OVER + 4
FAR = 16384.0
LIST = 6
NEG = -1.0e30


def build(nc, x, ln0_g, ln0_b, w_in, b_in, w_pool, pool_scale, attn_sinks, w_br_pool, w_br_attn,
          w_out, ln1_g, ln1_b, w_router, router_bias, w_exp_gate, w_exp_up, w_exp_down, w_sh_gate,
          w_sh_up, w_sh_down, ln2_g, ln2_b, out):
    f32, f32r, bf16, i32 = mybir.dt.float32, mybir.dt.float32r, mybir.dt.bfloat16, mybir.dt.int32
    ALU, ACT, AX = mybir.AluOpType, mybir.ActivationFunctionType, mybir.AxisListType

    x_t = x[0].rearrange("(t p) d -> t p d", p=P)
    out_t = out[0].rearrange("(t p) d -> t p d", p=P)
    win = w_in[0].rearrange("(p c) e -> p c e", c=ND)
    wg_e = w_exp_gate[0].rearrange("e (p c) f -> e p c f", c=ND)
    wu_e = w_exp_up[0].rearrange("e (p c) f -> e p c f", c=ND)
    wd_e = w_exp_down[0].rearrange("e (c p) d -> e p c d", p=P)
    x1_dram = nc.dram_tensor("x1_rows", (T + SLOTS, D), f32, kind="Internal").ap()
    acc_dram = nc.dram_tensor("acc_rows", (T + SLOTS, D), f32, kind="Internal").ap()

    ctx = ExitStack()
    with ctx:
        base = 16512
        KB = 1024

        def at(name, offset, shape, dt=f32):
            return nc.alloc_sbuf_tensor_at(name, shape, dt, offset=base + offset)

        def sem(name):
            return ctx.enter_context(nc.semaphore(name))

        xT = at("xT", 0, [P, ND, T])
        xh = at("xh", 32 * KB, [P, NT, D])
        mergedT = at("mergedT", 64 * KB, [P, ND, T])
        xin = at("xin", 64 * KB, [P, 2, D])
        S_sb = at("S_sb", 72 * KB, [P, HEADS, 2 * P])
        PT = at("PT", 80 * KB, [P, 2 * HEADS, P])
        o_sb = at("o_sb", 88 * KB, [P, HEADS * HD])
        uT = at("uT", 96 * KB, [P, POOL_G, T])
        pdiff = at("pdiff", 112 * KB, [P, POOL_G, T])
        wo_a = at("wo_a", 112 * KB, [P, ND, HALF])
        qT = at("qT", 128 * KB, [P, QC, T])
        kT = at("kT", 144 * KB, [P, 2, T])
        v_sb = at("v_sb", 152 * KB, [P, NT, P])
        WRING = 6
        wst = at("wst", 156 * KB, [P, WRING, ND, P])
        wo_b = at("wo_b", 180 * KB, [P, ND, HALF])
        ladder = at("ladder", 180 * KB, [P, 2, T])
        g1b = at("g1b", 188 * KB + 8 * KB, [P, D])
        c0 = 200 * KB
        b1b = at("b1b", c0, [P, D])
        ident = at("ident", c0 + 4096, [P, P])
        dist = at("dist", c0 + 4608, [P, 2 * P])
        cols = at("cols", c0 + 5632, [P, 64])
        small = at("small", c0 + 5888, [P, 160])
        mean_var = small[:, 96:112].rearrange("p (t s) -> p t s", t=NT)
        std = small[:, 112:120]
        eps = small[:, 120:121]
        rows = at("rows", 92 * KB, [P, P])
        vbias = at("vbias", 92 * KB + 512, [P, P])
        inv = at("inv", 93 * KB, [P, POOL_G, 16])
        gate_sb = at("gate_sb", 144 * KB, [P, 4, HALF])

        W = [at(f"W{j}", (96 + 24 * j) * KB, [P, 3 * 2048]) for j in range(2)]
        Wsh = at("Wsh", 144 * KB, [P, 3 * 2048])
        hsh = at("hsh", 64 * KB, [P, NF, T])
        sig_sh = at("sig_sh", 72 * KB, [P, 2, HALF])
        r0 = 76 * KB
        wr = at("wr", r0, [P, ND, NE])
        scores = at("scores", r0 + 2048, [P, NT, NE])
        biased = at("biased", r0 + 4096, [P, NT, NE])
        work = at("work", r0 + 6144, [P, NT, NE])
        mask = at("mask", r0 + 8192, [P, NT, NE])
        maskb = at("maskb", r0 + 10240, [P, NT, NE], bf16)
        gates = at("gates", r0 + 11264, [P, NT, NE])
        gpart = at("gpart", r0 + 13312, [P, NT, NE])
        top = at("top", r0 + 15360, [P, NT, GROUPS, 8])
        gs = at("gs", r0 + 17408, [P, NT, GROUPS])
        gtop = at("gtop", r0 + 17664, [P, NT, 8])
        etop = at("etop", r0 + 17920, [P, NT, 8])
        rbias = at("rbias", r0 + 18176, [P, NE])
        gsum = at("gsum", r0 + 18432, [P, NT])
        l0 = 168 * KB
        posm = at("posm", l0, [P, NE, NT])
        vlist = at("vlist", l0 + 2 * KB, [P, NE, NT, LIST], bf16)
        iotas = at("iotas", l0 + 8 * KB, [P, SLOTS])
        tri = at("tri", l0 + 9 * KB, [P, P], bf16)
        ones = at("ones", l0 + 9 * KB + 256, [P, P], bf16)
        etab = at("etab", l0 + 10 * KB, [P, NTAB], i32)
        etabf = at("etabf", l0 + 10 * KB + 512, [P, NTAB])
        btab = at("btab", l0 + 11 * KB, [P, NTAB])
        n_pairs = at("n_pairs", l0 + 11 * KB + 512, [P, 2], i32)
        trash = at("trash", l0 + 11 * KB + 544, [P, 2, NC])
        extra = at("extra", l0 + 12 * KB, [P, 4, NE])
        over = at("over", l0 + 13 * KB, [P, 4, MAX_OVER])
        cmp = at("cmp", 0, [P, MAX_OVER, NE])
        zrow = at("zrow", l0 + 14 * KB, [P, D])
        gidx = [at(f"gidx{j}", l0 + 18 * KB + 64 * j, [P, NC], i32) for j in range(2)]
        sidx = [at(f"sidx{j}", l0 + 18 * KB + 128 + 64 * j, [P, NC], i32) for j in range(2)]
        lst = [at(f"lst{j}", l0 + 18 * KB + 256 + 64 * j, [P, NC, 2]) for j in range(2)]
        sgate = [at(f"sgate{j}", l0 + 18 * KB + 384 + 64 * j, [P, NC, 1]) for j in range(2)]
        tmp = at("tmp", l0 + 18 * KB + 512, [P, NC, 1])
        onehot = at("onehot", 16 * KB, [P, NT, SLOTS], bf16)
        xg = [at(f"xg{j}", (20 + 8 * j) * KB, [P, NC, D]) for j in range(2)]
        xgT = [at(f"xgT{j}", (36 + 5 * j) * KB, [P, ND, SLOTS]) for j in range(2)]
        sig = at("sig", 46 * KB, [P, NF, SLOTS])
        h_full = at("h_full", 48 * KB, [P, NF, SLOTS])
        h_hi = [at(f"h_hi{j}", (66 + 4 * j) * KB, [P, NF, SLOTS], f32r) for j in range(2)]
        h_lo = [at(f"h_lo{j}", (68 + 4 * j) * KB, [P, NF, SLOTS], f32r) for j in range(2)]
        wd_hi = at("wd_hi", 0, [P, NF, D], f32r)
        wd_lo = at("wd_lo", 8 * KB, [P, NF, D], f32r)
        ysb = [at(f"ysb{j}", (50 + 8 * j) * KB, [P, NC, D]) for j in range(2)]
        accin = at("accin", 96 * KB, [P, NT, D])
        g2b = at("g2b", 128 * KB, [P, D])
        b2b = at("b2b", 132 * KB, [P, D])

        bank = [ctx.enter_context(nc.psum_tensor(f"bank{i}", [P, HALF], f32)) for i in range(8)]

        BIN_ROWS = D_IN // P
        C_G0, C_B0 = BIN_ROWS + 1 + POOL_G, BIN_ROWS + 1 + POOL_G + ND
        C_KSW, C_PS = BIN_ROWS, BIN_ROWS + 1
        NROWS = BIN_ROWS + 1 + POOL_G

        consts_loaded = sem("consts_loaded")
        rows_loaded = sem("rows_loaded")
        x_loaded = [sem(f"x_loaded{j}") for j in range(2)]
        ident_ready = sem("ident_ready")
        dve_chain = sem("dve_chain")
        act_chain = sem("act_chain")
        pool_chain = sem("pool_chain")
        rows_T = sem("rows_T")
        cols_ready = sem("cols_ready")
        xhat_ready = sem("xhat_ready")
        tr_ready = sem("tr_ready")
        tr_taken = sem("tr_taken")
        w_loaded = [sem(f"w_loaded{j}") for j in range(WRING)]
        proj_ready = sem("proj_ready")
        proj_taken = sem("proj_taken")
        wp_loaded = sem("wp_loaded")
        pdiff_ready = sem("pdiff_ready")
        ladder_ready = sem("ladder_ready")
        mixed_ready = sem("mixed_ready")
        mixed_taken = sem("mixed_taken")
        x0_ready = sem("x0_ready")
        sc_ready = sem("sc_ready")
        sc_taken = sem("sc_taken")
        negm_ready = sem("negm_ready")
        exp_done = sem("exp_done")
        pt_ready = sem("pt_ready")
        pt_taken = sem("pt_taken")
        o_ready = sem("o_ready")
        o_scaled = sem("o_scaled")
        oT_ready = sem("oT_ready")
        oT_taken = sem("oT_taken")
        mw_loaded = [sem(f"mw_loaded{j}") for j in range(2)]
        mg_ready = sem("mg_ready")
        sg_ready = sem("sg_ready")
        merged_ready = sem("merged_ready")
        wo_loaded = sem("wo_loaded")
        mix_ready = sem("mix_ready")
        mix_taken = sem("mix_taken")
        ln1_ready = sem("ln1_ready")
        x1_ready = sem("x1_ready")
        x1T_ready = sem("x1T_ready")
        x1T_taken = sem("x1T_taken")
        x1_stored = sem("x1_stored")
        r_loaded = sem("r_loaded")
        logits_ready = sem("logits_ready")
        score_ready = sem("score_ready")
        mask_ready = sem("mask_ready")
        pos_ready = sem("pos_ready")
        pool_consts = sem("pool_consts")
        shw_loaded = sem("shw_loaded")
        sh_ready = sem("sh_ready")
        sh_sig = sem("sh_sig")
        sh_h = sem("sh_h")
        shd_ready = sem("shd_ready")
        acc_ready = sem("acc_ready")
        acc_stored = sem("acc_stored")
        tables_ready = sem("tables_ready")
        gu_loaded = [sem(f"gu_loaded{j}") for j in range(2)]
        wd_loaded = [sem(f"wd_loaded{j}") for j in range(2)]
        onehot_ready = sem("onehot_ready")
        list_ready = sem("list_ready")
        idx_ready = sem("idx_ready")
        gathered = [sem(f"gathered{j}") for j in range(2)]
        xgT_ready = sem("xgT_ready")
        xgT_taken = sem("xgT_taken")
        gu_ready = sem("gu_ready")
        sig_ready = sem("sig_ready")
        h_ready = sem("h_ready")
        h_ready_full = sem("h_ready_full")
        h_hi_ready = sem("h_hi_ready")
        wd_hi_ready = sem("wd_hi_ready")
        wd_split = sem("wd_split")
        y_ready = sem("y_ready")
        y_taken_dve = sem("y_taken_dve")
        y_taken_act = sem("y_taken_act")
        sidx_ready = sem("sidx_ready")
        scattered = [sem(f"scattered{j}") for j in range(2)]
        pool_turn = sem("pool_turn")
        acc_loaded = [sem(f"acc_loaded{t}") for t in range(NT)]
        g2_loaded = sem("g2_loaded")
        out_ready = sem("out_ready")
        out_scaled = sem("out_scaled")
        out_stored = sem("out_stored")
        last_chain = sem("last_chain")
        var_ready = sem("var_ready")
        std_ready = sem("std_ready")

        def score_place(h, w):
            o = (h // 2 % 2) * 2 * P
            return bank[2 * (h % 2) + h // 4][:, o:o + w]

        def wait(engine, semaphore, value):
            if not isinstance(value, int) or value > 0:
                engine.wait_ge(semaphore, value)

        def behind(step, it, j):
            if j:
                step(it, 0)
            elif not isinstance(it, int) or it > 0:
                step(it - 1, 1)

        N_CONST = 5
        feature_chunks = [("u", g, g * P) for g in range(POOL_G)] + \
                         [("q", c, 512 + c * P) for c in range(QC)] + [("k", 0, K_COL), ("k", 1, None)]
        NPROJ = 1 + len(feature_chunks)
        block = ctx.enter_context(nc.Block())

        @block.sync
        def _(sp):
            sp.dma_start(rows[0:BIN_ROWS, :], b_in[0].rearrange("(r n) -> r n", n=P)).then_inc(rows_loaded, 16)
            sp.dma_start(rows[C_KSW:C_KSW + 1, 0:HD], b_in[0:1, K_COL + HD:K_COL + P]).then_inc(rows_loaded, 16)
            sp.dma_start(rows[C_KSW:C_KSW + 1, HD:P], b_in[0:1, K_COL:K_COL + HD]).then_inc(rows_loaded, 16)
            sp.dma_start(rows[C_PS:C_PS + POOL_G, :], pool_scale[0].rearrange("(r n) -> r n", n=P)).then_inc(rows_loaded, 16)
            sp.dma_start(cols[:, C_G0:C_G0 + ND], ln0_g.rearrange("(p c) -> p c", c=ND)).then_inc(rows_loaded, 16)
            sp.dma_start(cols[:, C_B0:C_B0 + ND], ln0_b.rearrange("(p c) -> p c", c=ND)).then_inc(rows_loaded, 16)
            for t in range(NT):
                if t >= 2:
                    sp.wait_ge(xhat_ready, t - 1)
                sp.dma_start(xin[:, t % 2, :], x_t[t]).then_inc(x_loaded[t % 2], 16)
                if t == 1:
                    sp.dma_start(vbias[:, :], b_in[0:1, V_COL:V_COL + P].to_broadcast([P, P])).then_inc(consts_loaded, 16)
                    sp.dma_start(small[:, 0:HEADS], attn_sinks[0:1, :].to_broadcast([P, HEADS])).then_inc(consts_loaded, 16)
                    sp.dma_start(g1b[:, :], ln0_g.rearrange("(a n) -> a n", a=1).to_broadcast([P, D])).then_inc(consts_loaded, 16)
                    sp.dma_start(b1b[:, :], ln0_b.rearrange("(a n) -> a n", a=1).to_broadcast([P, D])).then_inc(consts_loaded, 16)
                    sp.dma_start(o_sb[:, :].rearrange("p (g d) -> p g d", g=POOL_G),
                                 w_pool[0].rearrange("g c d -> c g d")).then_inc(consts_loaded, 16)
            for n in range(NPROJ):
                dst = wst[:, n % WRING, :, :]
                if n >= WRING:
                    sp.wait_ge(proj_ready, NT + 2 * (n - WRING))
                if n == 0:
                    sp.dma_start(dst, win[:, :, V_COL:V_COL + P]).then_inc(w_loaded[n % WRING], 16)
                elif feature_chunks[n - 1][2] is None:
                    sp.dma_start(dst[:, :, 0:HD], win[:, :, K_COL + HD:K_COL + P]).then_inc(w_loaded[n % WRING], 16)
                    sp.dma_start(dst[:, :, HD:P], win[:, :, K_COL:K_COL + HD]).then_inc(w_loaded[n % WRING], 16)
                else:
                    c = feature_chunks[n - 1][2]
                    sp.dma_start(dst, win[:, :, c:c + P]).then_inc(w_loaded[n % WRING], 16)
            sp.wait_ge(proj_ready, NT + 2 * (NPROJ - 1))
            for c in range(ND):
                if c >= 2:
                    sp.wait_ge(mg_ready, 8 * (c - 1))
                j = c % 2
                sp.dma_start(wst[:, 3 * j, :, :], win[:, :, GP_COL + c * P:GP_COL + (c + 1) * P]).then_inc(mw_loaded[j], 16)
                sp.dma_start(wst[:, 3 * j + 1, :, :], win[:, :, GA_COL + c * P:GA_COL + (c + 1) * P]).then_inc(mw_loaded[j], 16)
                for h, w in ((0, w_br_pool), (1, w_br_attn)):
                    sp.dma_start(wst[:, 3 * j + 2, 4 * h:4 * h + 4, :],
                                 w[0].rearrange("(k p) d -> p k d", p=P)[:, :, c * P:(c + 1) * P]).then_inc(mw_loaded[j], 16)
                if c == 1:
                    sp.wait_ge(mixed_ready, 2 * POOL_G)
                    wo = w_out[0].rearrange("(k p) e -> p k e", p=P)
                    sp.dma_start(wo_a[:, :, :], wo[:, :, 0:HALF]).then_inc(wo_loaded, 16)
                    sp.dma_start(wo_b[:, :, :], wo[:, :, HALF:D]).then_inc(wo_loaded, 16)
                if c == 2:
                    sp.wait_ge(x0_ready, NT)
                    sp.dma_start(g1b[:, :], ln1_g[0:1, :].to_broadcast([P, D])).then_inc(r_loaded, 16)
                    sp.dma_start(b1b[:, :], ln1_b[0:1, :].to_broadcast([P, D])).then_inc(r_loaded, 16)
            sp.wait_ge(mix_ready, 1)
            sp.wait_ge(merged_ready, 2 * ND)
            sp.dma_start(Wsh[:, 0:2048].rearrange("p (c f) -> p c f", c=ND), w_sh_gate[0].rearrange("(p c) f -> p c f", c=ND)).then_inc(shw_loaded, 16)
            sp.dma_start(Wsh[:, 2048:4096].rearrange("p (c f) -> p c f", c=ND), w_sh_up[0].rearrange("(p c) f -> p c f", c=ND)).then_inc(shw_loaded, 16)
            sp.dma_start(Wsh[:, 4096:6144].rearrange("p (c d) -> p c d", c=NF), w_sh_down[0].rearrange("(c p) d -> p c d", p=P)).then_inc(shw_loaded, 16)
            sp.wait_ge(mix_ready, 2 * NT)
            sp.dma_start(wr[:, :, :], w_router[0].rearrange("(p c) e -> p c e", c=ND)).then_inc(r_loaded, 16)
            sp.dma_start(rbias[:, :], router_bias[0:1, :].to_broadcast([P, NE])).then_inc(r_loaded, 16)

            def load_expert(j, e):
                w = W[j]
                sp.dma_start(w[:, 0:2048].rearrange("p (c f) -> p c f", c=ND), wg_e[e]).then_inc(gu_loaded[j], 16)
                sp.dma_start(w[:, 2048:4096].rearrange("p (c f) -> p c f", c=ND), wu_e[e]).then_inc(gu_loaded[j], 16)
                sp.dma_start(w[:, 4096:6144].rearrange("p (c d) -> p c d", c=NF), wd_e[e]).then_inc(wd_loaded[j], 16)

            for j in range(2):
                load_expert(j, j)
            for t in range(NT):
                sp.wait_ge(x1_ready, t + 1)
                sp.dma_start(x1_dram[t * P:(t + 1) * P, :], xh[:, t, :]).then_inc(x1_stored, 16)
            sp.wait_ge(pool_consts, 3)
            for d in (x1_dram, acc_dram):
                sp.dma_start(d[T:T + P, :], zrow[:, :]).then_inc(x1_stored, 16)
                sp.dma_start(d[T + P:T + SLOTS, :], zrow[0:SLOTS - P, :]).then_inc(x1_stored, 16)
            for t in range(NT):
                sp.wait_ge(acc_ready, t + 1)
                sp.dma_start(acc_dram[t * P:(t + 1) * P, :], xh[:, t, :]).then_inc(acc_stored, 16)
            sp.wait_ge(tables_ready, 1)
            pairs = sp.value_load(n_pairs[0:1, 0:1], min_val=NE // 2, max_val=(NE + MAX_OVER) // 2)
            with sp.Fori(0, pairs - 1) as it:
                for j in range(2):
                    e = sp.value_load(etab[0:1, bass.ds(it * 2 + (j + 2), 1)], min_val=0, max_val=NE - 1)
                    w = W[j]
                    sp.wait_ge(wd_split, it * 2 + (j + 1))
                    sp.dma_start(w[:, 4096:6144].rearrange("p (o c d) -> p o c d", o=1, c=NF),
                                 wd_e[bass.ds(e, 1)].rearrange("e p c d -> p e c d")).then_inc(wd_loaded[j], 16)
                    sp.wait_ge(gu_ready, it * 2 + (j + 1))
                    sp.dma_start(w[:, 0:2048].rearrange("p (o c f) -> p o c f", o=1, c=ND),
                                 wg_e[bass.ds(e, 1)].rearrange("e p c f -> p e c f")).then_inc(gu_loaded[j], 16)
                    sp.dma_start(w[:, 2048:4096].rearrange("p (o c f) -> p o c f", o=1, c=ND),
                                 wu_e[bass.ds(e, 1)].rearrange("e p c f -> p e c f")).then_inc(gu_loaded[j], 16)
            sp.wait_ge(y_ready, pairs * 8)
            sp.dma_start(g2b[:, :], ln2_g[0:1, :].to_broadcast([P, D])).then_inc(g2_loaded, 16)
            sp.dma_start(b2b[:, :], ln2_b[0:1, :].to_broadcast([P, D])).then_inc(g2_loaded, 16)
            for j in range(2):
                sp.wait_ge(scattered[j], pairs * 32)
            for t in range(NT):
                sp.dma_start(accin[:, t, :], acc_dram[t * P:(t + 1) * P, :]).then_inc(acc_loaded[t], 16)
            for t in range(NT):
                sp.wait_ge(out_scaled, t + 1)
                sp.dma_start(out_t[t], accin[:, t, :]).then_inc(out_stored, 16)
            sp.wait_ge(out_stored, 16 * NT)

        @block.gpsimd
        def _(pool):
            gp = nc.gpsimd
            n = [0]

            def link(ins):
                n[0] += 1
                ins.then_inc(pool_chain, 1)
                pool.wait_ge(pool_chain, n[0])

            link(gp.memset(eps[:, :], EPS))
            link(gp.memset(ident[:, :], 0.0))
            gp.affine_select(out=ident[:, :], in_=ident[:, :], compare_op=ALU.not_equal, fill=1.0, base=0,
                             pattern=[[-1, P]], channel_multiplier=1).then_inc(ident_ready, 1)
            link(gp.iota(dist[:, :], [[-1, 2 * P]], base=P, channel_multiplier=1, allow_small_or_imprecise_dtypes=True))
            link(gp.affine_select(out=dist[:, :], in_=dist[:, :], compare_op=ALU.is_ge, fill=1.0e32, base=P,
                                  pattern=[[-1, 2 * P]], channel_multiplier=1))
            link(gp.affine_select(out=dist[:, :], in_=dist[:, :], compare_op=ALU.is_ge, fill=1.0e32, base=-1,
                                  pattern=[[1, 2 * P]], channel_multiplier=-1))
            gp.iota(inv[:, :, :], [[0, POOL_G], [1, 16]], base=1, channel_multiplier=0,
                    allow_small_or_imprecise_dtypes=True).then_inc(ident_ready, 1)
            for g in range(POOL_G):
                pool.wait_ge(proj_taken, NT + 2 * (g + 1))
                if g >= 1:
                    pool.wait_ge(pdiff_ready, g)
                src = uT[:, g, :]
                for s in range(g + 1):
                    k = 1 << s
                    dst = ladder[:, s % 2, :]
                    link(gp.tensor_copy(dst[:, 0:k], src[:, 0:k]))
                    add = gp.tensor_tensor(dst[:, k:T], src[:, k:T], src[:, 0:T - k], ALU.add)
                    if s < g:
                        link(add)
                    else:
                        add.then_inc(ladder_ready, 1)
                    src = dst
            pool.wait_ge(consts_loaded, 16 * N_CONST)
            pool.wait_ge(tr_ready, 2 * NT)
            for t in range(NT):
                link(gp.tensor_tensor(xh[:, t, :], xh[:, t, :], g1b[:, :], ALU.mult))
                gp.tensor_tensor(xh[:, t, :], xh[:, t, :], b1b[:, :], ALU.add).then_inc(x0_ready, 1)
            pool.wait_ge(r_loaded, 32)
            for t in range(NT):
                pool.wait_ge(ln1_ready, t + 1)
                link(gp.tensor_tensor(xh[:, t, :], xh[:, t, :], g1b[:, :], ALU.mult))
                gp.tensor_tensor(xh[:, t, :], xh[:, t, :], b1b[:, :], ALU.add).then_inc(x1_ready, 1)
                if t == NT - 1:
                    pool.wait_ge(mix_ready, 2 * NT)
                    gp.memset(zrow[:, :], 0.0).then_inc(pool_consts, 1)
                    gp.iota(iotas[:, :], [[1, SLOTS]], base=0, channel_multiplier=0, allow_small_or_imprecise_dtypes=True).then_inc(pool_consts, 1)
                    link(gp.memset(tri[:, :], 1.0))
                    gp.affine_select(out=tri[:, :], in_=tri[:, :], compare_op=ALU.is_gt, fill=0.0, base=0,
                                     pattern=[[1, P]], channel_multiplier=-1).then_inc(pool_consts, 1)
                    gp.memset(ones[:, :], 1.0).then_inc(pool_consts, 1)
                    gp.iota(trash[:, 0, :], [[CS, NC]], base=T, channel_multiplier=1, allow_small_or_imprecise_dtypes=True).then_inc(pool_consts, 1)
                    gp.iota(trash[:, 1, :], [[-CS, NC]], base=-T, channel_multiplier=-1, allow_small_or_imprecise_dtypes=True).then_inc(pool_consts, 1)
                    gp.iota(vlist[:, :, :, 0], [[0, NE], [P, NT]], base=0, channel_multiplier=0, allow_small_or_imprecise_dtypes=True).then_inc(pool_consts, 1)
                    gp.iota(vlist[:, :, :, 1], [[0, NE], [0, NT]], base=0, channel_multiplier=1, allow_small_or_imprecise_dtypes=True).then_inc(pool_consts, 1)
                    gp.memset(vlist[:, :, :, 2], 1.0).then_inc(pool_consts, 1)
                    gp.iota(over[:, 0, :], [[1, MAX_OVER]], base=0, channel_multiplier=0, allow_small_or_imprecise_dtypes=True).then_inc(pool_consts, 1)
                    gp.iota(etabf[:, 0:NE], [[1, NE]], base=0, channel_multiplier=0, allow_small_or_imprecise_dtypes=True).then_inc(pool_consts, 1)
            pool.wait_ge(tables_ready, 1)
            pool.wait_ge(x1_stored, 16 * (NT + 4))
            pairs = pool.value_load(n_pairs[0:1, 0:1], min_val=NE // 2, max_val=(NE + MAX_OVER) // 2)

            def gather(j):
                for c in range(NC):
                    gp.indirect_dma_start(out=xg[j][0:CS, c, :], out_offset=None, in_=x1_dram[:, :],
                                          in_offset=bass.IndirectOffsetOnAxis(ap=gidx[j][0:CS, c:c + 1], axis=0)
                                          ).then_inc(gathered[j], 16)

            pool.wait_ge(acc_stored, 16 * NT)
            for j in range(2):
                pool.wait_ge(idx_ready, j + 1)
                gather(j)
            def scatter(it, j):
                wait(pool, y_taken_dve, it * 4 + 2 * (j + 1))
                wait(pool, y_taken_act, it * 4 + 2 * (j + 1))
                wait(pool, scattered[1 - j], it * 32 + 32 * j)
                pool.sem_inc(pool_turn, 1)
                for c in range(NC):
                    gp.indirect_dma_start(out=acc_dram[:, :],
                                          out_offset=bass.IndirectOffsetOnAxis(ap=sidx[j][0:CS, c:c + 1], axis=0),
                                          in_=ysb[j][0:CS, c, :], in_offset=None,
                                          compute_op=ALU.add).then_inc(scattered[j], 16)

            def pair(it):
                for j in range(2):
                    wait(pool, xgT_ready, it * 2 + (j + 1))
                    wait(pool, idx_ready, it * 2 + (j + 3))
                    pool.sem_inc(pool_turn, 1)
                    gather(j)
                    behind(scatter, it, j)

            pair(0)
            with pool.Fori(1, pairs) as it:
                pair(it)
            last = pool.value_load(n_pairs[0:1, 1:2], min_val=NE // 2 - 1, max_val=(NE + MAX_OVER) // 2 - 1)
            scatter(last, 1)
            for j in range(2):
                pool.wait_ge(gathered[j], pairs * 32 + 32)
            pool.wait_ge(g2_loaded, 32)
            for t in range(NT):
                pool.wait_ge(out_ready, t + 1)
                link(gp.tensor_tensor(accin[:, t, :], accin[:, t, :], g2b[:, :], ALU.mult))
                gp.tensor_tensor(accin[:, t, :], accin[:, t, :], b2b[:, :], ALU.add).then_inc(out_scaled, 1)

        @block.tensor
        def _(pe):
            mm = nc.tensor.matmul
            pe.wait_ge(ident_ready, 1)
            pe.wait_ge(rows_loaded, 16 * 6)
            nc.tensor.transpose(bank[7][:, 0:NROWS], rows[0:NROWS, :], ident[0:NROWS, 0:NROWS]).then_inc(rows_T, 1)
            for t in range(NT):
                pe.wait_ge(xhat_ready, t + 1)
                for h in range(2):
                    b = bank[(2 * t + h) % 4]
                    if 2 * t + h >= 4:
                        pe.wait_ge(tr_taken, 2 * t + h - 3)
                    for c in range(4):
                        last = nc.tensor.transpose(b[:, c * P:(c + 1) * P], xh[:, t, 4 * h + c::ND], ident[:, :])
                    last.then_inc(tr_ready, 1)
            k = 0
            pe.wait_ge(w_loaded[0], 16)
            pe.wait_ge(cols_ready, 1)
            for t in range(NT):
                pe.wait_ge(tr_taken, 2 * (t + 1))
                if k >= 4:
                    pe.wait_ge(proj_taken, k - 3)
                for c in range(ND):
                    last = mm(bank[4 + k % 4][:, 0:P], xT[:, c, t * P:(t + 1) * P], wst[:, 0, c, :], start=c == 0, stop=c == ND - 1)
                last.then_inc(proj_ready, 1)
                k += 1
            for n in range(1, NPROJ):
                s = n % WRING
                pe.wait_ge(w_loaded[s], 16 * (n // WRING + 1) + (16 if feature_chunks[n - 1][2] is None else 0))
                for h in range(2):
                    pe.wait_ge(proj_taken, k - 3)
                    for c in range(ND):
                        last = mm(bank[4 + k % 4][:, :], wst[:, s, c, :], xT[:, c, h * HALF:(h + 1) * HALF], start=c == 0, stop=c == ND - 1)
                    last.then_inc(proj_ready, 1)
                    k += 1
            for g in range(POOL_G):
                pe.wait_ge(pdiff_ready, g + 1)
                for h in range(2):
                    m = 2 * g + h
                    if m >= 2:
                        pe.wait_ge(mixed_taken, m - 1)
                    if m < 2:
                        pe.wait_ge(proj_taken, k)
                    mm(bank[6 + m % 2][:, :], o_sb[:, g * P:(g + 1) * P], pdiff[:, g, h * HALF:(h + 1) * HALF],
                       start=True, stop=True).then_inc(mixed_ready, 1)
            pe.wait_ge(mixed_taken, 2 * POOL_G)
            pe.wait_ge(tr_taken, 2 * NT)

            def scores_of(b):
                k0 = (b - 1) * P if b else 0
                w = 2 * P if b else P
                for h in range(HEADS):
                    if b:
                        pe.wait_ge(sc_taken, HEADS * (b - 1) + (h | 2) + 1)
                    lo = HD * (h % 2)
                    kk = 0 if h // (HEADS // 2) == h % 2 else 1
                    mm(score_place(h, w),
                       qT[lo:lo + HD, h // 2, b * P:(b + 1) * P],
                       kT[lo:lo + HD, kk, k0:k0 + w], start=True, stop=True).then_inc(sc_ready, 1)

            scores_of(0)
            pt_n = 0
            for b in range(NT):
                kbs = (0, 1) if b else (1,)
                if b + 1 < NT:
                    scores_of(b + 1)
                for h2 in range(HEADS // 2):
                    pe.wait_ge(exp_done, HEADS * b + 2 * h2 + 2)
                    if pt_n >= 2:
                        pe.wait_ge(pt_taken, pt_n - 1)
                    for hh in range(2):
                        h = 2 * h2 + hh
                        for kb in kbs:
                            src = S_sb[:, h, kb * P:(kb + 1) * P] if b else S_sb[:, h, 0:P]
                            last = nc.tensor.transpose(bank[4 + pt_n % 2][:, (2 * hh + kb) * P:(2 * hh + kb + 1) * P], src, ident[:, :])
                    last.then_inc(pt_ready, 1)
                    pt_n += 1
                if b:
                    pe.wait_ge(o_scaled, b)
                for h in range(HEADS):
                    pe.wait_ge(pt_taken, 4 * b + h // 2 + 1)
                    g = h // (HEADS // 2)
                    for n, kb in enumerate(kbs):
                        last = mm(bank[6][:, h * HD:(h + 1) * HD], PT[:, 2 * h + kb, :],
                                  v_sb[:, b - 1 + kb, g * HD:(g + 1) * HD], start=n == 0, stop=n == len(kbs) - 1)
                last.then_inc(o_ready, 1)
                pe.wait_ge(o_scaled, b + 1)
                if b:
                    pe.wait_ge(oT_taken, b)
                for c in range(QC):
                    last = nc.tensor.transpose(bank[7][:, c * P:(c + 1) * P], o_sb[:, c * P:(c + 1) * P], ident[:, :])
                last.then_inc(oT_ready, 1)
            pe.wait_ge(oT_taken, NT)
            for c in range(ND):
                j = c % 2
                pe.wait_ge(mw_loaded[j], 64 * (c // 2 + 1))
                for h in range(2):
                    m = 2 * c + h
                    if m >= 2:
                        pe.wait_ge(merged_ready, m - 1)
                    bk = bank[4 * (m % 2):4 * (m % 2) + 4]
                    tok = slice(h * HALF, (h + 1) * HALF)
                    for q in range(2):
                        for k in range(ND):
                            last = mm(bk[q][:, :], wst[:, 3 * j + q, k, :], xT[:, k, tok], start=k == 0, stop=k == ND - 1)
                        last.then_inc(mg_ready, 1)
                    for q, src in ((0, uT), (1, qT)):
                        for k in range(4):
                            last = mm(bk[2 + q][:, :], wst[:, 3 * j + 2, 4 * q + k, :], src[:, k, tok], start=k == 0, stop=k == 3)
                        last.then_inc(mg_ready, 1)
            pe.wait_ge(merged_ready, 2 * ND)
            pe.wait_ge(wo_loaded, 32)

            def x1_transposes(t):
                pe.wait_ge(x1_ready, t + 1)
                for h in range(2):
                    n = 2 * t + h
                    if n >= 2:
                        pe.wait_ge(x1T_taken, n - 1)
                    for c in range(4):
                        last = nc.tensor.transpose(bank[4 + h][:, c * P:(c + 1) * P], xh[:, t, 4 * h + c::ND], ident[:, :])
                    last.then_inc(x1T_ready, 1)

            for t in range(NT):
                for h in range(2):
                    n = 2 * t + h
                    if n >= 4:
                        pe.wait_ge(mix_taken, n - 3)
                    for k in range(ND):
                        last = mm(bank[n % 4][:, :], mergedT[:, k, t * P:(t + 1) * P], (wo_a, wo_b)[h][:, k, :], start=k == 0, stop=k == ND - 1)
                    last.then_inc(mix_ready, 1)
                if t >= 1:
                    x1_transposes(t - 1)
            x1_transposes(NT - 1)
            pe.wait_ge(r_loaded, 64)
            for t in range(NT):
                pe.wait_ge(x1T_taken, 2 * t + 2)
                for c in range(ND):
                    last = mm(bank[6][:, t * NE:(t + 1) * NE], xT[:, c, t * P:(t + 1) * P], wr[:, c, :], start=c == 0, stop=c == ND - 1)
                last.then_inc(logits_ready, 1)
            pe.wait_ge(shw_loaded, 48)
            pe.wait_ge(mix_taken, 2 * NT)
            m = 0
            for f in range(NF):
                for h in range(2):
                    if m >= 2:
                        pe.wait_ge(sh_h, m - 1)
                    for q in range(2):
                        for c in range(ND):
                            last = mm(bank[2 * (m % 2) + q][:, :], Wsh[:, q * 2048 + c * FF + f * P:q * 2048 + c * FF + (f + 1) * P],
                                      xT[:, c, h * HALF:(h + 1) * HALF], start=c == 0, stop=c == ND - 1)
                    last.then_inc(sh_ready, 1)
                    m += 1
            pe.wait_ge(sh_h, 4)
            for t in range(NT):
                for h in range(2):
                    n = 2 * t + h
                    if n >= 4:
                        pe.wait_ge(acc_ready, t - 1)
                    for f in range(NF):
                        last = mm(bank[n % 4][:, :], hsh[:, f, t * P:(t + 1) * P], Wsh[:, 4096 + f * D + h * HALF:4096 + f * D + (h + 1) * HALF],
                                  start=f == 0, stop=f == NF - 1)
                    last.then_inc(shd_ready, 1)
            pe.wait_ge(mask_ready, 1)
            pe.wait_ge(pool_consts, 11)
            pe.wait_ge(score_ready, 1)
            for t in range(NT):
                for s in range(t + 1):
                    last = mm(bank[6][:, t * NE:(t + 1) * NE], tri[:, :] if s == t else ones[:, :], maskb[:, s, :], start=s == 0, stop=s == t)
            pe.wait_ge(x1T_taken, 2 * NT)
            for s in range(NT):
                last = mm(bank[5][:, 0:NE], ones[:, :], maskb[:, s, :], start=s == 0, stop=s == NT - 1)
            last.then_inc(pos_ready, 1)
            pe.wait_ge(tables_ready, 1)
            pairs = pe.value_load(n_pairs[0:1, 0:1], min_val=NE // 2, max_val=(NE + MAX_OVER) // 2)
            pe.wait_ge(acc_ready, NT)

            def make_list(e):
                for c in range(NC):
                    for t in range(NT):
                        last = mm(bank[7][0:CS, c * LIST:(c + 1) * LIST], onehot[:, t, c * CS:(c + 1) * CS],
                                  vlist[:, bass.ds(e, 1), t, :].rearrange("p o l -> p (o l)"), start=t == 0, stop=t == NT - 1)
                last.then_inc(list_ready, 1)

            def transposes(j):
                for c in range(ND):
                    for q in range(NC):
                        last = nc.tensor.transpose(bank[c // 3][:, (c % 3) * SLOTS + q * CS:(c % 3) * SLOTS + (q + 1) * CS],
                                                   xg[j][0:CS, q, c::ND], ident[0:CS, 0:CS])
                last.then_inc(xgT_ready, 1)

            def gate_up(j):
                for q in range(2):
                    for f in range(NF):
                        for c in range(ND):
                            last = mm(bank[3 + q][:, f * SLOTS:(f + 1) * SLOTS],
                                      W[j][:, q * 2048 + c * FF + f * P:q * 2048 + c * FF + (f + 1) * P],
                                      xgT[j][:, c, :], start=c == 0, stop=c == ND - 1)
                last.then_inc(gu_ready, 1)

            for i in range(2):
                pe.wait_ge(onehot_ready, i + 1)
                if i:
                    pe.wait_ge(idx_ready, i)
                make_list(i)
            pe.wait_ge(gathered[0], 32)
            transposes(0)
            def down(it, j):
                wait(pe, h_ready, it * 2 + (j + 1))
                wait(pe, wd_split, it * 2 + (j + 1))
                for c in range(NC):
                    for h in range(2):
                        wait(pe, (y_taken_dve, y_taken_act)[h], it * 4 + 2 * j + c)
                        for f in range(NF):
                            for n, (a, b) in enumerate(((h_hi[j], wd_hi), (h_hi[j], wd_lo), (h_lo[j], wd_hi))):
                                last = mm(bank[5 + h][0:CS, :], a[:, f, c * CS:(c + 1) * CS], b[:, f, h * HALF:(h + 1) * HALF],
                                          start=f + n == 0, stop=f == NF - 1 and n == 2)
                        last.then_inc(y_ready, 1)

            def pair(it):
                for j in range(2):
                    e2 = pe.value_load(etab[0:1, bass.ds(it * 2 + (j + 2), 1)], min_val=0, max_val=NE - 1)
                    wait(pe, gu_loaded[j], it * 32 + 32)
                    wait(pe, xgT_taken, it * 6 + 3 * (j + 1))
                    wait(pe, h_ready_full, it * 2 + j)
                    gate_up(j)
                    wait(pe, gathered[1 - j], it * 32 + 32 * (1 + j))
                    transposes(1 - j)
                    wait(pe, onehot_ready, it * 2 + (j + 3))
                    wait(pe, idx_ready, it * 2 + (j + 2))
                    make_list(e2)
                    behind(down, it, j)

            pair(0)
            with pe.Fori(1, pairs) as it:
                pair(it)
            last = pe.value_load(n_pairs[0:1, 1:2], min_val=NE // 2 - 1, max_val=(NE + MAX_OVER) // 2 - 1)
            down(last, 1)

        @block.scalar
        def _(act):
            A = nc.scalar.activation

            def root(t, round_):
                act.wait_ge(var_ready, round_ * NT + t + 1)
                A(std[:, t:t + 1], mean_var[:, t, 1:2], ACT.Sqrt, bias=eps[:, :]).then_inc(std_ready, 1)

            act.wait_ge(ident_ready, 1)
            root(0, 0)
            for t in range(NT):
                if t + 1 < NT:
                    root(t + 1, 0)
                if t == 0:
                    act.wait_ge(cols_ready, 1)
                for h in range(2):
                    act.wait_ge(tr_ready, 2 * t + h + 1)
                    for c in range(4):
                        k = 4 * h + c
                        last = A(xT[:, k, t * P:(t + 1) * P], bank[(2 * t + h) % 4][:, c * P:(c + 1) * P], ACT.Identity,
                                 scale=cols[:, C_G0 + k:C_G0 + k + 1], bias=cols[:, C_B0 + k:C_B0 + k + 1])
                    last.then_inc(tr_taken, 1)
            k = NT
            act.wait_ge(proj_taken, NT)
            for n in range(1, NPROJ):
                kind, c, col = feature_chunks[n - 1]
                dst = {"u": uT, "q": qT, "k": kT}[kind]
                bcol = C_KSW if col is None else col // P
                for h in range(2):
                    act.wait_ge(proj_ready, k + 1)
                    A(dst[:, c, h * HALF:(h + 1) * HALF], bank[4 + k % 4][:, :], ACT.Identity,
                      bias=cols[:, bcol:bcol + 1]).then_inc(proj_taken, 1)
                    k += 1
            for g in range(POOL_G):
                for h in range(2):
                    m = 2 * g + h
                    act.wait_ge(mixed_ready, m + 1)
                    act.wait_ge(pdiff_ready, g + 1)
                    act.wait_ge(ladder_ready, g + 1)
                    A(uT[:, g, h * HALF:(h + 1) * HALF], bank[6 + m % 2][:, :], ACT.Copy,
                      scale=cols[:, C_PS + g:C_PS + g + 1]).then_inc(mixed_taken, 1)
            n_act = 0
            for b in range(NT):
                w = 2 * P if b else P
                act.wait_ge(negm_ready, b + 1)
                for h in range(HEADS):
                    A(S_sb[:, h, 0:w], S_sb[:, h, 0:w], ACT.Exp, scale=HD ** -0.5, bias=small[:, 32 + h:33 + h],
                      accum_out=small[:, 40 + h:41 + h]).then_inc(exp_done, 1)
                A(small[:, 56:64], small[:, 48:56], ACT.Exp).then_inc(act_chain, 1)
                for q in range(4):
                    n = 4 * b + q
                    if q % 2 == 1:
                        act.wait_ge(pt_ready, n + 1)
                        act.wait_ge(pt_taken, n)
                        if b:
                            src = bank[4 + n % 2][:, :].rearrange("p (a c) -> p a c", a=4)
                            dst = PT[:, 4 * q:4 * q + 4, :]
                            act.wait_ge(o_ready, b)
                        else:
                            src = bank[4 + n % 2][:, :].rearrange("p (a c) -> p a c", a=4)[:, 1::2, :]
                            dst = PT[:, 4 * q + 1:4 * q + 4:2, :]
                        A(dst, src, ACT.Copy).then_inc(pt_taken, 1)
                act.wait_ge(oT_ready, b + 1)
                act.wait_ge(sc_ready, min(NT, b + 1) * HEADS)
                A(qT[:, :, b * P:(b + 1) * P], bank[7][:, :].rearrange("p (c q) -> p c q", c=QC), ACT.Copy).then_inc(oT_taken, 1)
            for m in range(2 * ND):
                for q in range(2):
                    act.wait_ge(mg_ready, 4 * m + q + 1)
                    if m >= 2:
                        act.wait_ge(merged_ready, m - 1)
                    A(gate_sb[:, 2 * (m % 2) + q, :], bank[4 * (m % 2) + q][:, :], ACT.Sigmoid,
                      bias=cols[:, GP_COL // P + q * ND + m // 2:GP_COL // P + q * ND + m // 2 + 1]).then_inc(sg_ready, 1)
            root(0, 1)
            for n in range(2 * NT):
                t, h = n // 2, n % 2
                if h == 0 and t + 1 < NT:
                    root(t + 1, 1)
                act.wait_ge(x1T_ready, n + 1)
                A(xT[:, 4 * h:4 * h + 4, t * P:(t + 1) * P], bank[4 + h][:, :].rearrange("p (c q) -> p c q", c=4), ACT.Copy).then_inc(x1T_taken, 1)
            act.wait_ge(logits_ready, NT)
            A(scores[:, :, :], bank[6][:, :].rearrange("p (t e) -> p t e", t=NT), ACT.Sigmoid).then_inc(score_ready, 1)
            for m in range(4):
                act.wait_ge(sh_ready, m + 1)
                if m >= 2:
                    act.wait_ge(sh_h, m - 1)
                A(sig_sh[:, m % 2, :], bank[2 * (m % 2)][:, :], ACT.Sigmoid).then_inc(sh_sig, 1)
            act.wait_ge(tables_ready, 1)
            pairs = act.value_load(n_pairs[0:1, 0:1], min_val=NE // 2, max_val=(NE + MAX_OVER) // 2)

            def take_transposes(j):
                for q, n in ((0, 3), (1, 3), (2, 2)):
                    A(xgT[j][:, 3 * q:3 * q + n, :], bank[q][:, 0:n * SLOTS].rearrange("p (c s) -> p c s", c=n),
                      ACT.Copy).then_inc(xgT_taken, 1)

            act.wait_ge(xgT_ready, 1)
            take_transposes(0)
            def take_y(it, j):
                wait(act, sidx_ready, it * 2 + (j + 1))
                for c in range(NC):
                    wait(act, y_ready, it * 8 + 4 * j + 2 * c + 2)
                    A(ysb[j][0:CS, c, HALF:D], bank[6][0:CS, :], ACT.Copy, scale=sgate[j][0:CS, c, :]).then_inc(y_taken_act, 1)

            def pair(it):
                for j in range(2):
                    wait(act, gu_ready, it * 2 + (j + 1))
                    wait(act, h_ready_full, it * 2 + j)
                    A(sig[:, :, :], bank[3][:, 0:NF * SLOTS].rearrange("p (f s) -> p f s", f=NF), ACT.Sigmoid).then_inc(sig_ready, 1)
                    wait(act, h_ready_full, it * 2 + (j + 1))
                    A(h_hi[j][:, :, :], h_full[:, :, :], ACT.Copy).then_inc(h_hi_ready, 1)
                    wait(act, xgT_ready, it * 2 + (j + 2))
                    take_transposes(1 - j)
                    behind(take_y, it, j)
                    wait(act, wd_loaded[j], it * 16 + 16)
                    wait(act, y_ready, it * 8 + 4 * j)
                    A(wd_hi[:, :, :], W[j][:, 4096:6144].rearrange("p (f d) -> p f d", f=NF), ACT.Copy).then_inc(wd_hi_ready, 1)

            pair(0)
            with act.Fori(1, pairs) as it:
                pair(it)
            last = act.value_load(n_pairs[0:1, 1:2], min_val=NE // 2 - 1, max_val=(NE + MAX_OVER) // 2 - 1)
            take_y(last, 1)
            for t in range(NT):
                root(t, 2)

        @block.vector
        def _(dve):
            v = nc.vector
            n = [0]

            def link(ins):
                n[0] += 1
                ins.then_inc(dve_chain, 1)
                dve.wait_ge(dve_chain, n[0])

            stats = small[:, 64:76].rearrange("p (a b) -> p a b", a=2)

            def statistics(src, t):
                for h in range(2):
                    v.bn_stats(stats[:, h, :], src[:, h * HALF:(h + 1) * HALF]).then_inc(dve_chain, 1)
                n[0] += 2
                dve.wait_ge(dve_chain, n[0])
                v.bn_aggr(mean_var[:, t, :], small[:, 64:76]).then_inc(var_ready, 1)

            def normalise(dst, src, t, round_, signal):
                dve.wait_ge(std_ready, round_ * NT + t + 1)
                link(v.reciprocal(std[:, t:t + 1], std[:, t:t + 1]))
                v.tensor_scalar(dst, src, mean_var[:, t, 0:1], std[:, t:t + 1], ALU.subtract, ALU.mult).then_inc(signal, 1)

            for t in range(NT):
                dve.wait_ge(x_loaded[t % 2], 16 * (t // 2 + 1))
                if t:
                    dve.wait_ge(var_ready, t)
                statistics(xin[:, t % 2, :], t)
                normalise(xh[:, t, :], xin[:, t % 2, :], t, 0, xhat_ready)
                if t == 0:
                    dve.wait_ge(rows_T, 1)
                    v.tensor_copy(cols[:, 0:NROWS], bank[7][:, 0:NROWS]).then_inc(cols_ready, 1)
            dve.wait_ge(consts_loaded, 16 * N_CONST)
            for t in range(NT):
                dve.wait_ge(proj_ready, t + 1)
                v.tensor_tensor(v_sb[:, t, :], bank[4 + t % 4][:, 0:P], vbias[:, :], ALU.add).then_inc(proj_taken, 1)
            dve.wait_ge(ident_ready, 2)
            for g in range(POOL_G):
                link(v.tensor_scalar(inv[:, g, :], inv[:, g, :], float(2 << g), None, ALU.min))
                link(v.reciprocal(inv[:, g, :], inv[:, g, :]))
            for g in range(POOL_G):
                dve.wait_ge(ladder_ready, g + 1)
                sm = ladder[:, g % 2, :]
                link(v.tensor_tensor(pdiff[:, g, 0:16], sm[:, 0:16], inv[:, g, :], ALU.mult))
                link(v.tensor_tensor(pdiff[:, g, 0:16], pdiff[:, g, 0:16], uT[:, g, 0:16], ALU.subtract))
                v.scalar_tensor_tensor(pdiff[:, g, 16:T], sm[:, 16:T], 1.0 / (2 << g), uT[:, g, 16:T], ALU.mult,
                                       ALU.subtract).then_inc(pdiff_ready, 1)
            for b in range(NT):
                w = 2 * P if b else P
                if b:
                    dve.wait_ge(pt_ready, 4 * b)
                for h in range(HEADS):
                    dve.wait_ge(sc_ready, HEADS * b + (h | 2) + 1)
                    slope = 2.0 ** (-8.0 * (h + 1) / HEADS)
                    v.scalar_tensor_tensor(S_sb[:, h, 0:w], dist[:, 2 * P - w:2 * P], -slope * HD ** 0.5,
                                           score_place(h, w),
                                           ALU.mult, ALU.add).then_inc(sc_taken, 1)
                dve.wait_ge(sc_taken, HEADS * (b + 1))
                link(v.tensor_reduce(small[:, 8:16], S_sb[:, :, 0:w], axis=AX.X, op=ALU.max))
                link(v.scalar_tensor_tensor(small[:, 16:24], small[:, 8:16], HD ** -0.5, small[:, 0:8], ALU.mult, ALU.max))
                link(v.tensor_tensor(small[:, 48:56], small[:, 0:8], small[:, 16:24], ALU.subtract))
                v.tensor_scalar(small[:, 32:40], small[:, 16:24], -1.0, None, ALU.mult).then_inc(negm_ready, 1)
                for q in (0, 2):
                    m = 4 * b + q
                    dve.wait_ge(pt_ready, m + 1)
                    dve.wait_ge(pt_taken, m)
                    src = bank[4 + m % 2][:, :].rearrange("p (a c) -> p a c", a=4)
                    if b:
                        dve.wait_ge(o_ready, b)
                        v.tensor_copy(PT[:, 4 * q:4 * q + 4, :], src).then_inc(pt_taken, 1)
                    else:
                        v.tensor_copy(PT[:, 4 * q + 1:4 * q + 4:2, :], src[:, 1::2, :]).then_inc(pt_taken, 1)
                dve.wait_ge(act_chain, b + 1)
                dve.wait_ge(exp_done, HEADS * (b + 1))
                link(v.tensor_tensor(small[:, 24:32], small[:, 40:48], small[:, 56:64], ALU.add))
                link(v.reciprocal(small[:, 24:32], small[:, 24:32]))
                dve.wait_ge(o_ready, b + 1)
                if b:
                    dve.wait_ge(oT_ready, b)
                else:
                    dve.wait_ge(mixed_ready, 2 * POOL_G)
                v.tensor_tensor(o_sb[:, :].rearrange("p (h d) -> p h d", h=HEADS),
                                bank[6][:, :].rearrange("p (h d) -> p h d", h=HEADS),
                                small[:, 24:32].rearrange("p (h o) -> p h o", o=1).to_broadcast([P, HEADS, HD]),
                                ALU.mult).then_inc(o_scaled, 1)
            for m in range(2 * ND):
                c, h = m // 2, m % 2
                dve.wait_ge(mg_ready, 4 * m + 4)
                dve.wait_ge(sg_ready, 2 * m + 2)
                gt = [gate_sb[:, 2 * (m % 2) + q, :] for q in range(2)]
                for q in range(2):
                    v.tensor_tensor(gt[q], gt[q], bank[4 * (m % 2) + 2 + q][:, :], ALU.mult).then_inc(dve_chain, 1)
                n[0] += 2
                dve.wait_ge(dve_chain, n[0])
                v.tensor_tensor(mergedT[:, c, h * HALF:(h + 1) * HALF], gt[0], gt[1], ALU.add).then_inc(merged_ready, 1)
            for t in range(NT):
                dve.wait_ge(x0_ready, t + 1)
                for h in range(2):
                    dve.wait_ge(mix_ready, 2 * t + h + 1)
                    v.scalar_tensor_tensor(xh[:, t, h * HALF:(h + 1) * HALF], xh[:, t, h * HALF:(h + 1) * HALF], ALPHA,
                                           bank[(2 * t + h) % 4][:, :], ALU.mult, ALU.add).then_inc(mix_taken, 1)
                dve.wait_ge(mix_taken, 2 * t + 2)
                dve.wait_ge(var_ready, NT + t)
                statistics(xh[:, t, :], t)
                normalise(xh[:, t, :], xh[:, t, :], t, 1, ln1_ready)
            dve.wait_ge(score_ready, 1)
            dve.wait_ge(r_loaded, 64)
            link(v.tensor_tensor(biased[:, :, :], scores[:, :, :], rbias[:, :].rearrange("p (o e) -> p o e", o=1).to_broadcast([P, NT, NE]), ALU.add))
            for t in range(NT):
                for g in range(GROUPS):
                    v.max(top[:, t, g, :], biased[:, t, g * PER_GROUP:(g + 1) * PER_GROUP]).then_inc(dve_chain, 1)
            n[0] += NT * GROUPS
            dve.wait_ge(dve_chain, n[0])
            link(v.tensor_tensor(gs[:, :, :], top[:, :, :, 0], top[:, :, :, 1], ALU.add))
            for t in range(NT):
                v.max(gtop[:, t, :], gs[:, t, :]).then_inc(dve_chain, 1)
            n[0] += NT
            dve.wait_ge(dve_chain, n[0])
            link(v.memset(gtop[:, :, KEEP_GROUPS:8], -NEG))
            for t in range(NT):
                v.match_replace(etop[:, t, :], gtop[:, t, :], gs[:, t, :], NEG).then_inc(dve_chain, 1)
            n[0] += NT
            dve.wait_ge(dve_chain, n[0])
            link(v.tensor_tensor(gs[:, :, :], etop[:, :, :], gs[:, :, :], ALU.is_equal))
            link(v.tensor_scalar(gs[:, :, :], gs[:, :, :], NEG, None, ALU.mult))
            link(v.tensor_tensor(work[:, :, :].rearrange("p t (g k) -> p (t g) k", g=GROUPS),
                                 biased[:, :, :].rearrange("p t (g k) -> p (t g) k", g=GROUPS),
                                 gs[:, :, :].rearrange("p t (g o) -> p (t g) o", o=1).to_broadcast([P, NT * GROUPS, PER_GROUP]), ALU.add))
            for t in range(NT):
                v.max(etop[:, t, :], work[:, t, :]).then_inc(dve_chain, 1)
            n[0] += NT
            dve.wait_ge(dve_chain, n[0])
            for t in range(NT):
                v.match_replace(mask[:, t, :], etop[:, t, :], work[:, t, :], 2 * NEG).then_inc(dve_chain, 1)
            n[0] += NT
            dve.wait_ge(dve_chain, n[0])
            link(v.tensor_tensor(mask[:, :, :], mask[:, :, :], work[:, :, :], ALU.not_equal))
            v.tensor_copy(maskb[:, :, :], mask[:, :, :]).then_inc(mask_ready, 1)
            link(v.tensor_tensor(gates[:, :, :], scores[:, :, :], mask[:, :, :], ALU.mult))
            link(v.tensor_reduce(gsum[:, :], gates[:, :, :], axis=AX.X, op=ALU.add))
            link(v.reciprocal(gsum[:, :], gsum[:, :]))
            link(v.tensor_tensor(gates[:, :, :], gates[:, :, :], gsum[:, :].rearrange("p (t o) -> p t o", o=1).to_broadcast([P, NT, NE]), ALU.mult))
            link(v.tensor_scalar(gates[:, :, :], gates[:, :, :], ROUTED_SCALE, None, ALU.mult))
            dve.wait_ge(pool_consts, 11)
            for q in range(3):
                part = vlist[:, :, :, 3 + q].rearrange("p e t -> p t e")
                link(v.tensor_copy(part, gates[:, :, :]))
                if q < 2:
                    link(v.tensor_tensor(gates[:, :, :], gates[:, :, :], part, ALU.subtract))
            for m in range(4):
                f, h = m // 2, m % 2
                dve.wait_ge(sh_sig, m + 1)
                link(v.tensor_tensor(sig_sh[:, m % 2, :], sig_sh[:, m % 2, :], bank[2 * (m % 2)][:, :], ALU.mult))
                v.tensor_tensor(hsh[:, f, h * HALF:(h + 1) * HALF], sig_sh[:, m % 2, :], bank[2 * (m % 2) + 1][:, :], ALU.mult).then_inc(sh_h, 1)
            for t in range(NT):
                dve.wait_ge(x1_stored, 16 * (NT + 4))
                dve.wait_ge(x1T_ready, 2 * NT)
                for h in range(2):
                    dve.wait_ge(shd_ready, 2 * t + h + 1)
                    ins = v.scalar_tensor_tensor(xh[:, t, h * HALF:(h + 1) * HALF], xh[:, t, h * HALF:(h + 1) * HALF], ALPHA,
                                                 bank[(2 * t + h) % 4][:, :], ALU.mult, ALU.add)
                    if h == 0:
                        link(ins)
                    else:
                        ins.then_inc(acc_ready, 1)
            dve.wait_ge(pos_ready, 1)
            pt = posm[:, :, :].rearrange("p e t -> p t e")
            link(v.scalar_tensor_tensor(pt, bank[6][:, :].rearrange("p (t e) -> p t e", t=NT), 1.0, mask[:, :, :], ALU.add, ALU.mult))
            link(v.tensor_scalar(pt, pt, -1.0, None, ALU.add))
            link(v.tensor_scalar(extra[:, 0, :], bank[5][:, 0:NE], float(SLOTS), None, ALU.is_gt))
            for k in range(2, T // SLOTS + 1):
                link(v.tensor_scalar(extra[:, 1, :], bank[5][:, 0:NE], float(k * SLOTS), None, ALU.is_gt))
                link(v.tensor_tensor(extra[:, 0, :], extra[:, 0, :], extra[:, 1, :], ALU.add))
            link(v.memset(extra[:, 1, :], 1.0))
            link(v.tensor_tensor_scan(extra[:, 2, :], extra[:, 1, :], extra[:, 0, :], 0.0, ALU.mult, ALU.add))
            dve.wait_ge(sh_ready, 4)
            link(v.tensor_tensor(cmp[:, :, :], extra[:, 2, :].rearrange("p (o e) -> p o e", o=1).to_broadcast([P, MAX_OVER, NE]),
                                 over[:, 0, :].rearrange("p (o e) -> p o e", e=1).to_broadcast([P, MAX_OVER, NE]), ALU.is_le))
            link(v.tensor_reduce(over[:, 1, :], cmp[:, :, :], axis=AX.X, op=ALU.add))
            link(v.tensor_tensor(cmp[:, :, :], cmp[:, :, :], extra[:, 0, :].rearrange("p (o e) -> p o e", o=1).to_broadcast([P, MAX_OVER, NE]), ALU.mult))
            link(v.tensor_reduce(over[:, 2, :], cmp[:, :, :], axis=AX.X, op=ALU.add))
            link(v.tensor_tensor(over[:, 2, :], over[:, 0, :], over[:, 2, :], ALU.subtract))
            link(v.tensor_scalar(over[:, 2, :], over[:, 2, :], 1.0, float(SLOTS), ALU.add, ALU.mult))
            link(v.tensor_scalar(over[:, 3, :], over[:, 1, :], float(NE), FAR, ALU.is_ge, ALU.mult))
            link(v.memset(btab[:, :], 0.0))
            link(v.memset(btab[:, NE + MAX_OVER:NTAB], FAR))
            link(v.tensor_tensor(btab[:, NE:NE + MAX_OVER], over[:, 2, :], over[:, 3, :], ALU.add))
            link(v.memset(etabf[:, NE + MAX_OVER:NTAB], 0.0))
            link(v.tensor_scalar(etabf[:, NE:NE + MAX_OVER], over[:, 1, :], float(NE - 1), None, ALU.min))
            link(v.tensor_copy(etab[:, :], etabf[:, :]))
            link(v.tensor_scalar(over[:, 1, :], over[:, 0, :], extra[:, 2, NE - 1:NE], None, ALU.is_lt))
            link(v.tensor_reduce(small[:, 80:81], over[:, 1, 0:MAX_OVER:2], axis=AX.X, op=ALU.add))
            link(v.tensor_scalar(n_pairs[:, 0:1], small[:, 80:81], float(NE // 2), None, ALU.add))
            v.tensor_scalar(n_pairs[:, 1:2], small[:, 80:81], float(NE // 2 - 1), None, ALU.add).then_inc(tables_ready, 1)
            dve.wait_ge(tables_ready, 1)
            pairs = dve.value_load(n_pairs[0:1, 0:1], min_val=NE // 2, max_val=(NE + MAX_OVER) // 2)
            n0 = n[0]

            def make_onehot(e):
                v.tensor_tensor(onehot[:, :, :],
                                posm[:, bass.ds(e, 1), :].rearrange("p o t -> p (o t)").rearrange("p (t o) -> p t o", o=1).to_broadcast([P, NT, SLOTS]),
                                iotab[:, :].rearrange("p (o s) -> p o s", o=1).to_broadcast([P, NT, SLOTS]),
                                ALU.is_equal).then_inc(onehot_ready, 1)

            def make_index(j, chain):
                lp = bank[7][0:CS, 0:NC * LIST].rearrange("p (c l) -> p c l", c=NC)
                lf = lst[j]
                chain(v.tensor_reduce(lf[0:CS, :, 0], lp[:, :, 0:2], axis=AX.X, op=ALU.add), 0)
                chain(v.tensor_reduce(lf[0:CS, :, 1], lp[:, :, 3:6], axis=AX.X, op=ALU.add), 1)
                chain(v.tensor_tensor(tmp[0:CS, :, 0], lp[:, :, 2], trash[0:CS, 1, :], ALU.mult), 2)
                chain(v.tensor_tensor(tmp[0:CS, :, 0], tmp[0:CS, :, 0], trash[0:CS, 0, :], ALU.add), 3)
                v.tensor_tensor(gidx[j][0:CS, :], tmp[0:CS, :, 0], lf[0:CS, :, 0], ALU.add).then_inc(idx_ready, 1)

            iotab = at("iotab", l0 + 19 * KB, [P, SLOTS])
            for i in range(2):
                if i:
                    dve.wait_ge(list_ready, i)
                link(v.tensor_scalar(iotab[:, :], iotas[:, :], btab[:, i:i + 1], None, ALU.add))
                make_onehot(i)
                dve.wait_ge(list_ready, i + 1)
                make_index(i, lambda ins, q: link(ins))
            n0 = n[0]
            STEPS = 7
            def take_y(it, j, chunks=range(NC)):
                for c in chunks:
                    wait(dve, y_ready, it * 8 + 4 * j + 2 * c + 1)
                    v.tensor_scalar(ysb[j][0:CS, c, 0:HALF], bank[5][0:CS, :], sgate[j][0:CS, c, :], None, ALU.mult).then_inc(y_taken_dve, 1)

            def pair(it):
                for j in range(2):
                    def chain(ins, q):
                        ins.then_inc(dve_chain, 1)
                        dve.wait_ge(dve_chain, it * (2 * STEPS) + (n0 + j * STEPS + q + 1))

                    e2 = dve.value_load(etab[0:1, bass.ds(it * 2 + (j + 2), 1)], min_val=0, max_val=NE - 1)
                    wait(dve, list_ready, it * 2 + (j + 2))
                    chain(v.tensor_scalar(iotab[:, :], iotas[:, :], btab[:, bass.ds(it * 2 + (j + 2), 1)], None, ALU.add), 0)
                    make_onehot(e2)
                    wait(dve, sig_ready, it * 2 + (j + 1))
                    chain(v.tensor_tensor(sig[:, :, :], sig[:, :, :], bank[3][:, 0:NF * SLOTS].rearrange("p (f s) -> p f s", f=NF), ALU.mult), 1)
                    wait(dve, h_ready, it * 2 + j)
                    v.tensor_tensor(h_full[:, :, :], sig[:, :, :], bank[4][:, 0:NF * SLOTS].rearrange("p (f s) -> p f s", f=NF), ALU.mult).then_inc(h_ready_full, 1)
                    wait(dve, h_hi_ready, it * 2 + (j + 1))
                    v.tensor_tensor(h_lo[j][:, :, :], h_full[:, :, :], h_hi[j][:, :, :].bitcast(f32), ALU.subtract).then_inc(h_ready, 1)
                    behind(lambda it, j: take_y(it, j, (0,)), it, j)
                    wait(dve, scattered[j], it * 32)
                    wait(dve, idx_ready, it * 2 + (j + 2))
                    chain(v.tensor_copy(sidx[j][0:CS, :], gidx[j][0:CS, :]), 2)
                    v.tensor_copy(sgate[j][0:CS, :, 0], lst[j][0:CS, :, 1]).then_inc(sidx_ready, 1)
                    wait(dve, list_ready, it * 2 + (j + 3))
                    wait(dve, sidx_ready, it * 2 + (j + 1))
                    wait(dve, gathered[j], it * 32 + 32)
                    make_index(j, lambda ins, q: chain(ins, 3 + q))
                    behind(lambda it, j: take_y(it, j, (1,)), it, j)
                    wait(dve, wd_hi_ready, it * 2 + (j + 1))
                    v.tensor_tensor(wd_lo[:, :, :], W[j][:, 4096:6144].rearrange("p (f d) -> p f d", f=NF),
                                    wd_hi[:, :, :].bitcast(f32), ALU.subtract).then_inc(wd_split, 1)

            pair(0)
            with dve.Fori(1, pairs) as it:
                pair(it)
            last = dve.value_load(n_pairs[0:1, 1:2], min_val=NE // 2 - 1, max_val=(NE + MAX_OVER) // 2 - 1)
            take_y(last, 1)
            for t in range(NT):
                src = accin[:, t, :]
                dve.wait_ge(acc_loaded[t], 16)
                if t:
                    dve.wait_ge(var_ready, 2 * NT + t)
                for h in range(2):
                    v.bn_stats(stats[:, h, :], src[:, h * HALF:(h + 1) * HALF]).then_inc(last_chain, 1)
                dve.wait_ge(last_chain, 3 * t + 2)
                v.bn_aggr(mean_var[:, t, :], small[:, 64:76]).then_inc(var_ready, 1)
                dve.wait_ge(std_ready, 2 * NT + t + 1)
                v.reciprocal(std[:, t:t + 1], std[:, t:t + 1]).then_inc(last_chain, 1)
                dve.wait_ge(last_chain, 3 * t + 3)
                v.tensor_scalar(src, src, mean_var[:, t, 0:1], std[:, t:t + 1], ALU.subtract, ALU.mult).then_inc(out_ready, 1)


_INS = ['x', 'ln0_g', 'ln0_b', 'w_in', 'b_in', 'w_pool', 'pool_scale', 'attn_sinks', 'w_br_pool', 'w_br_attn', 'w_out',
        'ln1_g', 'ln1_b', 'w_router', 'router_bias', 'w_exp_gate', 'w_exp_up', 'w_exp_down', 'w_sh_gate', 'w_sh_up',
        'w_sh_down', 'ln2_g', 'ln2_b']


def kernel(**inputs):
    import numpy as _np
    import concourse.bacc as _bacc
    from concourse import mybir as _mybir
    from concourse.bass_utils import run_bass_kernel_spmd as _run

    nc = _bacc.Bacc("TRN2", target_bir_lowering=False, num_devices=1)
    arrays, args = {}, []
    for name in _INS:
        a = _np.ascontiguousarray(inputs[name])
        arrays[f"in_{name}_dram"] = a
        args.append(nc.dram_tensor(f"in_{name}_dram", a.shape, _mybir.dt.from_np(a.dtype), kind="ExternalInput").ap())
    args.append(nc.dram_tensor("out_dram", (1, 1024, 1024), _mybir.dt.float32, kind="ExternalOutput").ap())
    build(nc, *args)
    r = _run(nc, [arrays], core_ids=[0])
    return r.results[0]["out_dram"]
```

```python
import concourse.bass as bass
from concourse import mybir
from contextlib import ExitStack

T, D, P = 1024, 1024, 128
NT = T // P
ND = D // P
POOL_G = 4
HEADS, HD = 8, 64
QC = HEADS * HD // P
D_IN = 3328
K_COL, V_COL, GP_COL, GA_COL = 1024, 1152, 1280, 2304
NE, FF = 64, 256
NF = FF // P
TOPK = 8
GROUPS, PER_GROUP, KEEP_GROUPS = 8, 8, 4
ROUTED_SCALE = 2.5
ALPHA = 2.0 ** 0.25
EPS = 1e-5
HALF = 512

CS = 76
NC = 2
SLOTS = CS * NC
MAX_OVER = T * TOPK // SLOTS
MAX_OVER += MAX_OVER % 2
NTAB = NE + MAX_OVER + 4
FAR = 16384.0
LIST = 6
NEG = -1.0e30


def build(nc, x, ln0_g, ln0_b, w_in, b_in, w_pool, pool_scale, attn_sinks, w_br_pool, w_br_attn,
          w_out, ln1_g, ln1_b, w_router, router_bias, w_exp_gate, w_exp_up, w_exp_down, w_sh_gate,
          w_sh_up, w_sh_down, ln2_g, ln2_b, out):
    f32, f32r, bf16, i32 = mybir.dt.float32, mybir.dt.float32r, mybir.dt.bfloat16, mybir.dt.int32
    ALU, ACT, AX = mybir.AluOpType, mybir.ActivationFunctionType, mybir.AxisListType

    x_t = x[0].rearrange("(t p) d -> t p d", p=P)
    out_t = out[0].rearrange("(t p) d -> t p d", p=P)
    win = w_in[0].rearrange("(p c) e -> p c e", c=ND)
    wg_e = w_exp_gate[0].rearrange("e (p c) f -> e p c f", c=ND)
    wu_e = w_exp_up[0].rearrange("e (p c) f -> e p c f", c=ND)
    wd_e = w_exp_down[0].rearrange("e (c p) d -> e p c d", p=P)
    x1_dram = nc.dram_tensor("x1_rows", (T + SLOTS, D), f32, kind="Internal").ap()
    acc_dram = nc.dram_tensor("acc_rows", (T + SLOTS, D), f32, kind="Internal").ap()

    ctx = ExitStack()
    with ctx:
        base = 16512
        XBUF = 4
        KB = 1024

        def at(name, offset, shape, dt=f32):
            return nc.alloc_sbuf_tensor_at(name, shape, dt, offset=base + offset)

        def sem(name):
            return ctx.enter_context(nc.semaphore(name))

        XT = at("XT", 0, [P, 2, 2, ND, HALF], f32r)
        xin = at("xin", 76 * KB, [P, XBUF, D])
        x_full = at("x_full", 72 * KB, [P, 2, HALF])
        m_full = at("m_full", 76 * KB, [P, 2, HALF])
        S_sb = [at(f"S_sb{j}", (72 + 8 * j) * KB, [P, HEADS, 2 * P]) for j in range(2)]
        PT = at("PT", 88 * KB, [P, 2 * HEADS, P])
        mergedT = at("mergedT", 64 * KB, [P, ND, T])
        uT = at("uT", 96 * KB, [P, POOL_G, T])
        pdiff = at("pdiff", 112 * KB, [P, POOL_G, T])
        mixT = at("mixT", 96 * KB, [P, 2, POOL_G, T], f32r)
        xhat = at("xhat", 128 * KB, [P, 4, D])
        qT = at("qT", 128 * KB, [P, QC, T])
        oT = at("oT", 128 * KB, [P, 2, QC, T], f32r)
        ladder = at("ladder", 144 * KB, [P, 2, T])
        vT = at("vT", 152 * KB, [P, T])
        wpool = at("wpool", 156 * KB, [P, POOL_G, P])
        rows = at("rows", 158 * KB, [P, P])
        inv = at("inv", 158 * KB + 512, [P, POOL_G, 16])
        kT = at("kT", 160 * KB, [P, 2, T])
        v_sb = at("v_sb", 168 * KB, [P, NT, P])
        gate_sb = at("gate_sb", 160 * KB, [P, 4, HALF])
        RING = 4
        u_raw = [at(f"u_raw{r}", (172 + 8 * r) * KB, [P, D]) for r in range(RING)]
        u_lo = [at(f"u_lo{r}", (172 + 8 * r) * KB, [P, D], f32r) for r in range(RING)]
        u_hi = [at(f"u_hi{r}", (176 + 8 * r) * KB, [P, D], f32r) for r in range(RING)]
        o_raw = [at(f"o_raw{r}", (96 + 8 * r) * KB, [P, D]) for r in range(4)]
        o_lo = [at(f"o_lo{r}", (96 + 8 * r) * KB, [P, D], f32r) for r in range(4)]
        o_hi = [at(f"o_hi{r}", (100 + 8 * r) * KB, [P, D], f32r) for r in range(4)]
        xh = at("xh", 128 * KB, [P, NT, D])
        g1b = at("g1b", 160 * KB, [P, D])
        b1b = at("b1b", 164 * KB, [P, D])
        c0 = 204 * KB
        ident = at("ident", c0, [P, P])
        dist = at("dist", c0 + 512, [P, 2 * P])
        cols = at("cols", c0 + 1536, [P, 64])
        small = at("small", c0 + 1792, [P, 160])
        mean_var = at("mean_var", c0 + 2432, [P, NT, 2])
        std = at("std", c0 + 2496, [P, NT])
        mean_var0 = at("mean_var0", c0 + 2528, [P, NT, 2])
        std0 = at("std0", c0 + 2592, [P, NT])
        eps = at("eps", c0 + 2624, [P, 1])

        W = [at(f"W{j}", 24 * j * KB, [P, 3 * 2048]) for j in range(2)]
        hsh = at("hsh", 64 * KB, [P, 2, NF, T], f32r)
        sig_sh = at("sig_sh", 80 * KB, [P, HALF])
        h_sh = at("h_sh", 82 * KB, [P, HALF])
        r0 = 86 * KB
        scores = at("scores", r0, [P, NT, NE])
        biased = at("biased", r0 + 2048, [P, NT, NE])
        work = at("work", r0 + 4096, [P, NT, NE])
        top = at("top", r0 + 6144, [P, NT, GROUPS, 8])
        mask = at("mask", r0 + 8192, [P, NT, NE])
        scoresT = at("scoresT", r0 + 4096, [P, T])
        maskb = at("maskb", r0 + 10240, [P, NT, NE], bf16)
        gates = at("gates", r0 + 11264, [P, NT, NE])
        gs = at("gs", r0 + 13312, [P, NT, GROUPS])
        gtop = at("gtop", r0 + 13568, [P, NT, 8])
        etop = at("etop", r0 + 13824, [P, NT, 8])
        gsum = at("gsum", r0 + 14080, [P, NT])
        rbias = at("rbias", r0 + 17 * KB, [P, NE])
        cmp = at("cmp", 160 * KB, [P, MAX_OVER, NE], bf16)
        l0 = 105 * KB
        posm = at("posm", l0, [P, NE, NT])
        vlist = at("vlist", l0 + 2 * KB, [P, NE, NT, LIST], bf16)
        iotas = at("iotas", l0 + 8 * KB, [P, SLOTS])
        tri = at("tri", l0 + 9 * KB, [P, P], bf16)
        ones = at("ones", l0 + 9 * KB + 256, [P, P], bf16)
        etab = at("etab", l0 + 10 * KB, [P, NTAB], i32)
        etabf = at("etabf", l0 + 10 * KB + 512, [P, NTAB])
        btab = at("btab", l0 + 11 * KB, [P, NTAB])
        n_pairs = at("n_pairs", l0 + 11 * KB + 512, [P, 2], i32)
        trash = at("trash", l0 + 11 * KB + 544, [P, 2, NC])
        extra = at("extra", l0 + 12 * KB, [P, 4, NE])
        over = at("over", l0 + 13 * KB, [P, 4, MAX_OVER])
        extra_b = at("extra_b", l0 + 14 * KB + 640, [P, 2, NE], bf16)
        over_b = at("over_b", l0 + 14 * KB + 896, [P, MAX_OVER], bf16)
        iotab = at("iotab", l0 + 14 * KB, [P, SLOTS])
        gidx = [at(f"gidx{j}", l0 + 15 * KB + 64 * j, [P, NC], i32) for j in range(2)]
        sidx = [at(f"sidx{j}", l0 + 15 * KB + 128 + 64 * j, [P, NC], i32) for j in range(2)]
        lst = [at(f"lst{j}", l0 + 15 * KB + 256 + 64 * j, [P, NC, 2]) for j in range(2)]
        sgate = [at(f"sgate{j}", l0 + 15 * KB + 384 + 64 * j, [P, NC, 1]) for j in range(2)]
        tmp = at("tmp", l0 + 15 * KB + 512, [P, NC, 1])
        wr = at("wr", 121 * KB, [P, ND, NE])
        wr_hi = at("wr_hi", 123 * KB, [P, ND, NE], f32r)
        wr_lo = at("wr_lo", 125 * KB, [P, ND, NE], f32r)
        zrow = at("zrow", 168 * KB, [P, D])
        onehot = at("onehot", 83 * KB, [P, NT, SLOTS], bf16)
        xg = [at(f"xg{j}", r0 + 8 * j * KB, [P, NC, D]) for j in range(2)]
        xgT = [at(f"xgT{j}", (122, 144)[j] * KB, [P, ND, SLOTS]) for j in range(2)]
        ysb = [at(f"ysb{j}", (128 + 8 * j) * KB, [P, NC, D]) for j in range(2)]
        wd_hi = at("wd_hi", 48 * KB, [P, NF, D], f32r)
        wd_lo = at("wd_lo", 56 * KB, [P, NF, D], f32r)
        sig = at("sig", 172 * KB, [P, NF, SLOTS])
        h_full = at("h_full", 174 * KB, [P, NF, SLOTS])
        h_hi = [at(f"h_hi{j}", (176 + 4 * j) * KB, [P, NF, SLOTS], f32r) for j in range(2)]
        h_lo = [at(f"h_lo{j}", (178 + 4 * j) * KB, [P, NF, SLOTS], f32r) for j in range(2)]
        g2b = at("g2b", 188 * KB, [P, D])
        b2b = at("b2b", 192 * KB, [P, D])
        accin = at("accin", 0, [P, NT, D])

        bank = [ctx.enter_context(nc.psum_tensor(f"bank{i}", [P, HALF], f32)) for i in range(8)]

        BIN_ROWS = D_IN // P
        C_G0, C_B0 = BIN_ROWS + 1 + POOL_G, BIN_ROWS + 1 + POOL_G + ND
        C_KSW, C_PS = BIN_ROWS, BIN_ROWS + 1
        NROWS = BIN_ROWS + 1 + POOL_G

        consts_loaded = sem("consts_loaded")
        rows_loaded = sem("rows_loaded")
        x_loaded = [sem(f"x_loaded{j}") for j in range(XBUF)]
        ident_ready = sem("ident_ready")
        dve_chain = sem("dve_chain")
        act_chain = sem("act_chain")
        pool_chain = sem("pool_chain")
        rows_T = sem("rows_T")
        cols_ready = sem("cols_ready")
        xhat_ready = sem("xhat_ready")
        tr_ready = sem("tr_ready")
        tr_taken = sem("tr_taken")
        unit_loaded = [sem(f"unit_loaded{r}") for r in range(RING)]
        wo_loaded = [sem(f"wo_loaded{r}") for r in range(4)]
        unit_hi = sem("unit_hi")
        unit_split = sem("unit_split")
        wo_done = sem("wo_done")
        x0_full = sem("x0_full")
        x0_hi = sem("x0_hi")
        v_ready = sem("v_ready")
        v_taken = sem("v_taken")
        m_full_ready = sem("m_full_ready")
        m_hi_ready = sem("m_hi_ready")
        rden_ready = sem("rden_ready")
        scaled = sem("scaled")
        sink_exp = sem("sink_exp")
        pv_ready = sem("pv_ready")
        o_hi_ready = sem("o_hi_ready")
        o_taken = sem("o_taken")
        piece_hi = sem("piece_hi")
        piece_split = sem("piece_split")
        xr_loaded = [sem(f"xr_loaded{t}") for t in range(NT)]
        x0hat_ready = sem("x0hat_ready")
        x1_hi = sem("x1_hi")
        wr_ready = sem("wr_ready")
        sh_full = sem("sh_full")
        sh_hi = sem("sh_hi")
        proj_ready = sem("proj_ready")
        proj_taken = sem("proj_taken")
        wp_loaded = sem("wp_loaded")
        pdiff_ready = sem("pdiff_ready")
        ladder_ready = sem("ladder_ready")
        mixed_ready = sem("mixed_ready")
        mixed_taken = sem("mixed_taken")
        x0_ready = sem("x0_ready")
        sc_ready = sem("sc_ready")
        sc_taken = sem("sc_taken")
        negm_ready = sem("negm_ready")
        exp_done = sem("exp_done")
        pt_ready = sem("pt_ready")
        pt_taken = sem("pt_taken")
        mg_ready = sem("mg_ready")
        sg_ready = sem("sg_ready")
        merged_ready = sem("merged_ready")
        mix_ready = sem("mix_ready")
        mix_taken = sem("mix_taken")
        ln1_ready = sem("ln1_ready")
        x1_ready = sem("x1_ready")
        x1T_ready = sem("x1T_ready")
        x1T_taken = sem("x1T_taken")
        x1_stored = sem("x1_stored")
        r_loaded = sem("r_loaded")
        g1_loaded = sem("g1_loaded")
        wr_loaded = sem("wr_loaded")
        logits_ready = sem("logits_ready")
        score_ready = sem("score_ready")
        scoresT_ready = sem("scoresT_ready")
        scores_tr = sem("scores_tr")
        mask_ready = sem("mask_ready")
        pos_ready = sem("pos_ready")
        pool_consts = sem("pool_consts")
        sh_ready = sem("sh_ready")
        sh_sig = sem("sh_sig")
        sh_h = sem("sh_h")
        shd_ready = sem("shd_ready")
        shd_taken = sem("shd_taken")
        acc_stored = sem("acc_stored")
        tables_ready = sem("tables_ready")
        gu_loaded = [sem(f"gu_loaded{j}") for j in range(2)]
        wd_loaded = [sem(f"wd_loaded{j}") for j in range(2)]
        onehot_ready = sem("onehot_ready")
        list_ready = sem("list_ready")
        idx_ready = sem("idx_ready")
        gathered = [sem(f"gathered{j}") for j in range(2)]
        xgT_ready = sem("xgT_ready")
        xgT_taken = sem("xgT_taken")
        gu_ready = sem("gu_ready")
        sig_ready = sem("sig_ready")
        h_ready = sem("h_ready")
        h_ready_full = sem("h_ready_full")
        h_hi_ready = sem("h_hi_ready")
        wd_hi_ready = sem("wd_hi_ready")
        wd_split = sem("wd_split")
        y_ready = sem("y_ready")
        y_taken_dve = sem("y_taken_dve")
        y_taken_act = sem("y_taken_act")
        sidx_ready = sem("sidx_ready")
        scattered = [sem(f"scattered{j}") for j in range(2)]
        pool_turn = sem("pool_turn")
        acc_loaded = [sem(f"acc_loaded{t}") for t in range(NT)]
        g2_loaded = sem("g2_loaded")
        out_ready = sem("out_ready")
        out_scaled = sem("out_scaled")
        last_scaled = sem("last_scaled")
        scale_ready = sem("scale_ready")
        normal_ready = sem("normal_ready")
        out_stored = sem("out_stored")
        last_chain = sem("last_chain")
        var_ready = sem("var_ready")
        std_ready = sem("std_ready")

        def score_place(h, w):
            o = (h // 2 % 2) * 2 * P
            return bank[2 * (h % 2) + h // 4][:, o:o + w]

        def wait(engine, semaphore, value):
            if not isinstance(value, int) or value > 0:
                engine.wait_ge(semaphore, value)

        def behind(step, it, j):
            if j:
                step(it, 0)
            elif not isinstance(it, int) or it > 0:
                step(it - 1, 1)

        win_k = [("u", g, g * P) for g in range(POOL_G)] + [("q", c, 512 + c * P) for c in range(QC)] + \
                [("k", 0, K_COL), ("k", 1, None), ("v", 0, V_COL)]
        NPROJ = len(win_k)
        U_MERGE, U_OUT, U_SH = NPROJ, NPROJ + 3 * ND, NPROJ + 3 * ND + ND
        MERGE_INCS = 8

        def unit(n):
            if U_OUT + 4 <= n < U_SH:
                r = n - U_OUT - 4
                return o_raw[r], o_hi[r], o_lo[r]
            return u_raw[n % RING], u_hi[n % RING], u_lo[n % RING]

        def wait_unit_loaded(engine, n):
            if U_OUT + 4 <= n < U_SH:
                engine.wait_ge(wo_loaded[n - U_OUT - 4], 16)
            else:
                r = n % RING
                earlier = [m for m in range(n + 1) if m % RING == r and not U_OUT + 4 <= m < U_SH]
                engine.wait_ge(unit_loaded[r], sum(16 * pieces(m) for m in earlier))

        def pieces(n):
            if n < U_MERGE:
                return 2 if win_k[n][2] is None else 1
            if n < U_OUT:
                return 2 if (n - U_MERGE) % 3 == 2 else 1
            return 1

        def wait_unit_used(engine, n):
            if n < U_MERGE:
                engine.wait_ge(proj_ready, 2 * (n + 1))
            elif n < U_OUT:
                c, q = divmod(n - U_MERGE, 3)
                engine.wait_ge(mg_ready, MERGE_INCS * c + (2, 4, 8)[q])
            elif n < U_SH:
                engine.wait_ge(wo_done, n - U_OUT + 1)
            else:
                engine.wait_ge(sh_ready, 3)

        SPLIT = ((0, 0), (0, 1), (1, 0))

        block = ctx.enter_context(nc.Block())

        @block.sync
        def _(sp):
            def load_unit(n):
                raw = unit(n)[0]
                rc = raw[:, :].rearrange("p (c e) -> p c e", c=ND)
                if U_OUT + 4 <= n < U_SH:
                    signal = wo_loaded[n - U_OUT - 4]
                    wait_unit_used(sp, U_OUT - 1)
                else:
                    signal = unit_loaded[n % RING]
                    before = [m for m in range(n) if m % RING == n % RING and not U_OUT + 4 <= m < U_SH]
                    if before:
                        wait_unit_used(sp, before[-1])
                if n < U_MERGE:
                    col = win_k[n][2]
                    if col is None:
                        sp.dma_start(rc[:, :, 0:HD], win[:, :, K_COL + HD:K_COL + P]).then_inc(signal, 16)
                        sp.dma_start(rc[:, :, HD:P], win[:, :, K_COL:K_COL + HD]).then_inc(signal, 16)
                    else:
                        sp.dma_start(rc, win[:, :, col:col + P]).then_inc(signal, 16)
                elif n < U_OUT:
                    c, q = divmod(n - U_MERGE, 3)
                    if q < 2:
                        col = (GP_COL, GA_COL)[q] + c * P
                        sp.dma_start(rc, win[:, :, col:col + P]).then_inc(signal, 16)
                    else:
                        for h, w in ((0, w_br_pool), (1, w_br_attn)):
                            sp.dma_start(rc[:, 4 * h:4 * h + 4, :],
                                         w[0].rearrange("(k p) d -> p k d", p=P)[:, :, c * P:(c + 1) * P]).then_inc(signal, 16)
                elif n < U_SH:
                    k = n - U_OUT
                    sp.dma_start(raw[:, :], w_out[0, k * P:(k + 1) * P, :]).then_inc(signal, 16)
                elif n < U_SH + 4:
                    f, q = divmod(n - U_SH, 2)
                    w = (w_sh_gate, w_sh_up)[q][0].rearrange("(p c) f -> p c f", c=ND)
                    sp.dma_start(rc, w[:, :, f * P:(f + 1) * P]).then_inc(signal, 16)
                else:
                    f = n - U_SH - 4
                    sp.dma_start(raw[:, :], w_sh_down[0, f * P:(f + 1) * P, :]).then_inc(signal, 16)

            for t in range(NT):
                if t >= XBUF:
                    sp.wait_ge(xhat_ready, t - XBUF + 1)
                sp.dma_start(xin[:, t % XBUF, :], x_t[t]).then_inc(x_loaded[t % XBUF], 16)
                if t == 0:
                    sp.dma_start(rows[0:BIN_ROWS, :], b_in[0].rearrange("(r n) -> r n", n=P)).then_inc(rows_loaded, 16)
                    sp.dma_start(rows[C_KSW:C_KSW + 1, 0:HD], b_in[0:1, K_COL + HD:K_COL + P]).then_inc(rows_loaded, 16)
                    sp.dma_start(rows[C_KSW:C_KSW + 1, HD:P], b_in[0:1, K_COL:K_COL + HD]).then_inc(rows_loaded, 16)
                    sp.dma_start(rows[C_PS:C_PS + POOL_G, :], pool_scale[0].rearrange("(r n) -> r n", n=P)).then_inc(rows_loaded, 16)
                    sp.dma_start(cols[:, C_G0:C_G0 + ND], ln0_g.rearrange("(p c) -> p c", c=ND)).then_inc(rows_loaded, 16)
                    sp.dma_start(cols[:, C_B0:C_B0 + ND], ln0_b.rearrange("(p c) -> p c", c=ND)).then_inc(rows_loaded, 16)
                if t == 3:
                    load_unit(0)
                if t == 5:
                    load_unit(1)
                if t == NT - 1:
                    sp.dma_start(small[:, 0:HEADS], attn_sinks[0:1, :].to_broadcast([P, HEADS])).then_inc(consts_loaded, 16)
                    sp.dma_start(wpool[:, :, :], w_pool[0].rearrange("g c d -> c g d")).then_inc(consts_loaded, 16)
            for n in range(2, U_OUT + 4):
                load_unit(n)
            sp.wait_ge(mg_ready, MERGE_INCS * ND)
            for t in range(NT):
                sp.dma_start(xh[:, t, :], x_t[t]).then_inc(xr_loaded[t], 16)
                if t < 4:
                    load_unit(U_OUT + 4 + t)
                if t == 0:
                    sp.wait_ge(merged_ready, 2 * ND)
                    sp.dma_start(g1b[:, :], ln0_g.rearrange("(a n) -> a n", a=1).to_broadcast([P, D])).then_inc(r_loaded, 16)
                    sp.dma_start(b1b[:, :], ln0_b.rearrange("(a n) -> a n", a=1).to_broadcast([P, D])).then_inc(r_loaded, 16)
            sp.wait_ge(x0_ready, NT)
            sp.dma_start(g1b[:, :], ln1_g[0:1, :].to_broadcast([P, D])).then_inc(g1_loaded, 16)
            sp.dma_start(b1b[:, :], ln1_b[0:1, :].to_broadcast([P, D])).then_inc(g1_loaded, 16)
            for n in range(U_SH, U_SH + 4):
                load_unit(n)
            sp.wait_ge(mix_ready, 2 * NT)
            sp.dma_start(wr[:, :, :], w_router[0].rearrange("(p c) e -> p c e", c=ND)).then_inc(wr_loaded, 16)
            sp.dma_start(rbias[:, :], router_bias[0:1, :].to_broadcast([P, NE])).then_inc(wr_loaded, 16)
            for t in range(NT):
                sp.wait_ge(x1_ready, t + 1)
                sp.dma_start(x1_dram[t * P:(t + 1) * P, :], xh[:, t, :]).then_inc(x1_stored, 16)
            sp.wait_ge(pool_consts, 11)
            for d in (x1_dram, acc_dram):
                sp.dma_start(d[T:T + P, :], zrow[:, :]).then_inc(x1_stored, 16)
                sp.dma_start(d[T + P:T + SLOTS, :], zrow[0:SLOTS - P, :]).then_inc(x1_stored, 16)
            for n in range(U_SH + 4, U_SH + 6):
                load_unit(n)
            sp.wait_ge(sh_ready, 4)
            for j in range(2):
                w = W[j]
                sp.dma_start(w[:, 0:2048].rearrange("p (c f) -> p c f", c=ND), wg_e[j]).then_inc(gu_loaded[j], 16)
                sp.dma_start(w[:, 2048:4096].rearrange("p (c f) -> p c f", c=ND), wu_e[j]).then_inc(gu_loaded[j], 16)
                sp.dma_start(w[:, 4096:6144].rearrange("p (c d) -> p c d", c=NF), wd_e[j]).then_inc(wd_loaded[j], 16)
            for t in range(NT):
                sp.wait_ge(shd_taken, 2 * t + 2)
                sp.dma_start(acc_dram[t * P:(t + 1) * P, :], xh[:, t, :]).then_inc(acc_stored, 16)
            sp.dma_start(g2b[:, :], ln2_g[0:1, :].to_broadcast([P, D])).then_inc(g2_loaded, 16)
            sp.dma_start(b2b[:, :], ln2_b[0:1, :].to_broadcast([P, D])).then_inc(g2_loaded, 16)
            sp.wait_ge(tables_ready, 1)
            pairs = sp.value_load(n_pairs[0:1, 0:1], min_val=NE // 2, max_val=(NE + MAX_OVER) // 2)
            with sp.Fori(0, pairs - 1) as it:
                for j in range(2):
                    e = sp.value_load(etab[0:1, bass.ds(it * 2 + (j + 2), 1)], min_val=0, max_val=NE - 1)
                    w = W[j]
                    sp.wait_ge(gu_ready, it * 2 + (j + 1))
                    sp.dma_start(w[:, 0:2048].rearrange("p (o c f) -> p o c f", o=1, c=ND),
                                 wg_e[bass.ds(e, 1)].rearrange("e p c f -> p e c f")).then_inc(gu_loaded[j], 16)
                    sp.dma_start(w[:, 2048:4096].rearrange("p (o c f) -> p o c f", o=1, c=ND),
                                 wu_e[bass.ds(e, 1)].rearrange("e p c f -> p e c f")).then_inc(gu_loaded[j], 16)
                    sp.wait_ge(wd_split, it * 2 + (j + 1))
                    sp.dma_start(w[:, 4096:6144].rearrange("p (o c d) -> p o c d", o=1, c=NF),
                                 wd_e[bass.ds(e, 1)].rearrange("e p c d -> p e c d")).then_inc(wd_loaded[j], 16)
            for j in range(2):
                sp.wait_ge(scattered[j], pairs * 32)
            for t in range(NT):
                sp.dma_start(accin[:, t, :], acc_dram[t * P:(t + 1) * P, :]).then_inc(acc_loaded[t], 16)
            for t in range(NT):
                if t < NT - 1:
                    sp.wait_ge(out_scaled, t + 1)
                else:
                    sp.wait_ge(last_scaled, 1)
                sp.dma_start(out_t[t], accin[:, t, :]).then_inc(out_stored, 16)
            sp.wait_ge(out_stored, 16 * NT)

        @block.gpsimd
        def _(pool):
            gp = nc.gpsimd
            n = [0]

            def link(ins):
                n[0] += 1
                ins.then_inc(pool_chain, 1)
                pool.wait_ge(pool_chain, n[0])

            link(gp.memset(eps[:, :], EPS))
            link(gp.memset(ident[:, :], 0.0))
            gp.affine_select(out=ident[:, :], in_=ident[:, :], compare_op=ALU.not_equal, fill=1.0, base=0,
                             pattern=[[-1, P]], channel_multiplier=1).then_inc(ident_ready, 1)
            link(gp.iota(dist[:, :], [[-1, 2 * P]], base=P, channel_multiplier=1, allow_small_or_imprecise_dtypes=True))
            link(gp.affine_select(out=dist[:, :], in_=dist[:, :], compare_op=ALU.is_ge, fill=1.0e32, base=P,
                                  pattern=[[-1, 2 * P]], channel_multiplier=1))
            link(gp.affine_select(out=dist[:, :], in_=dist[:, :], compare_op=ALU.is_ge, fill=1.0e32, base=-1,
                                  pattern=[[1, 2 * P]], channel_multiplier=-1))
            gp.iota(inv[:, :, :], [[0, POOL_G], [1, 16]], base=1, channel_multiplier=0,
                    allow_small_or_imprecise_dtypes=True).then_inc(ident_ready, 1)
            for g in range(POOL_G):
                pool.wait_ge(proj_taken, 2 * (g + 1))
                if g >= 1:
                    pool.wait_ge(pdiff_ready, g)
                src = uT[:, g, :]
                for s in range(g + 1):
                    k = 1 << s
                    dst = ladder[:, s % 2, :]
                    link(gp.tensor_copy(dst[:, 0:k], src[:, 0:k]))
                    add = gp.tensor_tensor(dst[:, k:T], src[:, k:T], src[:, 0:T - k], ALU.add)
                    if s < g:
                        link(add)
                    else:
                        add.then_inc(ladder_ready, 1)
                    src = dst
            pool.wait_ge(r_loaded, 32)
            for t in range(NT):
                pool.wait_ge(x0hat_ready, t + 1)
                link(gp.tensor_tensor(xh[:, t, :], xh[:, t, :], g1b[:, :], ALU.mult))
                gp.tensor_tensor(xh[:, t, :], xh[:, t, :], b1b[:, :], ALU.add).then_inc(x0_ready, 1)
            pool.wait_ge(g1_loaded, 32)
            for t in range(NT):
                pool.wait_ge(ln1_ready, t + 1)
                link(gp.tensor_tensor(xh[:, t, :], xh[:, t, :], g1b[:, :], ALU.mult))
                gp.tensor_tensor(xh[:, t, :], xh[:, t, :], b1b[:, :], ALU.add).then_inc(x1_ready, 1)
                if t == NT - 1:
                    pool.wait_ge(mix_ready, 2 * NT)
                    gp.memset(zrow[:, :], 0.0).then_inc(pool_consts, 1)
                    gp.iota(iotas[:, :], [[1, SLOTS]], base=0, channel_multiplier=0, allow_small_or_imprecise_dtypes=True).then_inc(pool_consts, 1)
                    link(gp.memset(tri[:, :], 1.0))
                    gp.affine_select(out=tri[:, :], in_=tri[:, :], compare_op=ALU.is_gt, fill=0.0, base=0,
                                     pattern=[[1, P]], channel_multiplier=-1).then_inc(pool_consts, 1)
                    gp.memset(ones[:, :], 1.0).then_inc(pool_consts, 1)
                    gp.iota(trash[:, 0, :], [[CS, NC]], base=T, channel_multiplier=1, allow_small_or_imprecise_dtypes=True).then_inc(pool_consts, 1)
                    gp.iota(trash[:, 1, :], [[-CS, NC]], base=-T, channel_multiplier=-1, allow_small_or_imprecise_dtypes=True).then_inc(pool_consts, 1)
                    gp.iota(vlist[:, :, :, 0], [[0, NE], [P, NT]], base=0, channel_multiplier=0, allow_small_or_imprecise_dtypes=True).then_inc(pool_consts, 1)
                    gp.iota(vlist[:, :, :, 1], [[0, NE], [0, NT]], base=0, channel_multiplier=1, allow_small_or_imprecise_dtypes=True).then_inc(pool_consts, 1)
                    gp.memset(vlist[:, :, :, 2], 1.0).then_inc(pool_consts, 1)
                    gp.iota(over[:, 0, :], [[1, MAX_OVER]], base=0, channel_multiplier=0, allow_small_or_imprecise_dtypes=True).then_inc(pool_consts, 1)
                    gp.iota(etabf[:, 0:NE], [[1, NE]], base=0, channel_multiplier=0, allow_small_or_imprecise_dtypes=True).then_inc(pool_consts, 1)
            pool.wait_ge(x1_stored, 16 * (NT + 4))

            def gather(j):
                for c in range(NC):
                    gp.indirect_dma_start(out=xg[j][0:CS, c, :], out_offset=None, in_=x1_dram[:, :],
                                          in_offset=bass.IndirectOffsetOnAxis(ap=gidx[j][0:CS, c:c + 1], axis=0)
                                          ).then_inc(gathered[j], 16)

            for j in range(2):
                pool.wait_ge(idx_ready, j + 1)
                gather(j)
            pool.wait_ge(acc_stored, 16 * NT)
            def scatter(it, j):
                wait(pool, y_taken_dve, it * 4 + 2 * (j + 1))
                wait(pool, y_taken_act, it * 4 + 2 * (j + 1))
                wait(pool, scattered[1 - j], it * 32 + 32 * j)
                pool.sem_inc(pool_turn, 1)
                for c in range(NC):
                    gp.indirect_dma_start(out=acc_dram[:, :],
                                          out_offset=bass.IndirectOffsetOnAxis(ap=sidx[j][0:CS, c:c + 1], axis=0),
                                          in_=ysb[j][0:CS, c, :], in_offset=None,
                                          compute_op=ALU.add).then_inc(scattered[j], 16)

            def pair(it):
                for j in range(2):
                    wait(pool, xgT_ready, it * 2 + (j + 1))
                    wait(pool, idx_ready, it * 2 + (j + 3))
                    pool.sem_inc(pool_turn, 1)
                    gather(j)
                    behind(scatter, it, j)

            pair(0)
            pool.wait_ge(tables_ready, 1)
            pairs = pool.value_load(n_pairs[0:1, 0:1], min_val=NE // 2, max_val=(NE + MAX_OVER) // 2)
            with pool.Fori(1, pairs) as it:
                pair(it)
            last = pool.value_load(n_pairs[0:1, 1:2], min_val=NE // 2 - 1, max_val=(NE + MAX_OVER) // 2 - 1)
            scatter(last, 1)
            for j in range(2):
                pool.wait_ge(gathered[j], pairs * 32 + 32)
            pool.wait_ge(g2_loaded, 32)
            for t in range(NT - 1):
                pool.wait_ge(out_ready, t + 1)
                gp.tensor_tensor(accin[:, t, :], accin[:, t, :], b2b[:, :], ALU.add).then_inc(out_scaled, 1)

        @block.tensor
        def _(pe):
            mm = nc.tensor.matmul
            pe.wait_ge(ident_ready, 1)
            pe.wait_ge(rows_loaded, 16 * 6)
            nc.tensor.transpose(bank[7][:, 0:NROWS], rows[0:NROWS, :], ident[0:NROWS, 0:NROWS]).then_inc(rows_T, 1)
            for t in range(NT):
                pe.wait_ge(xhat_ready, t + 1)
                for c in range(ND):
                    if t == NT // 2:
                        pe.wait_ge(x0_full, c + 1)
                    if t == 0 and c == ND - 1:
                        pe.wait_ge(cols_ready, 1)
                    last = nc.tensor.transpose(bank[c][:, (t % 4) * P:(t % 4 + 1) * P], xhat[:, t % 4, c::ND], ident[:, :])
                last.then_inc(tr_ready, 1)

            def product(out, n, cols_of, rhs_of, chunks, before=None):
                _, hi, lo = unit(n)
                for i, k in enumerate(chunks):
                    if before:
                        pe.wait_ge(before[0], before[1] + i + 1)
                    for q, (a, b) in enumerate(SPLIT):
                        last = mm(out, (hi, lo)[a][:, cols_of(k)], rhs_of(k, b), start=i + q == 0,
                                  stop=i == len(chunks) - 1 and q == 2)
                return last

            def chunk_cols(k):
                return slice(k * P, (k + 1) * P)

            for n in range(NPROJ):
                pe.wait_ge(unit_split, n + 1)
                for h in range(2):
                    k = 2 * n + h
                    if k >= 4:
                        pe.wait_ge(proj_taken, k - 3)
                    else:
                        pe.wait_ge(x0_full, ND + k + 1)
                    product(bank[k % 4][:, :], n, chunk_cols, lambda c, b: XT[:, h, b, c, :], range(ND),
                            (tr_taken, ND * h) if n == 0 else None).then_inc(proj_ready, 1)
            pe.wait_ge(proj_taken, 2 * NPROJ)
            for h in range(2):
                for c in range(4):
                    last = nc.tensor.transpose(bank[4 + h][:, c * P:(c + 1) * P], vT[:, (4 * h + c) * P:(4 * h + c + 1) * P], ident[:, :])
                last.then_inc(v_ready, 1)
            pe.wait_ge(consts_loaded, 32)
            for g in range(POOL_G):
                pe.wait_ge(pdiff_ready, g + 1)
                for h in range(2):
                    m = 2 * g + h
                    if m >= 2:
                        pe.wait_ge(m_full_ready, m - 1)
                    mm(bank[6 + m % 2][:, :], wpool[:, g, :], pdiff[:, g, h * HALF:(h + 1) * HALF],
                       start=True, stop=True).then_inc(mixed_ready, 1)

            def scores_of(b):
                k0 = (b - 1) * P if b else 0
                w = 2 * P if b else P
                for h in range(HEADS):
                    if b:
                        pe.wait_ge(sc_taken, HEADS * (b - 1) + (h | 2) + 1)
                    lo = HD * (h % 2)
                    kk = 0 if h // (HEADS // 2) == h % 2 else 1
                    mm(score_place(h, w),
                       qT[lo:lo + HD, h // 2, b * P:(b + 1) * P],
                       kT[lo:lo + HD, kk, k0:k0 + w], start=True, stop=True).then_inc(sc_ready, 1)

            scores_of(0)
            scores_of(1)
            pe.wait_ge(v_taken, 2)
            pe.wait_ge(m_full_ready, 2 * POOL_G)
            for b in range(NT):
                kbs = (0, 1) if b else (1,)
                for h2 in range(HEADS // 2):
                    n = 4 * b + h2
                    pe.wait_ge(scaled, HEADS * b + 2 * h2 + 2)
                    if n >= 2:
                        pe.wait_ge(pt_taken, n - 1)
                    for hh in range(2):
                        h = 2 * h2 + hh
                        for kb in kbs:
                            src = S_sb[b % 2][:, h, kb * P:(kb + 1) * P] if b else S_sb[0][:, h, 0:P]
                            last = nc.tensor.transpose(bank[4 + n % 2][:, (2 * hh + kb) * P:(2 * hh + kb + 1) * P], src, ident[:, :])
                    last.then_inc(pt_ready, 1)
                if b + 2 < NT:
                    scores_of(b + 2)
                pe.wait_ge(pt_taken, 4 * b + 4)
                if b >= 2:
                    pe.wait_ge(o_taken, b - 1)
                for g in range(2):
                    for par in range(2):
                        for i, kb in enumerate(kbs):
                            first = 2 * (4 * g + par) + kb
                            last = mm(bank[6 + b % 2][HD * par:HD * (par + 1), 2 * g * P:(2 * g + 2) * P],
                                      v_sb[:, b - 1 + kb, g * HD:(g + 1) * HD], PT[:, first:first + 5:4, :],
                                      start=i == 0, stop=i == len(kbs) - 1)
                last.then_inc(pv_ready, 1)
            for c in range(ND):
                for q in range(3):
                    n = U_MERGE + 3 * c + q
                    pe.wait_ge(unit_split, n + 1)
                    if c == 0:
                        if q == 0:
                            pe.wait_ge(sc_taken, HEADS * NT)
                        if q == 2:
                            pe.wait_ge(o_taken, NT)
                    if q < 2:
                        for h in range(2):
                            if c:
                                pe.wait_ge(sg_ready, 4 * (c - 1) + 2 * q + h + 1)
                            product(bank[2 * q + h][:, :], n, chunk_cols, lambda k, b: XT[:, h, b, k, :], range(ND)).then_inc(mg_ready, 1)
                    else:
                        for i, src in enumerate((mixT, oT)):
                            for h in range(2):
                                if c:
                                    pe.wait_ge(merged_ready, 2 * (c - 1) + h + 1)
                                product(bank[4 + 2 * i + h][:, :], n, lambda k: slice((4 * i + k) * P, (4 * i + k + 1) * P),
                                        lambda k, b: src[:, b, k, h * HALF:(h + 1) * HALF], range(4)).then_inc(mg_ready, 1)
            pe.wait_ge(sg_ready, 4 * ND)
            pe.wait_ge(merged_ready, 2 * ND)
            for half in range(2):
                for k in range(ND):
                    if half == 0:
                        pe.wait_ge(unit_split, U_OUT + k + 1)
                    pe.wait_ge(piece_split, ND * half + k + 1)
                    _, hi, lo = unit(U_OUT + k)
                    for tt in range(4):
                        for n in range(2):
                            if half and k == 0:
                                pe.wait_ge(mix_taken, 2 * tt + n + 1)
                            for q, (a, b) in enumerate(SPLIT):
                                last = mm(bank[2 * tt + n][:, :], XT[:, half, a, k, tt * P:(tt + 1) * P],
                                          (hi, lo)[b][:, n * HALF:(n + 1) * HALF], start=k + q == 0, stop=k == ND - 1 and q == 2)
                            if k == ND - 1:
                                last.then_inc(mix_ready, 1)
                    if half and k < ND - 1:
                        last.then_inc(wo_done, 1)

            def x1_transposes(t):
                pe.wait_ge(x1_ready, t + 1)
                for h in range(2):
                    n = 2 * t + h
                    if n >= 4:
                        pe.wait_ge(x1T_taken, n - 3)
                    for c in range(4):
                        last = nc.tensor.transpose(bank[n % 4][:, c * P:(c + 1) * P], xh[:, t, 4 * h + c::ND], ident[:, :])
                    last.then_inc(x1T_ready, 1)

            def shared_gate_up(m):
                h, f = divmod(m, 2)
                if m == 0:
                    pe.wait_ge(unit_split, U_SH + 2)
                if m == 1:
                    pe.wait_ge(unit_split, U_SH + 4)
                if m >= 2:
                    pe.wait_ge(sh_h, m - 1)
                pe.wait_ge(x1T_taken, 8 * (h + 1))
                for q in range(2):
                    last = product(bank[4 + 2 * (m % 2) + q][:, :], U_SH + 2 * f + q, chunk_cols, lambda k, b: XT[:, h, b, k, :], range(ND))
                last.then_inc(sh_ready, 1)

            pe.wait_ge(mix_taken, 2 * NT)
            for t in range(4):
                x1_transposes(t)
            shared_gate_up(0)
            shared_gate_up(1)
            for t in range(4, NT):
                x1_transposes(t)
            pe.wait_ge(wr_ready, 2)
            pe.wait_ge(x1T_taken, 2 * NT)
            for h in range(2):
                for c in range(ND):
                    for q, (a, b) in enumerate(SPLIT):
                        last = mm(bank[h][0:NE, :], (wr_hi, wr_lo)[a][:, c, :], XT[:, h, b, c, :],
                                  start=c + q == 0, stop=c == ND - 1 and q == 2)
                last.then_inc(logits_ready, 1)
            for t in range(NT):
                if t % 4 == 0:
                    pe.wait_ge(scoresT_ready, t // 4 + 1)
                last = nc.tensor.transpose(bank[3][:, t * NE:(t + 1) * NE], scoresT[0:NE, t * P:(t + 1) * P], ident[0:NE, 0:NE])
            last.then_inc(scores_tr, 1)
            shared_gate_up(2)
            shared_gate_up(3)
            pe.wait_ge(mask_ready, 1)
            pe.wait_ge(pool_consts, 11)
            for t in range(NT):
                for s in range(t + 1):
                    last = mm(bank[1][:, t * NE:(t + 1) * NE], tri[:, :] if s == t else ones[:, :], maskb[:, s, :], start=s == 0, stop=s == t)
            for s in range(NT):
                last = mm(bank[2][:, 0:NE], ones[:, :], maskb[:, s, :], start=s == 0, stop=s == NT - 1)
            last.then_inc(pos_ready, 1)
            def shared_down(n):
                t, h = divmod(n, 2)
                if n >= 4:
                    pe.wait_ge(shd_taken, n - 3)
                for f in range(NF):
                    _, hi, lo = unit(U_SH + 4 + f)
                    for q, (a, b) in enumerate(SPLIT):
                        last = mm(bank[(4, 5, 3, 6)[n % 4]][:, :], hsh[:, a, f, t * P:(t + 1) * P],
                                  (hi, lo)[b][:, h * HALF:(h + 1) * HALF], start=f + q == 0, stop=f == NF - 1 and q == 2)
                last.then_inc(shd_ready, 1)

            pe.wait_ge(sh_h, 4)
            pe.wait_ge(unit_split, U_SH + 6)
            for n in range(4):
                shared_down(n)
            def make_list(e):
                for c in range(NC):
                    for t in range(NT):
                        row = vlist[:, e, t, :] if isinstance(e, int) else vlist[:, bass.ds(e, 1), t, :].rearrange("p o l -> p (o l)")
                        last = mm(bank[7][0:CS, c * LIST:(c + 1) * LIST], onehot[:, t, c * CS:(c + 1) * CS], row,
                                  start=t == 0, stop=t == NT - 1)
                last.then_inc(list_ready, 1)

            def transposes(j):
                for c in range(ND):
                    for q in range(NC):
                        last = nc.tensor.transpose(bank[c // 3][:, (c % 3) * SLOTS + q * CS:(c % 3) * SLOTS + (q + 1) * CS],
                                                   xg[j][0:CS, q, c::ND], ident[0:CS, 0:CS])
                last.then_inc(xgT_ready, 1)

            def gate_up(j):
                for q in range(2):
                    for f in range(NF):
                        for c in range(ND):
                            last = mm(bank[3 + q][:, f * SLOTS:(f + 1) * SLOTS],
                                      W[j][:, q * 2048 + c * FF + f * P:q * 2048 + c * FF + (f + 1) * P],
                                      xgT[j][:, c, :], start=c == 0, stop=c == ND - 1)
                last.then_inc(gu_ready, 1)

            for i in range(2):
                pe.wait_ge(onehot_ready, i + 1)
                if i:
                    pe.wait_ge(idx_ready, i)
                make_list(i)
            for n in range(4, 12):
                shared_down(n)
            pe.wait_ge(gathered[0], 32)
            transposes(0)
            for n in range(12, 2 * NT):
                shared_down(n)
            pe.wait_ge(shd_taken, 2 * NT)
            def down(it, j):
                wait(pe, h_ready, it * 2 + (j + 1))
                wait(pe, wd_split, it * 2 + (j + 1))
                for c in range(NC):
                    for h in range(2):
                        wait(pe, (y_taken_dve, y_taken_act)[h], it * 4 + 2 * j + c)
                        for f in range(NF):
                            for n, (a, b) in enumerate(((h_hi[j], wd_hi), (h_hi[j], wd_lo), (h_lo[j], wd_hi))):
                                last = mm(bank[5 + h][0:CS, :], a[:, f, c * CS:(c + 1) * CS], b[:, f, h * HALF:(h + 1) * HALF],
                                          start=f + n == 0, stop=f == NF - 1 and n == 2)
                        last.then_inc(y_ready, 1)

            def pair(it):
                for j in range(2):
                    e2 = j + 2 if isinstance(it, int) else pe.value_load(etab[0:1, bass.ds(it * 2 + (j + 2), 1)], min_val=0, max_val=NE - 1)
                    wait(pe, gu_loaded[j], it * 32 + 32)
                    wait(pe, xgT_taken, it * 6 + 3 * (j + 1))
                    wait(pe, h_ready_full, it * 2 + j)
                    gate_up(j)
                    wait(pe, gathered[1 - j], it * 32 + 32 * (1 + j))
                    transposes(1 - j)
                    wait(pe, onehot_ready, it * 2 + (j + 3))
                    wait(pe, idx_ready, it * 2 + (j + 2))
                    make_list(e2)
                    behind(down, it, j)

            pair(0)
            pe.wait_ge(tables_ready, 1)
            pairs = pe.value_load(n_pairs[0:1, 0:1], min_val=NE // 2, max_val=(NE + MAX_OVER) // 2)
            with pe.Fori(1, pairs) as it:
                pair(it)
            last = pe.value_load(n_pairs[0:1, 1:2], min_val=NE // 2 - 1, max_val=(NE + MAX_OVER) // 2 - 1)
            down(last, 1)

        @block.scalar
        def _(act):
            A = nc.scalar.activation

            def root(t, round_):
                act.wait_ge(var_ready, round_ * NT + t + 1)
                s, m = (std0, mean_var0) if round_ == 0 else (std, mean_var)
                A(s[:, t:t + 1], m[:, t, 1:2], ACT.Sqrt, bias=eps[:, :]).then_inc(std_ready, 1)

            def unit_high(n):
                wait_unit_loaded(act, n)
                raw, hi, _ = unit(n)
                A(hi[:, :], raw[:, :], ACT.Copy).then_inc(unit_hi, 1)

            act.wait_ge(ident_ready, 1)
            for t in range(4):
                root(t, 0)
            act.wait_ge(cols_ready, 1)
            for n in range(2 * ND):
                half, c = divmod(n, ND)
                if half == 0 and n % 2:
                    root(4 + n // 2, 0)
                act.wait_ge(tr_ready, 4 * (half + 1))
                if n >= 2:
                    act.wait_ge(tr_taken, n - 1)
                A(x_full[:, n % 2, :], bank[c][:, :], ACT.Identity, scale=cols[:, C_G0 + c:C_G0 + c + 1],
                  bias=cols[:, C_B0 + c:C_B0 + c + 1]).then_inc(x0_full, 1)
                act.wait_ge(x0_full, n + 1)
                A(XT[:, half, 0, c, :], x_full[:, n % 2, :], ACT.Copy).then_inc(x0_hi, 1)
                if n in (ND - 1, ND + 3):
                    unit_high(n // ND)
            for n in range(NPROJ):
                if n + 2 < NPROJ + 2:
                    unit_high(n + 2)
                kind, c, col = win_k[n]
                dst = {"u": uT, "q": qT, "k": kT}[kind][:, c, :] if kind != "v" else vT[:, :]
                bcol = C_KSW if col is None else col // P
                for h in range(2):
                    k = 2 * n + h
                    act.wait_ge(proj_ready, k + 1)
                    A(dst[:, h * HALF:(h + 1) * HALF], bank[k % 4][:, :], ACT.Identity,
                      bias=cols[:, bcol:bcol + 1]).then_inc(proj_taken, 1)
            for g in range(POOL_G):
                for h in range(2):
                    m = 2 * g + h
                    act.wait_ge(mixed_ready, m + 1)
                    if m >= 2:
                        act.wait_ge(mixed_taken, m - 1)
                    A(m_full[:, m % 2, :], bank[6 + m % 2][:, :], ACT.Copy, scale=cols[:, C_PS + g:C_PS + g + 1]).then_inc(m_full_ready, 1)
                    act.wait_ge(m_full_ready, m + 1)
                    act.wait_ge(ladder_ready, g + 1)
                    A(mixT[:, 0, g, h * HALF:(h + 1) * HALF], m_full[:, m % 2, :], ACT.Copy).then_inc(m_hi_ready, 1)

            def exps(b):
                w = 2 * P if b else P
                act.wait_ge(negm_ready, b + 1)
                for h in range(HEADS):
                    A(S_sb[b % 2][:, h, 0:w], S_sb[b % 2][:, h, 0:w], ACT.Exp, scale=HD ** -0.5, bias=small[:, 32 + h:33 + h],
                      accum_out=small[:, 40 + h:41 + h]).then_inc(exp_done, 1)
                A(small[:, 56:64], small[:, 48:56], ACT.Exp).then_inc(sink_exp, 1)

            def divide(b):
                w = 2 * P if b else P
                act.wait_ge(rden_ready, b + 1)
                for h in range(HEADS):
                    A(S_sb[b % 2][:, h, 0:w], S_sb[b % 2][:, h, 0:w], ACT.Copy, scale=small[:, 24 + h:25 + h]).then_inc(scaled, 1)

            exps(0)
            divide(0)
            for b in range(NT):
                if b + 1 < NT:
                    exps(b + 1)
                    divide(b + 1)
                act.wait_ge(pv_ready, b + 1)
                A(oT[:, 0, :, b * P:(b + 1) * P], bank[6 + b % 2][:, :].rearrange("p (c q) -> p c q", c=QC), ACT.Copy).then_inc(o_hi_ready, 1)
            for c in range(ND):
                for q in range(3):
                    n = U_MERGE + 3 * c + q
                    if c == ND - 1 and q == 1:
                        pass
                    unit_high(n + 2)
                    if q < 2:
                        for h in range(2):
                            act.wait_ge(mg_ready, MERGE_INCS * c + 2 * q + h + 1)
                            if c:
                                act.wait_ge(merged_ready, 2 * (c - 1) + h + 1)
                            A(gate_sb[:, 2 * q + h, :], bank[2 * q + h][:, :], ACT.Sigmoid,
                              bias=cols[:, GP_COL // P + q * ND + c:GP_COL // P + q * ND + c + 1]).then_inc(sg_ready, 1)

            def piece_high(half, k):
                A(XT[:, half, 0, k, :], mergedT[:, k, half * HALF:(half + 1) * HALF], ACT.Copy).then_inc(piece_hi, 1)

            act.wait_ge(mg_ready, MERGE_INCS * ND)
            act.wait_ge(merged_ready, 2 * ND)
            for k in range(ND):
                piece_high(0, k)
                if 2 <= U_OUT + k + 2 - U_OUT < ND:
                    unit_high(U_OUT + k + 2)
            for k in range(ND):
                piece_high(1, k)
            for t in range(4):
                root(t, 1)
            unit_high(U_SH)
            unit_high(U_SH + 1)
            for t in range(NT):
                for h in range(2):
                    n = 2 * t + h
                    act.wait_ge(x1T_ready, n + 1)
                    A(XT[:, t // 4, 0, 4 * h:4 * h + 4, (t % 4) * P:(t % 4 + 1) * P],
                      bank[n % 4][:, :].rearrange("p (c q) -> p c q", c=4), ACT.Copy).then_inc(x1_hi, 1)
                if t == 3:
                    unit_high(U_SH + 2)
                    unit_high(U_SH + 3)
                    act.wait_ge(wr_loaded, 32)
                    A(wr_hi[:, :, :], wr[:, :, :], ACT.Copy).then_inc(wr_ready, 1)
                    for i in range(4, NT):
                        root(i, 1)
                    for m in range(2):
                        act.wait_ge(sh_ready, m + 1)
                        if m:
                            act.wait_ge(sh_full, m)
                        A(sig_sh[:, :], bank[4 + 2 * m][:, :], ACT.Sigmoid).then_inc(sh_sig, 1)
                        act.wait_ge(sh_full, m + 1)
                        A(hsh[:, 0, m, 0:HALF], h_sh[:, :], ACT.Copy).then_inc(sh_hi, 1)
            for h in range(2):
                act.wait_ge(logits_ready, h + 1)
                A(scoresT[0:NE, h * HALF:(h + 1) * HALF], bank[h][0:NE, :], ACT.Sigmoid).then_inc(scoresT_ready, 1)
            act.wait_ge(scores_tr, 1)
            A(scores[:, :, :], bank[3][:, :].rearrange("p (t e) -> p t e", t=NT), ACT.Copy).then_inc(score_ready, 1)
            for m in range(2, 4):
                act.wait_ge(sh_ready, m + 1)
                act.wait_ge(sh_full, m)
                A(sig_sh[:, :], bank[4 + 2 * (m % 2)][:, :], ACT.Sigmoid).then_inc(sh_sig, 1)
                act.wait_ge(sh_full, m + 1)
                A(hsh[:, 0, m % 2, HALF:T], h_sh[:, :], ACT.Copy).then_inc(sh_hi, 1)
                if m == 2:
                    unit_high(U_SH + 4)
                    unit_high(U_SH + 5)

            def take_transposes(j):
                for q, n in ((0, 3), (1, 3), (2, 2)):
                    A(xgT[j][:, 3 * q:3 * q + n, :], bank[q][:, 0:n * SLOTS].rearrange("p (c s) -> p c s", c=n),
                      ACT.Copy).then_inc(xgT_taken, 1)

            act.wait_ge(xgT_ready, 1)
            take_transposes(0)
            act.wait_ge(acc_stored, 16 * NT)
            def take_y(it, j):
                wait(act, sidx_ready, it * 2 + (j + 1))
                for c in range(NC):
                    wait(act, y_ready, it * 8 + 4 * j + 2 * c + 2)
                    A(ysb[j][0:CS, c, HALF:D], bank[6][0:CS, :], ACT.Copy, scale=sgate[j][0:CS, c, :]).then_inc(y_taken_act, 1)

            def pair(it):
                for j in range(2):
                    wait(act, gu_ready, it * 2 + (j + 1))
                    wait(act, h_ready_full, it * 2 + j)
                    A(sig[:, :, :], bank[3][:, 0:NF * SLOTS].rearrange("p (f s) -> p f s", f=NF), ACT.Sigmoid).then_inc(sig_ready, 1)
                    wait(act, h_ready_full, it * 2 + (j + 1))
                    A(h_hi[j][:, :, :], h_full[:, :, :], ACT.Copy).then_inc(h_hi_ready, 1)
                    wait(act, xgT_ready, it * 2 + (j + 2))
                    take_transposes(1 - j)
                    behind(take_y, it, j)
                    wait(act, wd_loaded[j], it * 16 + 16)
                    wait(act, y_ready, it * 8 + 4 * j)
                    A(wd_hi[:, :, :], W[j][:, 4096:6144].rearrange("p (f d) -> p f d", f=NF), ACT.Copy).then_inc(wd_hi_ready, 1)

            pair(0)
            act.wait_ge(tables_ready, 1)
            pairs = act.value_load(n_pairs[0:1, 0:1], min_val=NE // 2, max_val=(NE + MAX_OVER) // 2)
            with act.Fori(1, pairs) as it:
                pair(it)
            last = act.value_load(n_pairs[0:1, 1:2], min_val=NE // 2 - 1, max_val=(NE + MAX_OVER) // 2 - 1)
            take_y(last, 1)
            root(0, 2)
            for t in range(NT):
                if t + 1 < NT:
                    root(t + 1, 2)
                act.wait_ge(scale_ready, t + 1)
                A(accin[:, t, :], accin[:, t, :], ACT.Identity, scale=std[:, t:t + 1], bias=small[:, 128 + t:129 + t]).then_inc(normal_ready, 1)

        @block.vector
        def _(dve):
            v = nc.vector
            n = [0]

            def link(ins):
                n[0] += 1
                ins.then_inc(dve_chain, 1)
                dve.wait_ge(dve_chain, n[0])

            stats = small[:, 64:76].rearrange("p (a b) -> p a b", a=2)

            def statistics(src, t, round_):
                m = (mean_var0, mean_var)[round_]
                if t or round_:
                    dve.wait_ge(var_ready, NT * round_ + t)
                for h in range(2):
                    v.bn_stats(stats[:, h, :], src[:, h * HALF:(h + 1) * HALF]).then_inc(dve_chain, 1)
                n[0] += 2
                dve.wait_ge(dve_chain, n[0])
                v.bn_aggr(m[:, t, :], small[:, 64:76]).then_inc(var_ready, 1)

            def normalise(dst, src, t, round_, signal):
                m, s = ((mean_var0, std0), (mean_var, std))[round_]
                dve.wait_ge(std_ready, round_ * NT + t + 1)
                link(v.reciprocal(s[:, t:t + 1], s[:, t:t + 1]))
                v.tensor_scalar(dst, src, m[:, t, 0:1], s[:, t:t + 1], ALU.subtract, ALU.mult).then_inc(signal, 1)

            def unit_low(k):
                raw, hi, lo = unit(k)
                dve.wait_ge(unit_hi, k + 1)
                v.tensor_tensor(lo[:, :], raw[:, :], hi[:, :].bitcast(f32), ALU.subtract).then_inc(unit_split, 1)

            def x0_low(m):
                half, c = divmod(m, ND)
                dve.wait_ge(x0_hi, m + 1)
                v.tensor_tensor(XT[:, half, 1, c, :], x_full[:, m % 2, :], XT[:, half, 0, c, :].bitcast(f32),
                                ALU.subtract).then_inc(tr_taken, 1)

            for t in range(NT):
                dve.wait_ge(x_loaded[t % XBUF], 16 * (t // XBUF + 1))
                statistics(xin[:, t % XBUF, :], t, 0)
                if t >= 4:
                    x0_low(2 * (t - 4))
                    dve.wait_ge(tr_ready, t - 3)
                normalise(xhat[:, t % 4, :], xin[:, t % XBUF, :], t, 0, xhat_ready)
                if t == 0:
                    dve.wait_ge(rows_T, 1)
                    v.tensor_copy(cols[:, 0:NROWS], bank[7][:, 0:NROWS]).then_inc(cols_ready, 1)
                if t >= 4:
                    x0_low(2 * (t - 4) + 1)
            unit_low(0)
            for m in range(ND, 2 * ND):
                x0_low(m)
                if m == ND + 3:
                    unit_low(1)
            dve.wait_ge(ident_ready, 2)
            for g in range(POOL_G):
                link(v.tensor_scalar(inv[:, g, :], inv[:, g, :], float(2 << g), None, ALU.min))
                link(v.reciprocal(inv[:, g, :], inv[:, g, :]))

            def pool_difference(g):
                dve.wait_ge(ladder_ready, g + 1)
                sm = ladder[:, g % 2, :]
                link(v.tensor_tensor(pdiff[:, g, 0:16], sm[:, 0:16], inv[:, g, :], ALU.mult))
                link(v.tensor_tensor(pdiff[:, g, 0:16], pdiff[:, g, 0:16], uT[:, g, 0:16], ALU.subtract))
                v.scalar_tensor_tensor(pdiff[:, g, 16:T], sm[:, 16:T], 1.0 / (2 << g), uT[:, g, 16:T], ALU.mult,
                                       ALU.subtract).then_inc(pdiff_ready, 1)

            for k in range(NPROJ):
                unit_low(k + 2)
                if k >= 5 and (k - 5) < POOL_G:
                    pool_difference(k - 5)
            for h in range(2):
                dve.wait_ge(v_ready, h + 1)
                v.tensor_copy(v_sb[:, 4 * h:4 * h + 4, :], bank[4 + h][:, :].rearrange("p (t c) -> p t c", t=4)).then_inc(v_taken, 1)
            for m in range(2 * POOL_G):
                g, h = divmod(m, 2)
                dve.wait_ge(m_hi_ready, m + 1)
                dve.wait_ge(mixed_ready, 2 * g + 2)
                v.tensor_tensor(mixT[:, 1, g, h * HALF:(h + 1) * HALF], m_full[:, m % 2, :],
                                mixT[:, 0, g, h * HALF:(h + 1) * HALF].bitcast(f32), ALU.subtract).then_inc(mixed_taken, 1)

            def softmax_statistics(b):
                w = 2 * P if b else P
                S = S_sb[b % 2]
                if b >= 2:
                    dve.wait_ge(pt_ready, 4 * (b - 1))
                for h in range(HEADS):
                    dve.wait_ge(sc_ready, HEADS * b + (h | 2) + 1)
                    slope = 2.0 ** (-8.0 * (h + 1) / HEADS)
                    v.scalar_tensor_tensor(S[:, h, 0:w], dist[:, 2 * P - w:2 * P], -slope * HD ** 0.5,
                                           score_place(h, w), ALU.mult, ALU.add).then_inc(sc_taken, 1)
                dve.wait_ge(sc_taken, HEADS * (b + 1))
                link(v.tensor_reduce(small[:, 8:16], S[:, :, 0:w], axis=AX.X, op=ALU.max))
                link(v.scalar_tensor_tensor(small[:, 16:24], small[:, 8:16], HD ** -0.5, small[:, 0:8], ALU.mult, ALU.max))
                link(v.tensor_tensor(small[:, 48:56], small[:, 0:8], small[:, 16:24], ALU.subtract))
                v.tensor_scalar(small[:, 32:40], small[:, 16:24], -1.0, None, ALU.mult).then_inc(negm_ready, 1)

            def denominators(b):
                dve.wait_ge(sink_exp, b + 1)
                dve.wait_ge(exp_done, HEADS * (b + 1))
                if b:
                    dve.wait_ge(scaled, HEADS * b)
                link(v.tensor_tensor(small[:, 24:32], small[:, 40:48], small[:, 56:64], ALU.add))
                v.reciprocal(small[:, 24:32], small[:, 24:32]).then_inc(rden_ready, 1)

            dve.wait_ge(consts_loaded, 32)
            dve.wait_ge(mixed_taken, 2 * POOL_G)
            softmax_statistics(0)
            denominators(0)
            softmax_statistics(1)
            for b in range(NT):
                for q in range(4):
                    m = 4 * b + q
                    dve.wait_ge(pt_ready, m + 1)
                    if b and q == 0:
                        dve.wait_ge(pv_ready, b)
                    src = bank[4 + m % 2][:, :].rearrange("p (a c) -> p a c", a=4)
                    if b:
                        v.tensor_copy(PT[:, 4 * q:4 * q + 4, :], src).then_inc(pt_taken, 1)
                    else:
                        v.tensor_copy(PT[:, 4 * q + 1:4 * q + 4:2, :], src[:, 1::2, :]).then_inc(pt_taken, 1)
                if b + 1 < NT:
                    denominators(b + 1)
                if b + 2 < NT:
                    softmax_statistics(b + 2)
                dve.wait_ge(o_hi_ready, b + 1)
                v.tensor_tensor(oT[:, 1, :, b * P:(b + 1) * P], bank[6 + b % 2][:, :].rearrange("p (c q) -> p c q", c=QC),
                                oT[:, 0, :, b * P:(b + 1) * P].bitcast(f32), ALU.subtract).then_inc(o_taken, 1)
            for c in range(ND):
                for q in range(3):
                    unit_low(U_MERGE + 3 * c + q + 2)
                for h in range(2):
                    for q in range(2):
                        dve.wait_ge(mg_ready, MERGE_INCS * c + 4 + 2 * q + h + 1)
                        dve.wait_ge(sg_ready, 4 * c + 2 * q + h + 1)
                        v.tensor_tensor(gate_sb[:, 2 * q + h, :], gate_sb[:, 2 * q + h, :], bank[4 + 2 * q + h][:, :], ALU.mult).then_inc(dve_chain, 1)
                    n[0] += 2
                    dve.wait_ge(dve_chain, n[0])
                    v.tensor_tensor(mergedT[:, c, h * HALF:(h + 1) * HALF], gate_sb[:, h, :], gate_sb[:, 2 + h, :], ALU.add).then_inc(merged_ready, 1)

            def piece_low(half, k):
                dve.wait_ge(piece_hi, ND * half + k + 1)
                v.tensor_tensor(XT[:, half, 1, k, :], mergedT[:, k, half * HALF:(half + 1) * HALF],
                                XT[:, half, 0, k, :].bitcast(f32), ALU.subtract).then_inc(piece_split, 1)

            for k in range(ND):
                piece_low(0, k)
                if k + 2 < ND:
                    unit_low(U_OUT + k + 2)
            for t in range(NT):
                dve.wait_ge(xr_loaded[t], 16)
                v.tensor_scalar(xh[:, t, :], xh[:, t, :], mean_var0[:, t, 0:1], std0[:, t:t + 1], ALU.subtract, ALU.mult).then_inc(x0hat_ready, 1)
            for k in range(ND):
                piece_low(1, k)

            def residual(t):
                dve.wait_ge(x0_ready, t + 1)
                for h in range(2):
                    dve.wait_ge(mix_ready, 2 * t + h + 1)
                    v.scalar_tensor_tensor(xh[:, t, h * HALF:(h + 1) * HALF], xh[:, t, h * HALF:(h + 1) * HALF], ALPHA,
                                           bank[2 * (t % 4) + h][:, :], ALU.mult, ALU.add).then_inc(mix_taken, 1)

            def x1_low(t):
                for h in range(2):
                    m = 2 * t + h
                    dve.wait_ge(x1_hi, m + 1)
                    XTt = XT[:, t // 4, :, 4 * h:4 * h + 4, (t % 4) * P:(t % 4 + 1) * P]
                    v.tensor_tensor(XTt[:, 1], bank[m % 4][:, :].rearrange("p (c q) -> p c q", c=4),
                                    XTt[:, 0].bitcast(f32), ALU.subtract).then_inc(x1T_taken, 1)

            def shared_h(m):
                h, f = divmod(m, 2)
                g, u = bank[4 + 2 * (m % 2)], bank[5 + 2 * (m % 2)]
                dve.wait_ge(sh_sig, m + 1)
                link(v.tensor_tensor(sig_sh[:, :], sig_sh[:, :], g[:, :], ALU.mult))
                if m:
                    dve.wait_ge(sh_h, m)
                v.tensor_tensor(h_sh[:, :], sig_sh[:, :], u[:, :], ALU.mult).then_inc(sh_full, 1)
                dve.wait_ge(sh_hi, m + 1)
                v.tensor_tensor(hsh[:, 1, f, h * HALF:(h + 1) * HALF], h_sh[:, :],
                                hsh[:, 0, f, h * HALF:(h + 1) * HALF].bitcast(f32), ALU.subtract).then_inc(sh_h, 1)

            for t in range(4):
                residual(t)
            dve.wait_ge(mix_taken, NT)
            for t in range(4):
                statistics(xh[:, t, :], t, 1)
                normalise(xh[:, t, :], xh[:, t, :], t, 1, ln1_ready)
            unit_low(U_SH)
            unit_low(U_SH + 1)
            for t in range(4, NT):
                residual(t)
            for t in range(4):
                x1_low(t)
            unit_low(U_SH + 2)
            unit_low(U_SH + 3)
            dve.wait_ge(wr_ready, 1)
            v.tensor_tensor(wr_lo[:, :, :], wr[:, :, :], wr_hi[:, :, :].bitcast(f32), ALU.subtract).then_inc(wr_ready, 1)
            dve.wait_ge(mix_taken, 2 * NT)
            for t in range(4, NT):
                statistics(xh[:, t, :], t, 1)
                normalise(xh[:, t, :], xh[:, t, :], t, 1, ln1_ready)
            shared_h(0)
            shared_h(1)
            for t in range(4, NT):
                x1_low(t)
            dve.wait_ge(score_ready, 1)
            dve.wait_ge(wr_loaded, 32)
            link(v.tensor_tensor(biased[:, :, :], scores[:, :, :], rbias[:, :].rearrange("p (o e) -> p o e", o=1).to_broadcast([P, NT, NE]), ALU.add))
            for t in range(NT):
                for g in range(GROUPS):
                    v.max(top[:, t, g, :], biased[:, t, g * PER_GROUP:(g + 1) * PER_GROUP]).then_inc(dve_chain, 1)
            n[0] += NT * GROUPS
            dve.wait_ge(dve_chain, n[0])
            link(v.tensor_tensor(gs[:, :, :], top[:, :, :, 0], top[:, :, :, 1], ALU.add))
            for t in range(NT):
                v.max(gtop[:, t, :], gs[:, t, :]).then_inc(dve_chain, 1)
            n[0] += NT
            dve.wait_ge(dve_chain, n[0])
            link(v.memset(gtop[:, :, KEEP_GROUPS:8], -NEG))
            for t in range(NT):
                v.match_replace(etop[:, t, :], gtop[:, t, :], gs[:, t, :], NEG).then_inc(dve_chain, 1)
            n[0] += NT
            dve.wait_ge(dve_chain, n[0])
            link(v.tensor_tensor(gs[:, :, :], etop[:, :, :], gs[:, :, :], ALU.is_equal))
            link(v.tensor_scalar(gs[:, :, :], gs[:, :, :], NEG, None, ALU.mult))
            link(v.tensor_tensor(work[:, :, :].rearrange("p t (g k) -> p (t g) k", g=GROUPS),
                                 biased[:, :, :].rearrange("p t (g k) -> p (t g) k", g=GROUPS),
                                 gs[:, :, :].rearrange("p t (g o) -> p (t g) o", o=1).to_broadcast([P, NT * GROUPS, PER_GROUP]), ALU.add))
            for t in range(NT):
                v.max(etop[:, t, :], work[:, t, :]).then_inc(dve_chain, 1)
            n[0] += NT
            dve.wait_ge(dve_chain, n[0])
            for t in range(NT):
                v.match_replace(mask[:, t, :], etop[:, t, :], work[:, t, :], 2 * NEG).then_inc(dve_chain, 1)
            n[0] += NT
            dve.wait_ge(dve_chain, n[0])
            link(v.tensor_tensor(mask[:, :, :], mask[:, :, :], work[:, :, :], ALU.not_equal))
            v.tensor_copy(maskb[:, :, :], mask[:, :, :]).then_inc(mask_ready, 1)
            link(v.tensor_tensor(gates[:, :, :], scores[:, :, :], mask[:, :, :], ALU.mult))
            link(v.tensor_reduce(gsum[:, :], gates[:, :, :], axis=AX.X, op=ALU.add))
            link(v.reciprocal(gsum[:, :], gsum[:, :]))
            link(v.tensor_tensor(gates[:, :, :], gates[:, :, :], gsum[:, :].rearrange("p (t o) -> p t o", o=1).to_broadcast([P, NT, NE]), ALU.mult))
            link(v.tensor_scalar(gates[:, :, :], gates[:, :, :], ROUTED_SCALE, None, ALU.mult))
            dve.wait_ge(pool_consts, 11)
            for q in range(3):
                part = vlist[:, :, :, 3 + q].rearrange("p e t -> p t e")
                link(v.tensor_copy(part, gates[:, :, :]))
                if q < 2:
                    link(v.tensor_tensor(gates[:, :, :], gates[:, :, :], part, ALU.subtract))
            shared_h(2)
            unit_low(U_SH + 4)
            unit_low(U_SH + 5)
            shared_h(3)
            dve.wait_ge(pos_ready, 1)
            pt = posm[:, :, :].rearrange("p e t -> p t e")
            link(v.scalar_tensor_tensor(pt, bank[1][:, :].rearrange("p (t e) -> p t e", t=NT), 1.0, mask[:, :, :], ALU.add, ALU.mult))
            link(v.tensor_scalar(pt, pt, -1.0, None, ALU.add))
            link(v.tensor_copy(extra[:, 3, :], bank[2][:, 0:NE]))
            def make_onehot(e):
                slot, base = (posm[:, e, :], iotas) if isinstance(e, int) else (posm[:, bass.ds(e, 1), :].rearrange("p o t -> p (o t)"), iotab)
                v.tensor_tensor(onehot[:, :, :], slot.rearrange("p (t o) -> p t o", o=1).to_broadcast([P, NT, SLOTS]),
                                base[:, :].rearrange("p (o s) -> p o s", o=1).to_broadcast([P, NT, SLOTS]),
                                ALU.is_equal).then_inc(onehot_ready, 1)

            def make_index(j, chain):
                lp = bank[7][0:CS, 0:NC * LIST].rearrange("p (c l) -> p c l", c=NC)
                lf = lst[j]
                chain(v.tensor_reduce(lf[0:CS, :, 0], lp[:, :, 0:2], axis=AX.X, op=ALU.add), 0)
                chain(v.tensor_reduce(lf[0:CS, :, 1], lp[:, :, 3:6], axis=AX.X, op=ALU.add), 1)
                chain(v.tensor_tensor(tmp[0:CS, :, 0], lp[:, :, 2], trash[0:CS, 1, :], ALU.mult), 2)
                chain(v.tensor_tensor(tmp[0:CS, :, 0], tmp[0:CS, :, 0], trash[0:CS, 0, :], ALU.add), 3)
                v.tensor_tensor(gidx[j][0:CS, :], tmp[0:CS, :, 0], lf[0:CS, :, 0], ALU.add).then_inc(idx_ready, 1)

            for i in range(2):
                if i:
                    dve.wait_ge(list_ready, i)
                make_onehot(i)
                dve.wait_ge(list_ready, i + 1)
                make_index(i, lambda ins, q: link(ins))
            dve.wait_ge(x1_stored, 16 * (NT + 4))
            def accumulator(pieces_):
                for m in pieces_:
                    t, h = divmod(m, 2)
                    dve.wait_ge(shd_ready, m + 1)
                    v.scalar_tensor_tensor(xh[:, t, h * HALF:(h + 1) * HALF], xh[:, t, h * HALF:(h + 1) * HALF], ALPHA,
                                           bank[(4, 5, 3, 6)[m % 4]][:, :], ALU.mult, ALU.add).then_inc(shd_taken, 1)

            accumulator(range(4))
            link(v.tensor_scalar(extra[:, 0, :], extra[:, 3, :], float(SLOTS), None, ALU.is_gt))
            for k in range(2, T // SLOTS + 1):
                link(v.tensor_scalar(extra[:, 1, :], extra[:, 3, :], float(k * SLOTS), None, ALU.is_gt))
                link(v.tensor_tensor(extra[:, 0, :], extra[:, 0, :], extra[:, 1, :], ALU.add))
            link(v.memset(extra[:, 1, :], 1.0))
            link(v.tensor_tensor_scan(extra[:, 2, :], extra[:, 1, :], extra[:, 0, :], 0.0, ALU.mult, ALU.add))
            link(v.tensor_copy(extra_b[:, 0, :], extra[:, 0, :]))
            link(v.tensor_copy(extra_b[:, 1, :], extra[:, 2, :]))
            link(v.tensor_copy(over_b[:, :], over[:, 0, :]))
            link(v.tensor_tensor(cmp[:, :, :], extra_b[:, 1, :].rearrange("p (o e) -> p o e", o=1).to_broadcast([P, MAX_OVER, NE]),
                                 over_b[:, :].rearrange("p (o e) -> p o e", e=1).to_broadcast([P, MAX_OVER, NE]), ALU.is_le))
            accumulator(range(4, 7))
            link(v.tensor_reduce(over[:, 1, :], cmp[:, :, :], axis=AX.X, op=ALU.add))
            accumulator(range(7, 10))
            link(v.tensor_tensor(cmp[:, :, :], cmp[:, :, :], extra_b[:, 0, :].rearrange("p (o e) -> p o e", o=1).to_broadcast([P, MAX_OVER, NE]), ALU.mult))
            accumulator(range(10, 13))
            link(v.tensor_reduce(over[:, 2, :], cmp[:, :, :], axis=AX.X, op=ALU.add))
            accumulator(range(13, 16))
            link(v.tensor_tensor(over[:, 2, :], over[:, 0, :], over[:, 2, :], ALU.subtract))
            link(v.tensor_scalar(over[:, 2, :], over[:, 2, :], 1.0, float(SLOTS), ALU.add, ALU.mult))
            link(v.tensor_scalar(over[:, 3, :], over[:, 1, :], float(NE), FAR, ALU.is_ge, ALU.mult))
            link(v.memset(btab[:, :], 0.0))
            link(v.memset(btab[:, NE + MAX_OVER:NTAB], FAR))
            link(v.tensor_tensor(btab[:, NE:NE + MAX_OVER], over[:, 2, :], over[:, 3, :], ALU.add))
            link(v.memset(etabf[:, NE + MAX_OVER:NTAB], 0.0))
            link(v.tensor_scalar(etabf[:, NE:NE + MAX_OVER], over[:, 1, :], float(NE - 1), None, ALU.min))
            link(v.tensor_copy(etab[:, :], etabf[:, :]))
            link(v.tensor_scalar(over[:, 1, :], over[:, 0, :], extra[:, 2, NE - 1:NE], None, ALU.is_lt))
            link(v.tensor_reduce(small[:, 80:81], over[:, 1, 0:MAX_OVER:2], axis=AX.X, op=ALU.add))
            link(v.tensor_scalar(n_pairs[:, 0:1], small[:, 80:81], float(NE // 2), None, ALU.add))
            v.tensor_scalar(n_pairs[:, 1:2], small[:, 80:81], float(NE // 2 - 1), None, ALU.add).then_inc(tables_ready, 1)
            dve.wait_ge(acc_stored, 16 * NT)
            n0 = n[0]
            STEPS = 7
            def take_y(it, j, chunks=range(NC)):
                for c in chunks:
                    wait(dve, y_ready, it * 8 + 4 * j + 2 * c + 1)
                    v.tensor_scalar(ysb[j][0:CS, c, 0:HALF], bank[5][0:CS, :], sgate[j][0:CS, c, :], None, ALU.mult).then_inc(y_taken_dve, 1)

            def pair(it):
                for j in range(2):
                    def chain(ins, q):
                        ins.then_inc(dve_chain, 1)
                        dve.wait_ge(dve_chain, it * (2 * STEPS) + (n0 + j * STEPS + q + 1))

                    e2 = j + 2 if isinstance(it, int) else dve.value_load(etab[0:1, bass.ds(it * 2 + (j + 2), 1)], min_val=0, max_val=NE - 1)
                    wait(dve, list_ready, it * 2 + (j + 2))
                    chain(v.tensor_scalar(iotab[:, :], iotas[:, :], btab[:, bass.ds(it * 2 + (j + 2), 1)], None, ALU.add), 0)
                    make_onehot(e2)
                    wait(dve, sig_ready, it * 2 + (j + 1))
                    chain(v.tensor_tensor(sig[:, :, :], sig[:, :, :], bank[3][:, 0:NF * SLOTS].rearrange("p (f s) -> p f s", f=NF), ALU.mult), 1)
                    wait(dve, h_ready, it * 2 + j)
                    v.tensor_tensor(h_full[:, :, :], sig[:, :, :], bank[4][:, 0:NF * SLOTS].rearrange("p (f s) -> p f s", f=NF), ALU.mult).then_inc(h_ready_full, 1)
                    wait(dve, h_hi_ready, it * 2 + (j + 1))
                    v.tensor_tensor(h_lo[j][:, :, :], h_full[:, :, :], h_hi[j][:, :, :].bitcast(f32), ALU.subtract).then_inc(h_ready, 1)
                    behind(lambda it, j: take_y(it, j, (0,)), it, j)
                    wait(dve, scattered[j], it * 32)
                    wait(dve, idx_ready, it * 2 + (j + 2))
                    chain(v.tensor_copy(sidx[j][0:CS, :], gidx[j][0:CS, :]), 2)
                    v.tensor_copy(sgate[j][0:CS, :, 0], lst[j][0:CS, :, 1]).then_inc(sidx_ready, 1)
                    wait(dve, list_ready, it * 2 + (j + 3))
                    wait(dve, sidx_ready, it * 2 + (j + 1))
                    wait(dve, gathered[j], it * 32 + 32)
                    make_index(j, lambda ins, q: chain(ins, 3 + q))
                    behind(lambda it, j: take_y(it, j, (1,)), it, j)
                    wait(dve, wd_hi_ready, it * 2 + (j + 1))
                    v.tensor_tensor(wd_lo[:, :, :], W[j][:, 4096:6144].rearrange("p (f d) -> p f d", f=NF),
                                    wd_hi[:, :, :].bitcast(f32), ALU.subtract).then_inc(wd_split, 1)

            pair(0)
            dve.wait_ge(tables_ready, 1)
            pairs = dve.value_load(n_pairs[0:1, 0:1], min_val=NE // 2, max_val=(NE + MAX_OVER) // 2)
            with dve.Fori(1, pairs) as it:
                pair(it)
            last = dve.value_load(n_pairs[0:1, 1:2], min_val=NE // 2 - 1, max_val=(NE + MAX_OVER) // 2 - 1)
            take_y(last, 1)
            def affine(t):
                dve.wait_ge(normal_ready, t + 1)
                if t == 0:
                    dve.wait_ge(g2_loaded, 32)
                v.tensor_tensor(accin[:, t, :], accin[:, t, :], g2b[:, :], ALU.mult).then_inc(out_ready, 1)

            for t in range(NT):
                src = accin[:, t, :]
                dve.wait_ge(acc_loaded[t], 16)
                if t:
                    dve.wait_ge(var_ready, 2 * NT + t)
                for h in range(2):
                    v.bn_stats(stats[:, h, :], src[:, h * HALF:(h + 1) * HALF]).then_inc(last_chain, 1)
                dve.wait_ge(last_chain, 3 * t + 2)
                v.bn_aggr(mean_var[:, t, :], small[:, 64:76]).then_inc(var_ready, 1)
                dve.wait_ge(std_ready, 2 * NT + t + 1)
                v.reciprocal(std[:, t:t + 1], std[:, t:t + 1]).then_inc(last_chain, 1)
                dve.wait_ge(last_chain, 3 * t + 3)
                v.scalar_tensor_tensor(small[:, 128 + t:129 + t], mean_var[:, t, 0:1], -1.0, std[:, t:t + 1], ALU.mult, ALU.mult).then_inc(scale_ready, 1)
                if t > 1:
                    affine(t - 2)
            affine(NT - 2)
            affine(NT - 1)
            dve.wait_ge(out_ready, NT)
            v.tensor_tensor(accin[:, NT - 1, :], accin[:, NT - 1, :], b2b[:, :], ALU.add).then_inc(last_scaled, 1)


_INS = ['x', 'ln0_g', 'ln0_b', 'w_in', 'b_in', 'w_pool', 'pool_scale', 'attn_sinks', 'w_br_pool', 'w_br_attn', 'w_out',
        'ln1_g', 'ln1_b', 'w_router', 'router_bias', 'w_exp_gate', 'w_exp_up', 'w_exp_down', 'w_sh_gate', 'w_sh_up',
        'w_sh_down', 'ln2_g', 'ln2_b']


def kernel(**inputs):
    import numpy as _np
    import concourse.bacc as _bacc
    from concourse import mybir as _mybir
    from concourse.bass_utils import run_bass_kernel_spmd as _run

    nc = _bacc.Bacc("TRN2", target_bir_lowering=False, num_devices=1)
    arrays, args = {}, []
    for name in _INS:
        a = _np.ascontiguousarray(inputs[name])
        arrays[f"in_{name}_dram"] = a
        args.append(nc.dram_tensor(f"in_{name}_dram", a.shape, _mybir.dt.from_np(a.dtype), kind="ExternalInput").ap())
    args.append(nc.dram_tensor("out_dram", (1, 1024, 1024), _mybir.dt.float32, kind="ExternalOutput").ap())
    build(nc, *args)
    r = _run(nc, [arrays], core_ids=[0])
    return r.results[0]["out_dram"]
```

```python
import concourse.bass as bass
from concourse import mybir
from contextlib import ExitStack

T, D, P = 1024, 1024, 128
NT = T // P
ND = D // P
POOL_G = 4
HEADS, HD = 8, 64
QC = HEADS * HD // P
D_IN = 3328
K_COL, V_COL, GP_COL, GA_COL = 1024, 1152, 1280, 2304
NE, FF = 64, 256
NF = FF // P
TOPK = 8
GROUPS, PER_GROUP, KEEP_GROUPS = 8, 8, 4
ROUTED_SCALE = 2.5
ALPHA = 2.0 ** 0.25
EPS = 1e-5
HALF = 512

CHUNKS = ((0, 128), (128, 40))
NC = len(CHUNKS)
SLOTS = sum(size for _, size in CHUNKS)
SHORT = CHUNKS[0][1]
MIDDLE = 148
MAX_OVER = T * TOPK // SLOTS
MAX_OVER += MAX_OVER % 2
FIXED = 4
MAX_PAIRS = (NE + MAX_OVER) // 2 + 3
NTAB = 2 * MAX_PAIRS + 4
FAR = 16384.0
LIST = 6
NEG = -1.0e30


def build(nc, x, ln0_g, ln0_b, w_in, b_in, w_pool, pool_scale, attn_sinks, w_br_pool, w_br_attn,
          w_out, ln1_g, ln1_b, w_router, router_bias, w_exp_gate, w_exp_up, w_exp_down, w_sh_gate,
          w_sh_up, w_sh_down, ln2_g, ln2_b, out):
    f32, f32r, bf16, i32 = mybir.dt.float32, mybir.dt.float32r, mybir.dt.bfloat16, mybir.dt.int32
    ALU, ACT, AX = mybir.AluOpType, mybir.ActivationFunctionType, mybir.AxisListType

    x_t = x[0].rearrange("(t p) d -> t p d", p=P)
    out_t = out[0].rearrange("(t p) d -> t p d", p=P)
    win = w_in[0].rearrange("(p c) e -> p c e", c=ND)
    wg_e = w_exp_gate[0].rearrange("e (p c) f -> e p c f", c=ND)
    wu_e = w_exp_up[0].rearrange("e (p c) f -> e p c f", c=ND)
    wd_e = w_exp_down[0].rearrange("e (c p) d -> e p c d", p=P)
    x1_dram = nc.dram_tensor("x1_rows", (T + SLOTS, D), f32, kind="Internal").ap()
    acc_dram = nc.dram_tensor("acc_rows", (T + SLOTS, D), f32, kind="Internal").ap()

    ctx = ExitStack()
    with ctx:
        base = 16512
        XBUF = 4
        KB = 1024

        def at(name, offset, shape, dt=f32):
            return nc.alloc_sbuf_tensor_at(name, shape, dt, offset=base + offset)

        def sem(name):
            return ctx.enter_context(nc.semaphore(name))

        XT = at("XT", 0, [P, 2, 2, ND, HALF], f32r)
        xin = at("xin", 76 * KB, [P, XBUF, D])
        x_full = at("x_full", 72 * KB, [P, 2, HALF])
        m_full = at("m_full", 76 * KB, [P, 2, HALF])
        S_sb = [at(f"S_sb{j}", (72 + 8 * j) * KB, [P, HEADS, 2 * P]) for j in range(2)]
        PT = at("PT", 88 * KB, [P, 2 * HEADS, P])
        mergedT = at("mergedT", 64 * KB, [P, ND, T])
        uT = at("uT", 96 * KB, [P, POOL_G, T])
        pdiff = at("pdiff", 112 * KB, [P, POOL_G, T])
        mixT = at("mixT", 96 * KB, [P, 2, POOL_G, T], f32r)
        xhat = at("xhat", 128 * KB, [P, 4, D])
        qT = at("qT", 128 * KB, [P, QC, T])
        oT = at("oT", 128 * KB, [P, 2, QC, T], f32r)
        ladder = at("ladder", 144 * KB, [P, 2, T])
        vT = at("vT", 152 * KB, [P, T])
        wpool = at("wpool", 156 * KB, [P, POOL_G, P])
        rows = at("rows", 158 * KB, [P, P])
        inv = at("inv", 158 * KB + 512, [P, POOL_G, 16])
        kT = at("kT", 160 * KB, [P, 2, T])
        v_sb = at("v_sb", 168 * KB, [P, NT, P])
        gate_sb = at("gate_sb", 160 * KB, [P, 4, HALF])
        RING = 4
        u_raw = [at(f"u_raw{r}", (172 + 8 * r) * KB, [P, D]) for r in range(RING)]
        u_lo = [at(f"u_lo{r}", (172 + 8 * r) * KB, [P, D], f32r) for r in range(RING)]
        u_hi = [at(f"u_hi{r}", (176 + 8 * r) * KB, [P, D], f32r) for r in range(RING)]
        o_raw = [at(f"o_raw{r}", (96 + 8 * r) * KB, [P, D]) for r in range(4)]
        o_lo = [at(f"o_lo{r}", (96 + 8 * r) * KB, [P, D], f32r) for r in range(4)]
        o_hi = [at(f"o_hi{r}", (100 + 8 * r) * KB, [P, D], f32r) for r in range(4)]
        xh = at("xh", 128 * KB, [P, NT, D])
        g1b = at("g1b", 160 * KB, [P, D])
        b1b = at("b1b", 164 * KB, [P, D])
        c0 = 204 * KB
        ident = at("ident", c0, [P, P])
        dist = at("dist", c0 + 512, [P, 2 * P])
        cols = at("cols", c0 + 1536, [P, 64])
        small = at("small", c0 + 1792, [P, 160])
        mean_var = at("mean_var", c0 + 2432, [P, NT, 2])
        std = at("std", c0 + 2496, [P, NT])
        mean_var0 = at("mean_var0", c0 + 2528, [P, NT, 2])
        std0 = at("std0", c0 + 2592, [P, NT])
        eps = at("eps", c0 + 2624, [P, 1])

        W = [at(f"W{j}", 24 * j * KB, [P, 3 * 2048]) for j in range(2)]
        hsh = at("hsh", 64 * KB, [P, 2, NF, T], f32r)
        sig_sh = at("sig_sh", 80 * KB, [P, HALF])
        h_sh = at("h_sh", 82 * KB, [P, HALF])
        r0 = 86 * KB
        scores = at("scores", r0, [P, NT, NE])
        biased = at("biased", r0 + 2048, [P, NT, NE])
        work = at("work", r0 + 4096, [P, NT, NE])
        top = at("top", r0 + 6144, [P, NT, GROUPS, 8])
        mask = at("mask", r0 + 8192, [P, NT, NE])
        scoresT = at("scoresT", r0 + 4096, [P, T])
        maskb = at("maskb", r0 + 10240, [P, NT, NE], bf16)
        gates = at("gates", r0 + 11264, [P, NT, NE])
        gs = at("gs", r0 + 13312, [P, NT, GROUPS])
        gtop = at("gtop", r0 + 13568, [P, NT, 8])
        etop = at("etop", r0 + 13824, [P, NT, 8])
        gsum = at("gsum", r0 + 14080, [P, NT])
        rbias = at("rbias", r0 + 17 * KB, [P, NE])
        (T_IS_LONG, T_OVER, T_LONG_SUM, T_SHORT_SUM, T_OVER_SUM, T_PLACE, T_TMP, T_ONE,
         T_IS_MIDDLE, T_MIDDLE_SUM) = range(10)
        trow = at("trow", 160 * KB, [P, 10, NE])
        diag = at("diag", 163 * KB, [P, 2, P], bf16)
        l0 = 105 * KB
        posm = at("posm", l0, [P, NE, NT])
        vlist = at("vlist", l0 + 2 * KB, [P, NE, NT, LIST], bf16)
        iotas = at("iotas", l0 + 8 * KB, [P, SLOTS])
        tri = at("tri", l0 + 9 * KB, [P, P], bf16)
        ones = at("ones", l0 + 9 * KB + 256, [P, P], bf16)
        etab = at("etab", l0 + 10 * KB, [P, NTAB], i32)
        expert = at("expert", l0 + 10 * KB + 512, [P, NE])
        btab = at("btab", l0 + 11 * KB, [P, NTAB])
        n_pairs = at("n_pairs", l0 + 11 * KB + 512, [P, 4], i32)
        trash = at("trash", l0 + 11 * KB + 544, [P, 2, NC])
        counts = at("counts", l0 + 12 * KB, [P, NE])
        C_EXP, C_PREV, C_O, C_IN, C_A, C_B, C_BASE, C_TOTAL, C_LONG, C_MIDDLE = range(10)
        tcol = at("tcol", l0 + 13 * KB, [P, 10])
        block_no = at("block_no", l0 + 13 * KB + 128, [P, 1])
        iotab = at("iotab", l0 + 14 * KB, [P, SLOTS])
        gidx = [at(f"gidx{j}", l0 + 15 * KB + 64 * j, [P, NC], i32) for j in range(2)]
        sidx = [at(f"sidx{j}", l0 + 15 * KB + 128 + 64 * j, [P, NC], i32) for j in range(2)]
        lst = [at(f"lst{j}", l0 + 15 * KB + 256 + 64 * j, [P, NC, 2]) for j in range(2)]
        sgate = [at(f"sgate{j}", l0 + 15 * KB + 384 + 64 * j, [P, NC, 1]) for j in range(2)]
        tmp = at("tmp", l0 + 15 * KB + 512, [P, NC, 1])
        wr = at("wr", 121 * KB, [P, ND, NE])
        wr_hi = at("wr_hi", 123 * KB, [P, ND, NE], f32r)
        wr_lo = at("wr_lo", 125 * KB, [P, ND, NE], f32r)
        zrow = at("zrow", 168 * KB, [P, D])
        onehot = at("onehot", 83 * KB, [P, NT, SLOTS], bf16)
        xg = [at(f"xg{j}", r0 + 8 * j * KB, [P, NC, D]) for j in range(2)]
        xgT = [at(f"xgT{j}", (122, 144)[j] * KB, [P, ND, SLOTS]) for j in range(2)]
        ysb = [at(f"ysb{j}", (128 + 8 * j) * KB, [P, NC, D]) for j in range(2)]
        wd_hi = at("wd_hi", 48 * KB, [P, NF, D], f32r)
        wd_lo = at("wd_lo", 56 * KB, [P, NF, D], f32r)
        sig = at("sig", 172 * KB, [P, NF, SLOTS])
        h_full = at("h_full", 174 * KB, [P, NF, SLOTS])
        h_hi = [at(f"h_hi{j}", (176 + 4 * j) * KB, [P, NF, SLOTS], f32r) for j in range(2)]
        h_lo = [at(f"h_lo{j}", (178 + 4 * j) * KB, [P, NF, SLOTS], f32r) for j in range(2)]
        g2b = at("g2b", 188 * KB, [P, D])
        b2b = at("b2b", 192 * KB, [P, D])
        accin = at("accin", 0, [P, NT, D])

        bank = [ctx.enter_context(nc.psum_tensor(f"bank{i}", [P, HALF], f32)) for i in range(8)]

        BIN_ROWS = D_IN // P
        C_G0, C_B0 = BIN_ROWS + 1 + POOL_G, BIN_ROWS + 1 + POOL_G + ND
        C_KSW, C_PS = BIN_ROWS, BIN_ROWS + 1
        NROWS = BIN_ROWS + 1 + POOL_G

        consts_loaded = sem("consts_loaded")
        rows_loaded = sem("rows_loaded")
        x_loaded = [sem(f"x_loaded{j}") for j in range(XBUF)]
        ident_ready = sem("ident_ready")
        dve_chain = sem("dve_chain")
        pool_chain = sem("pool_chain")
        rows_T = sem("rows_T")
        cols_ready = sem("cols_ready")
        xhat_ready = sem("xhat_ready")
        tr_ready = sem("tr_ready")
        tr_taken = sem("tr_taken")
        unit_loaded = [sem(f"unit_loaded{r}") for r in range(RING)]
        wo_loaded = [sem(f"wo_loaded{r}") for r in range(4)]
        unit_hi = sem("unit_hi")
        unit_split = sem("unit_split")
        wo_done = sem("wo_done")
        x0_full = sem("x0_full")
        x0_hi = sem("x0_hi")
        v_ready = sem("v_ready")
        v_taken = sem("v_taken")
        m_full_ready = sem("m_full_ready")
        m_hi_ready = sem("m_hi_ready")
        rden_ready = sem("rden_ready")
        scaled = sem("scaled")
        sink_exp = sem("sink_exp")
        pv_ready = sem("pv_ready")
        o_hi_ready = sem("o_hi_ready")
        o_taken = sem("o_taken")
        piece_hi = sem("piece_hi")
        piece_split = sem("piece_split")
        xr_loaded = [sem(f"xr_loaded{t}") for t in range(NT)]
        x0hat_ready = sem("x0hat_ready")
        x1_hi = sem("x1_hi")
        wr_ready = sem("wr_ready")
        sh_full = sem("sh_full")
        sh_hi = sem("sh_hi")
        proj_ready = sem("proj_ready")
        proj_taken = sem("proj_taken")
        pdiff_ready = sem("pdiff_ready")
        ladder_ready = sem("ladder_ready")
        mixed_ready = sem("mixed_ready")
        mixed_taken = sem("mixed_taken")
        x0_ready = sem("x0_ready")
        sc_ready = sem("sc_ready")
        sc_taken = sem("sc_taken")
        negm_ready = sem("negm_ready")
        exp_done = sem("exp_done")
        pt_ready = sem("pt_ready")
        pt_taken = sem("pt_taken")
        mg_ready = sem("mg_ready")
        sg_ready = sem("sg_ready")
        merged_ready = sem("merged_ready")
        mix_ready = sem("mix_ready")
        mix_taken = sem("mix_taken")
        ln1_ready = sem("ln1_ready")
        x1_ready = sem("x1_ready")
        x1T_ready = sem("x1T_ready")
        x1T_taken = sem("x1T_taken")
        x1_stored = sem("x1_stored")
        r_loaded = sem("r_loaded")
        g1_loaded = sem("g1_loaded")
        wr_loaded = sem("wr_loaded")
        logits_ready = sem("logits_ready")
        score_ready = sem("score_ready")
        scoresT_ready = sem("scoresT_ready")
        scores_tr = sem("scores_tr")
        mask_ready = sem("mask_ready")
        pos_ready = sem("pos_ready")
        pool_consts = sem("pool_consts")
        sh_ready = sem("sh_ready")
        sh_sig = sem("sh_sig")
        sh_h = sem("sh_h")
        shd_ready = sem("shd_ready")
        shd_taken = sem("shd_taken")
        acc_stored = sem("acc_stored")
        tables_ready = sem("tables_ready")
        diag_ready = sem("diag_ready")
        rows_of_table = sem("rows_of_table")
        gu_loaded = [sem(f"gu_loaded{j}") for j in range(2)]
        wd_loaded = [sem(f"wd_loaded{j}") for j in range(2)]
        onehot_ready = sem("onehot_ready")
        list_ready = sem("list_ready")
        idx_ready = sem("idx_ready")
        gathered = [sem(f"gathered{j}") for j in range(2)]
        gathered_rest = [sem(f"gathered_rest{j}") for j in range(2)]
        xgT_ready = sem("xgT_ready")
        xgT_taken = sem("xgT_taken")
        gu_ready = sem("gu_ready")
        sig_ready = sem("sig_ready")
        h_ready = sem("h_ready")
        h_ready_full = sem("h_ready_full")
        h_hi_ready = sem("h_hi_ready")
        wd_hi_ready = sem("wd_hi_ready")
        wd_split = sem("wd_split")
        y_ready = sem("y_ready")
        y_taken_dve = sem("y_taken_dve")
        y_taken_act = sem("y_taken_act")
        sidx_ready = sem("sidx_ready")
        scattered = [sem(f"scattered{j}") for j in range(2)]
        scattered_rest = [sem(f"scattered_rest{j}") for j in range(2)]
        pool_turn = sem("pool_turn")
        acc_loaded = [sem(f"acc_loaded{t}") for t in range(NT)]
        g2_loaded = sem("g2_loaded")
        out_ready = sem("out_ready")
        out_scaled = sem("out_scaled")
        last_scaled = sem("last_scaled")
        scale_ready = sem("scale_ready")
        normal_ready = sem("normal_ready")
        out_stored = sem("out_stored")
        last_chain = sem("last_chain")
        var_ready = sem("var_ready")
        std_ready = sem("std_ready")

        def score_place(h, w):
            o = (h // 2 % 2) * 2 * P
            return bank[2 * (h % 2) + h // 4][:, o:o + w]

        def wait(engine, semaphore, value):
            if not isinstance(value, int) or value > 0:
                engine.wait_ge(semaphore, value)

        def behind(step, it, j, slots, slots_before):
            if j:
                step(it, 0, slots, slots_before)
            elif not isinstance(it, int) or it > 0:
                step(it - 1, 1, slots_before, slots_before)

        win_k = [("u", g, g * P) for g in range(POOL_G)] + [("q", c, 512 + c * P) for c in range(QC)] + \
                [("k", 0, K_COL), ("k", 1, None), ("v", 0, V_COL)]
        NPROJ = len(win_k)
        U_MERGE, U_OUT, U_SH = NPROJ, NPROJ + 3 * ND, NPROJ + 3 * ND + ND
        MERGE_INCS = 8

        def unit(n):
            if U_OUT + 4 <= n < U_SH:
                r = n - U_OUT - 4
                return o_raw[r], o_hi[r], o_lo[r]
            return u_raw[n % RING], u_hi[n % RING], u_lo[n % RING]

        def wait_unit_loaded(engine, n):
            if U_OUT + 4 <= n < U_SH:
                engine.wait_ge(wo_loaded[n - U_OUT - 4], 16)
            else:
                r = n % RING
                earlier = [m for m in range(n + 1) if m % RING == r and not U_OUT + 4 <= m < U_SH]
                engine.wait_ge(unit_loaded[r], sum(16 * pieces(m) for m in earlier))

        def pieces(n):
            if n < U_MERGE:
                return 2 if win_k[n][2] is None else 1
            if n < U_OUT:
                return 2 if (n - U_MERGE) % 3 == 2 else 1
            return 1

        def wait_unit_used(engine, n):
            if n < U_MERGE:
                engine.wait_ge(proj_ready, 2 * (n + 1))
            elif n < U_OUT:
                c, q = divmod(n - U_MERGE, 3)
                engine.wait_ge(mg_ready, MERGE_INCS * c + (2, 4, 8)[q])
            elif n < U_SH:
                engine.wait_ge(wo_done, n - U_OUT + 1)
            else:
                engine.wait_ge(sh_ready, 3)

        SPLIT = ((0, 0), (0, 1), (1, 0))

        block = ctx.enter_context(nc.Block())

        @block.sync
        def _(sp):
            def load_unit(n):
                raw = unit(n)[0]
                rc = raw[:, :].rearrange("p (c e) -> p c e", c=ND)
                if U_OUT + 4 <= n < U_SH:
                    signal = wo_loaded[n - U_OUT - 4]
                    wait_unit_used(sp, U_OUT - 1)
                else:
                    signal = unit_loaded[n % RING]
                    before = [m for m in range(n) if m % RING == n % RING and not U_OUT + 4 <= m < U_SH]
                    if before:
                        wait_unit_used(sp, before[-1])
                if n < U_MERGE:
                    col = win_k[n][2]
                    if col is None:
                        sp.dma_start(rc[:, :, 0:HD], win[:, :, K_COL + HD:K_COL + P]).then_inc(signal, 16)
                        sp.dma_start(rc[:, :, HD:P], win[:, :, K_COL:K_COL + HD]).then_inc(signal, 16)
                    else:
                        sp.dma_start(rc, win[:, :, col:col + P]).then_inc(signal, 16)
                elif n < U_OUT:
                    c, q = divmod(n - U_MERGE, 3)
                    if q < 2:
                        col = (GP_COL, GA_COL)[q] + c * P
                        sp.dma_start(rc, win[:, :, col:col + P]).then_inc(signal, 16)
                    else:
                        for h, w in ((0, w_br_pool), (1, w_br_attn)):
                            sp.dma_start(rc[:, 4 * h:4 * h + 4, :],
                                         w[0].rearrange("(k p) d -> p k d", p=P)[:, :, c * P:(c + 1) * P]).then_inc(signal, 16)
                elif n < U_SH:
                    k = n - U_OUT
                    sp.dma_start(raw[:, :], w_out[0, k * P:(k + 1) * P, :]).then_inc(signal, 16)
                elif n < U_SH + 4:
                    f, q = divmod(n - U_SH, 2)
                    w = (w_sh_gate, w_sh_up)[q][0].rearrange("(p c) f -> p c f", c=ND)
                    sp.dma_start(rc, w[:, :, f * P:(f + 1) * P]).then_inc(signal, 16)
                else:
                    f = n - U_SH - 4
                    sp.dma_start(raw[:, :], w_sh_down[0, f * P:(f + 1) * P, :]).then_inc(signal, 16)

            for t in range(NT):
                if t >= XBUF:
                    sp.wait_ge(xhat_ready, t - XBUF + 1)
                sp.dma_start(xin[:, t % XBUF, :], x_t[t]).then_inc(x_loaded[t % XBUF], 16)
                if t == 0:
                    sp.dma_start(rows[0:BIN_ROWS, :], b_in[0].rearrange("(r n) -> r n", n=P)).then_inc(rows_loaded, 16)
                    sp.dma_start(rows[C_KSW:C_KSW + 1, 0:HD], b_in[0:1, K_COL + HD:K_COL + P]).then_inc(rows_loaded, 16)
                    sp.dma_start(rows[C_KSW:C_KSW + 1, HD:P], b_in[0:1, K_COL:K_COL + HD]).then_inc(rows_loaded, 16)
                    sp.dma_start(rows[C_PS:C_PS + POOL_G, :], pool_scale[0].rearrange("(r n) -> r n", n=P)).then_inc(rows_loaded, 16)
                    sp.dma_start(cols[:, C_G0:C_G0 + ND], ln0_g.rearrange("(p c) -> p c", c=ND)).then_inc(rows_loaded, 16)
                    sp.dma_start(cols[:, C_B0:C_B0 + ND], ln0_b.rearrange("(p c) -> p c", c=ND)).then_inc(rows_loaded, 16)
                if t == 3:
                    load_unit(0)
                if t == 5:
                    load_unit(1)
                if t == NT - 1:
                    sp.dma_start(small[:, 0:HEADS], attn_sinks[0:1, :].to_broadcast([P, HEADS])).then_inc(consts_loaded, 16)
                    sp.dma_start(wpool[:, :, :], w_pool[0].rearrange("g c d -> c g d")).then_inc(consts_loaded, 16)
            for n in range(2, U_OUT + 4):
                load_unit(n)
            sp.wait_ge(mg_ready, MERGE_INCS * ND)
            for t in range(NT):
                sp.dma_start(xh[:, t, :], x_t[t]).then_inc(xr_loaded[t], 16)
                if t < 4:
                    load_unit(U_OUT + 4 + t)
                if t == 0:
                    sp.wait_ge(merged_ready, 2 * ND)
                    sp.dma_start(g1b[:, :], ln0_g.rearrange("(a n) -> a n", a=1).to_broadcast([P, D])).then_inc(r_loaded, 16)
                    sp.dma_start(b1b[:, :], ln0_b.rearrange("(a n) -> a n", a=1).to_broadcast([P, D])).then_inc(r_loaded, 16)
            sp.wait_ge(x0_ready, NT)
            sp.dma_start(g1b[:, :], ln1_g[0:1, :].to_broadcast([P, D])).then_inc(g1_loaded, 16)
            sp.dma_start(b1b[:, :], ln1_b[0:1, :].to_broadcast([P, D])).then_inc(g1_loaded, 16)
            for n in range(U_SH, U_SH + 4):
                load_unit(n)
            sp.wait_ge(mix_ready, 2 * NT)
            sp.dma_start(wr[:, :, :], w_router[0].rearrange("(p c) e -> p c e", c=ND)).then_inc(wr_loaded, 16)
            sp.dma_start(rbias[:, :], router_bias[0:1, :].to_broadcast([P, NE])).then_inc(wr_loaded, 16)
            for t in range(NT):
                sp.wait_ge(x1_ready, t + 1)
                sp.dma_start(x1_dram[t * P:(t + 1) * P, :], xh[:, t, :]).then_inc(x1_stored, 16)
            sp.wait_ge(pool_consts, 11)
            for d in (x1_dram, acc_dram):
                sp.dma_start(d[T:T + P, :], zrow[:, :]).then_inc(x1_stored, 16)
                sp.dma_start(d[T + P:T + SLOTS, :], zrow[0:SLOTS - P, :]).then_inc(x1_stored, 16)
            for n in range(U_SH + 4, U_SH + 6):
                load_unit(n)
            sp.wait_ge(sh_ready, 4)
            for j in range(2):
                w = W[j]
                sp.dma_start(w[:, 0:2048].rearrange("p (c f) -> p c f", c=ND), wg_e[j]).then_inc(gu_loaded[j], 16)
                sp.dma_start(w[:, 2048:4096].rearrange("p (c f) -> p c f", c=ND), wu_e[j]).then_inc(gu_loaded[j], 16)
                sp.dma_start(w[:, 4096:6144].rearrange("p (c d) -> p c d", c=NF), wd_e[j]).then_inc(wd_loaded[j], 16)
            for t in range(NT):
                sp.wait_ge(shd_taken, 2 * t + 2)
                sp.dma_start(acc_dram[t * P:(t + 1) * P, :], xh[:, t, :]).then_inc(acc_stored, 16)
            sp.dma_start(g2b[:, :], ln2_g[0:1, :].to_broadcast([P, D])).then_inc(g2_loaded, 16)
            sp.dma_start(b2b[:, :], ln2_b[0:1, :].to_broadcast([P, D])).then_inc(g2_loaded, 16)
            sp.wait_ge(tables_ready, 1)
            pairs = sp.value_load(n_pairs[0:1, 1:2], min_val=5, max_val=MAX_PAIRS)
            more_than_short = sp.value_load(n_pairs[0:1, 0:1], min_val=2, max_val=MAX_PAIRS - 3)
            with sp.Fori(0, pairs - 1) as it:
                for j in range(2):
                    e = sp.value_load(etab[0:1, bass.ds(it * 2 + (j + 2), 1)], min_val=0, max_val=NE - 1)
                    w = W[j]
                    sp.wait_ge(gu_ready, it * 2 + (j + 1))
                    sp.dma_start(w[:, 0:2048].rearrange("p (o c f) -> p o c f", o=1, c=ND),
                                 wg_e[bass.ds(e, 1)].rearrange("e p c f -> p e c f")).then_inc(gu_loaded[j], 16)
                    sp.dma_start(w[:, 2048:4096].rearrange("p (o c f) -> p o c f", o=1, c=ND),
                                 wu_e[bass.ds(e, 1)].rearrange("e p c f -> p e c f")).then_inc(gu_loaded[j], 16)
                    sp.wait_ge(wd_split, it * 2 + (j + 1))
                    sp.dma_start(w[:, 4096:6144].rearrange("p (o c d) -> p o c d", o=1, c=NF),
                                 wd_e[bass.ds(e, 1)].rearrange("e p c d -> p e c d")).then_inc(wd_loaded[j], 16)
            for j in range(2):
                sp.wait_ge(scattered[j], pairs * 16)
            for j in range(2):
                sp.wait_ge(scattered_rest[j], more_than_short * 16 + 16)
            for t in range(NT):
                sp.dma_start(accin[:, t, :], acc_dram[t * P:(t + 1) * P, :]).then_inc(acc_loaded[t], 16)
            for t in range(NT):
                if t < NT - 1:
                    sp.wait_ge(out_scaled, t + 1)
                else:
                    sp.wait_ge(last_scaled, 1)
                sp.dma_start(out_t[t], accin[:, t, :]).then_inc(out_stored, 16)
            sp.wait_ge(out_stored, 16 * NT)

        @block.gpsimd
        def _(pool):
            gp = nc.gpsimd
            n = [0]

            def link(ins):
                n[0] += 1
                ins.then_inc(pool_chain, 1)
                pool.wait_ge(pool_chain, n[0])

            link(gp.memset(eps[:, :], EPS))
            link(gp.memset(ident[:, :], 0.0))
            gp.affine_select(out=ident[:, :], in_=ident[:, :], compare_op=ALU.not_equal, fill=1.0, base=0,
                             pattern=[[-1, P]], channel_multiplier=1).then_inc(ident_ready, 1)
            link(gp.iota(dist[:, :], [[-1, 2 * P]], base=P, channel_multiplier=1, allow_small_or_imprecise_dtypes=True))
            link(gp.affine_select(out=dist[:, :], in_=dist[:, :], compare_op=ALU.is_ge, fill=1.0e32, base=P,
                                  pattern=[[-1, 2 * P]], channel_multiplier=1))
            link(gp.affine_select(out=dist[:, :], in_=dist[:, :], compare_op=ALU.is_ge, fill=1.0e32, base=-1,
                                  pattern=[[1, 2 * P]], channel_multiplier=-1))
            gp.iota(inv[:, :, :], [[0, POOL_G], [1, 16]], base=1, channel_multiplier=0,
                    allow_small_or_imprecise_dtypes=True).then_inc(ident_ready, 1)
            for g in range(POOL_G):
                pool.wait_ge(proj_taken, 2 * (g + 1))
                if g >= 1:
                    pool.wait_ge(pdiff_ready, g)
                src = uT[:, g, :]
                for s in range(g + 1):
                    k = 1 << s
                    dst = ladder[:, s % 2, :]
                    link(gp.tensor_copy(dst[:, 0:k], src[:, 0:k]))
                    add = gp.tensor_tensor(dst[:, k:T], src[:, k:T], src[:, 0:T - k], ALU.add)
                    if s < g:
                        link(add)
                    else:
                        add.then_inc(ladder_ready, 1)
                    src = dst
            pool.wait_ge(r_loaded, 32)
            for t in range(NT):
                pool.wait_ge(x0hat_ready, t + 1)
                link(gp.tensor_tensor(xh[:, t, :], xh[:, t, :], g1b[:, :], ALU.mult))
                gp.tensor_tensor(xh[:, t, :], xh[:, t, :], b1b[:, :], ALU.add).then_inc(x0_ready, 1)
            pool.wait_ge(g1_loaded, 32)
            for t in range(NT):
                pool.wait_ge(ln1_ready, t + 1)
                link(gp.tensor_tensor(xh[:, t, :], xh[:, t, :], g1b[:, :], ALU.mult))
                gp.tensor_tensor(xh[:, t, :], xh[:, t, :], b1b[:, :], ALU.add).then_inc(x1_ready, 1)
                if t == NT - 1:
                    pool.wait_ge(mix_ready, 2 * NT)
                    gp.memset(zrow[:, :], 0.0).then_inc(pool_consts, 1)
                    gp.iota(iotas[:, :], [[1, SLOTS]], base=0, channel_multiplier=0, allow_small_or_imprecise_dtypes=True).then_inc(pool_consts, 1)
                    link(gp.memset(tri[:, :], 1.0))
                    gp.affine_select(out=tri[:, :], in_=tri[:, :], compare_op=ALU.is_gt, fill=0.0, base=0,
                                     pattern=[[1, P]], channel_multiplier=-1).then_inc(pool_consts, 1)
                    gp.memset(ones[:, :], 1.0).then_inc(pool_consts, 1)
                    gp.iota(trash[:, 0, :], [[SHORT, NC]], base=T, channel_multiplier=1, allow_small_or_imprecise_dtypes=True).then_inc(pool_consts, 1)
                    gp.iota(trash[:, 1, :], [[-SHORT, NC]], base=-T, channel_multiplier=-1, allow_small_or_imprecise_dtypes=True).then_inc(pool_consts, 1)
                    gp.iota(vlist[:, :, :, 0], [[0, NE], [P, NT]], base=0, channel_multiplier=0, allow_small_or_imprecise_dtypes=True).then_inc(pool_consts, 1)
                    gp.iota(vlist[:, :, :, 1], [[0, NE], [0, NT]], base=0, channel_multiplier=1, allow_small_or_imprecise_dtypes=True).then_inc(pool_consts, 1)
                    gp.memset(vlist[:, :, :, 2], 1.0).then_inc(pool_consts, 1)
                    gp.iota(block_no[:, :], [[0, 1]], base=0, channel_multiplier=1, allow_small_or_imprecise_dtypes=True).then_inc(pool_consts, 1)
                    gp.iota(expert[:, :], [[1, NE]], base=0, channel_multiplier=0, allow_small_or_imprecise_dtypes=True).then_inc(pool_consts, 1)
            pool.wait_ge(x1_stored, 16 * (NT + 4))

            def gather(j, slots):
                for c, (_, size) in enumerate(CHUNKS if slots > SHORT else CHUNKS[:1]):
                    gp.indirect_dma_start(out=xg[j][0:size, c, :], out_offset=None, in_=x1_dram[:, :],
                                          in_offset=bass.IndirectOffsetOnAxis(ap=gidx[j][0:size, c:c + 1], axis=0)
                                          ).then_inc((gathered, gathered_rest)[c][j], 16)

            for j in range(2):
                pool.wait_ge(idx_ready, j + 1)
                gather(j, SLOTS)
            pool.wait_ge(acc_stored, 16 * NT)
            def scatter(it, j, slots, slots_before):
                wait(pool, y_taken_dve, it * 4 + 2 * (j + 1))
                wait(pool, y_taken_act, it * 4 + 2 * (j + 1))
                wait(pool, scattered[1 - j], it * 16 + 16 * j)
                if (slots if j else slots_before) > SHORT:
                    wait(pool, scattered_rest[1 - j], it * 16 + 16 * j)
                pool.sem_inc(pool_turn, 1)
                for c, (_, size) in enumerate(CHUNKS if slots > SHORT else CHUNKS[:1]):
                    gp.indirect_dma_start(out=acc_dram[:, :],
                                          out_offset=bass.IndirectOffsetOnAxis(ap=sidx[j][0:size, c:c + 1], axis=0),
                                          in_=ysb[j][0:size, c, :], in_offset=None,
                                          compute_op=ALU.add).then_inc((scattered, scattered_rest)[c][j], 16)

            def pair(it, slots, slots_before):
                for j in range(2):
                    wait(pool, xgT_ready, it * 2 + (j + 1))
                    wait(pool, idx_ready, it * 2 + (j + 3))
                    pool.sem_inc(pool_turn, 1)
                    gather(j, slots)
                    behind(scatter, it, j, slots, slots_before)

            pair(0, SLOTS, SLOTS)
            pool.wait_ge(tables_ready, 1)
            long_pairs = pool.value_load(n_pairs[0:1, 3:4], min_val=1, max_val=MAX_PAIRS - 4) + 1
            more_than_short = pool.value_load(n_pairs[0:1, 0:1], min_val=2, max_val=MAX_PAIRS - 3)
            first_short = more_than_short + 1
            pairs = pool.value_load(n_pairs[0:1, 1:2], min_val=5, max_val=MAX_PAIRS)
            with pool.Fori(1, long_pairs) as it:
                pair(it, SLOTS, SLOTS)
            with pool.Fori(long_pairs, first_short) as it:
                pair(it, MIDDLE, SLOTS)
            pair(first_short, SHORT, MIDDLE)
            with pool.Fori(more_than_short + 2, pairs) as it:
                pair(it, SHORT, SHORT)
            last = pool.value_load(n_pairs[0:1, 2:3], min_val=4, max_val=MAX_PAIRS - 1)
            scatter(last, 1, SHORT, SHORT)
            for j in range(2):
                pool.wait_ge(gathered[j], pairs * 16 + 16)
            pool.wait_ge(g2_loaded, 32)
            for t in range(NT - 1):
                pool.wait_ge(out_ready, t + 1)
                gp.tensor_tensor(accin[:, t, :], accin[:, t, :], b2b[:, :], ALU.add).then_inc(out_scaled, 1)

        @block.tensor
        def _(pe):
            mm = nc.tensor.matmul
            pe.wait_ge(ident_ready, 1)
            pe.wait_ge(rows_loaded, 16 * 6)
            nc.tensor.transpose(bank[7][:, 0:NROWS], rows[0:NROWS, :], ident[0:NROWS, 0:NROWS]).then_inc(rows_T, 1)
            for t in range(NT):
                pe.wait_ge(xhat_ready, t + 1)
                for c in range(ND):
                    if t == NT // 2:
                        pe.wait_ge(x0_full, c + 1)
                    if t == 0 and c == ND - 1:
                        pe.wait_ge(cols_ready, 1)
                    last = nc.tensor.transpose(bank[c][:, (t % 4) * P:(t % 4 + 1) * P], xhat[:, t % 4, c::ND], ident[:, :])
                last.then_inc(tr_ready, 1)

            def product(out, n, cols_of, rhs_of, chunks, before=None):
                _, hi, lo = unit(n)
                for i, k in enumerate(chunks):
                    if before:
                        pe.wait_ge(before[0], before[1] + i + 1)
                    for q, (a, b) in enumerate(SPLIT):
                        last = mm(out, (hi, lo)[a][:, cols_of(k)], rhs_of(k, b), start=i + q == 0,
                                  stop=i == len(chunks) - 1 and q == 2)
                return last

            def chunk_cols(k):
                return slice(k * P, (k + 1) * P)

            for n in range(NPROJ):
                pe.wait_ge(unit_split, n + 1)
                for h in range(2):
                    k = 2 * n + h
                    if k >= 4:
                        pe.wait_ge(proj_taken, k - 3)
                    else:
                        pe.wait_ge(x0_full, ND + k + 1)
                    product(bank[k % 4][:, :], n, chunk_cols, lambda c, b: XT[:, h, b, c, :], range(ND),
                            (tr_taken, ND * h) if n == 0 else None).then_inc(proj_ready, 1)
            pe.wait_ge(proj_taken, 2 * NPROJ)
            for h in range(2):
                for c in range(4):
                    last = nc.tensor.transpose(bank[4 + h][:, c * P:(c + 1) * P], vT[:, (4 * h + c) * P:(4 * h + c + 1) * P], ident[:, :])
                last.then_inc(v_ready, 1)
            pe.wait_ge(consts_loaded, 32)
            for g in range(POOL_G):
                pe.wait_ge(pdiff_ready, g + 1)
                for h in range(2):
                    m = 2 * g + h
                    if m >= 2:
                        pe.wait_ge(m_full_ready, m - 1)
                    mm(bank[6 + m % 2][:, :], wpool[:, g, :], pdiff[:, g, h * HALF:(h + 1) * HALF],
                       start=True, stop=True).then_inc(mixed_ready, 1)

            def scores_of(b):
                k0 = (b - 1) * P if b else 0
                w = 2 * P if b else P
                for h in range(HEADS):
                    if b:
                        pe.wait_ge(sc_taken, HEADS * (b - 1) + (h | 2) + 1)
                    lo = HD * (h % 2)
                    kk = 0 if h // (HEADS // 2) == h % 2 else 1
                    mm(score_place(h, w),
                       qT[lo:lo + HD, h // 2, b * P:(b + 1) * P],
                       kT[lo:lo + HD, kk, k0:k0 + w], start=True, stop=True).then_inc(sc_ready, 1)

            scores_of(0)
            scores_of(1)
            pe.wait_ge(v_taken, 2)
            pe.wait_ge(m_full_ready, 2 * POOL_G)
            for b in range(NT):
                kbs = (0, 1) if b else (1,)
                for h2 in range(HEADS // 2):
                    n = 4 * b + h2
                    pe.wait_ge(scaled, HEADS * b + 2 * h2 + 2)
                    if n >= 2:
                        pe.wait_ge(pt_taken, n - 1)
                    for hh in range(2):
                        h = 2 * h2 + hh
                        for kb in kbs:
                            src = S_sb[b % 2][:, h, kb * P:(kb + 1) * P] if b else S_sb[0][:, h, 0:P]
                            last = nc.tensor.transpose(bank[4 + n % 2][:, (2 * hh + kb) * P:(2 * hh + kb + 1) * P], src, ident[:, :])
                    last.then_inc(pt_ready, 1)
                if b + 2 < NT:
                    scores_of(b + 2)
                pe.wait_ge(pt_taken, 4 * b + 4)
                if b >= 2:
                    pe.wait_ge(o_taken, b - 1)
                for g in range(2):
                    for par in range(2):
                        for i, kb in enumerate(kbs):
                            first = 2 * (4 * g + par) + kb
                            last = mm(bank[6 + b % 2][HD * par:HD * (par + 1), 2 * g * P:(2 * g + 2) * P],
                                      v_sb[:, b - 1 + kb, g * HD:(g + 1) * HD], PT[:, first:first + 5:4, :],
                                      start=i == 0, stop=i == len(kbs) - 1)
                last.then_inc(pv_ready, 1)
            for c in range(ND):
                for q in range(3):
                    n = U_MERGE + 3 * c + q
                    pe.wait_ge(unit_split, n + 1)
                    if c == 0:
                        if q == 0:
                            pe.wait_ge(sc_taken, HEADS * NT)
                        if q == 2:
                            pe.wait_ge(o_taken, NT)
                    if q < 2:
                        for h in range(2):
                            if c:
                                pe.wait_ge(sg_ready, 4 * (c - 1) + 2 * q + h + 1)
                            product(bank[2 * q + h][:, :], n, chunk_cols, lambda k, b: XT[:, h, b, k, :], range(ND)).then_inc(mg_ready, 1)
                    else:
                        for i, src in enumerate((mixT, oT)):
                            for h in range(2):
                                if c:
                                    pe.wait_ge(merged_ready, 2 * (c - 1) + h + 1)
                                product(bank[4 + 2 * i + h][:, :], n, lambda k: slice((4 * i + k) * P, (4 * i + k + 1) * P),
                                        lambda k, b: src[:, b, k, h * HALF:(h + 1) * HALF], range(4)).then_inc(mg_ready, 1)
            pe.wait_ge(sg_ready, 4 * ND)
            pe.wait_ge(merged_ready, 2 * ND)
            for half in range(2):
                for k in range(ND):
                    if half == 0:
                        pe.wait_ge(unit_split, U_OUT + k + 1)
                    pe.wait_ge(piece_split, ND * half + k + 1)
                    _, hi, lo = unit(U_OUT + k)
                    for tt in range(4):
                        for n in range(2):
                            if half and k == 0:
                                pe.wait_ge(mix_taken, 2 * tt + n + 1)
                            for q, (a, b) in enumerate(SPLIT):
                                last = mm(bank[2 * tt + n][:, :], XT[:, half, a, k, tt * P:(tt + 1) * P],
                                          (hi, lo)[b][:, n * HALF:(n + 1) * HALF], start=k + q == 0, stop=k == ND - 1 and q == 2)
                            if k == ND - 1:
                                last.then_inc(mix_ready, 1)
                    if half and k < ND - 1:
                        last.then_inc(wo_done, 1)

            def x1_transposes(t):
                pe.wait_ge(x1_ready, t + 1)
                for h in range(2):
                    n = 2 * t + h
                    if n >= 4:
                        pe.wait_ge(x1T_taken, n - 3)
                    for c in range(4):
                        last = nc.tensor.transpose(bank[n % 4][:, c * P:(c + 1) * P], xh[:, t, 4 * h + c::ND], ident[:, :])
                    last.then_inc(x1T_ready, 1)

            def shared_gate_up(m):
                h, f = divmod(m, 2)
                if m == 0:
                    pe.wait_ge(unit_split, U_SH + 2)
                if m == 1:
                    pe.wait_ge(unit_split, U_SH + 4)
                if m >= 2:
                    pe.wait_ge(sh_h, m - 1)
                pe.wait_ge(x1T_taken, 8 * (h + 1))
                for q in range(2):
                    last = product(bank[4 + 2 * (m % 2) + q][:, :], U_SH + 2 * f + q, chunk_cols, lambda k, b: XT[:, h, b, k, :], range(ND))
                last.then_inc(sh_ready, 1)

            pe.wait_ge(mix_taken, 2 * NT)
            for t in range(4):
                x1_transposes(t)
            shared_gate_up(0)
            shared_gate_up(1)
            for t in range(4, NT):
                x1_transposes(t)
            pe.wait_ge(wr_ready, 2)
            pe.wait_ge(x1T_taken, 2 * NT)
            for h in range(2):
                for c in range(ND):
                    for q, (a, b) in enumerate(SPLIT):
                        last = mm(bank[h][0:NE, :], (wr_hi, wr_lo)[a][:, c, :], XT[:, h, b, c, :],
                                  start=c + q == 0, stop=c == ND - 1 and q == 2)
                last.then_inc(logits_ready, 1)
            for t in range(NT):
                if t % 4 == 0:
                    pe.wait_ge(scoresT_ready, t // 4 + 1)
                last = nc.tensor.transpose(bank[3][:, t * NE:(t + 1) * NE], scoresT[0:NE, t * P:(t + 1) * P], ident[0:NE, 0:NE])
            last.then_inc(scores_tr, 1)
            shared_gate_up(2)
            shared_gate_up(3)
            pe.wait_ge(mask_ready, 1)
            pe.wait_ge(pool_consts, 11)
            for t in range(NT):
                for s in range(t + 1):
                    last = mm(bank[1][:, t * NE:(t + 1) * NE], tri[:, :] if s == t else ones[:, :], maskb[:, s, :], start=s == 0, stop=s == t)
            for s in range(NT):
                last = mm(bank[2][:, 0:NE], ones[:, :], maskb[:, s, :], start=s == 0, stop=s == NT - 1)
            last.then_inc(pos_ready, 1)
            def shared_down(n):
                t, h = divmod(n, 2)
                if n >= 4:
                    pe.wait_ge(shd_taken, n - 3)
                for f in range(NF):
                    _, hi, lo = unit(U_SH + 4 + f)
                    for q, (a, b) in enumerate(SPLIT):
                        last = mm(bank[(4, 5, 3, 6)[n % 4]][:, :], hsh[:, a, f, t * P:(t + 1) * P],
                                  (hi, lo)[b][:, h * HALF:(h + 1) * HALF], start=f + q == 0, stop=f == NF - 1 and q == 2)
                last.then_inc(shd_ready, 1)

            pe.wait_ge(sh_h, 4)
            pe.wait_ge(unit_split, U_SH + 6)
            for n in range(4):
                shared_down(n)
            def make_list(e):
                for c, (s0, size) in enumerate(CHUNKS):
                    for t in range(NT):
                        row = vlist[:, e, t, :] if isinstance(e, int) else vlist[:, bass.ds(e, 1), t, :].rearrange("p o l -> p (o l)")
                        last = mm(bank[7][0:size, c * LIST:(c + 1) * LIST], onehot[:, t, s0:s0 + size], row,
                                  start=t == 0, stop=t == NT - 1)
                last.then_inc(list_ready, 1)

            def transposes(j, slots):
                for c in range(ND):
                    for q, (s0, size) in enumerate(CHUNKS if slots > SHORT else CHUNKS[:1]):
                        last = nc.tensor.transpose(bank[c // 3][:, (c % 3) * SLOTS + s0:(c % 3) * SLOTS + s0 + size],
                                                   xg[j][0:size, q, c::ND], ident[0:size, 0:size])
                last.then_inc(xgT_ready, 1)

            def gate_up(j, slots):
                for q in range(2):
                    for f in range(NF):
                        for c in range(ND):
                            last = mm(bank[3 + q][:, f * SLOTS:f * SLOTS + slots],
                                      W[j][:, q * 2048 + c * FF + f * P:q * 2048 + c * FF + (f + 1) * P],
                                      xgT[j][:, c, 0:slots], start=c == 0, stop=c == ND - 1)
                last.then_inc(gu_ready, 1)

            for i in range(2):
                pe.wait_ge(onehot_ready, i + 1)
                if i:
                    pe.wait_ge(idx_ready, i)
                make_list(i)
            for n in range(4, 12):
                shared_down(n)
            pe.wait_ge(gathered[0], 16)
            pe.wait_ge(gathered_rest[0], 16)
            transposes(0, SLOTS)
            for n in range(12, 2 * NT):
                shared_down(n)
            pe.wait_ge(idx_ready, 2)
            pe.wait_ge(diag_ready, 1)
            mm(bank[7][:, 2 * P:4 * P], ones[:, :], diag[:, :, :].rearrange("p a b -> p (a b)"), start=True, stop=True).then_inc(rows_of_table, 1)
            pe.wait_ge(shd_taken, 2 * NT)
            def down(it, j, slots, slots_before):
                wait(pe, h_ready, it * 2 + (j + 1))
                wait(pe, wd_split, it * 2 + (j + 1))
                for c, (s0, size) in enumerate(CHUNKS if slots > SHORT else CHUNKS[:1]):
                    for h in range(2):
                        wait(pe, (y_taken_dve, y_taken_act)[h], it * 4 + 2 * j + c)
                        for f in range(NF):
                            for n, (a, b) in enumerate(((h_hi[j], wd_hi), (h_hi[j], wd_lo), (h_lo[j], wd_hi))):
                                last = mm(bank[5 + h][0:size, :], a[:, f, s0:s0 + size], b[:, f, h * HALF:(h + 1) * HALF],
                                          start=f + n == 0, stop=f == NF - 1 and n == 2)
                        last.then_inc(y_ready, 3 if h and slots == SHORT else 1)

            def pair(it, slots, slots_before):
                for j in range(2):
                    e2 = j + 2 if isinstance(it, int) else pe.value_load(etab[0:1, bass.ds(it * 2 + (j + 2), 1)], min_val=0, max_val=NE - 1)
                    wait(pe, gu_loaded[j], it * 32 + 32)
                    wait(pe, xgT_taken, it * 6 + 3 * (j + 1))
                    wait(pe, h_ready_full, it * 2 + j)
                    gate_up(j, slots)
                    wait(pe, gathered[1 - j], it * 16 + 16 * (1 + j))
                    if slots > SHORT:
                        wait(pe, gathered_rest[1 - j], it * 16 + 16 * (1 + j))
                    transposes(1 - j, slots)
                    wait(pe, onehot_ready, it * 2 + (j + 3))
                    wait(pe, idx_ready, it * 2 + (j + 2))
                    if isinstance(it, int) and j == 0:
                        pe.wait_ge(tables_ready, 1)
                    make_list(e2)
                    behind(down, it, j, slots, slots_before)

            pair(0, SLOTS, SLOTS)
            pe.wait_ge(tables_ready, 1)
            long_pairs = pe.value_load(n_pairs[0:1, 3:4], min_val=1, max_val=MAX_PAIRS - 4) + 1
            more_than_short = pe.value_load(n_pairs[0:1, 0:1], min_val=2, max_val=MAX_PAIRS - 3)
            first_short = more_than_short + 1
            pairs = pe.value_load(n_pairs[0:1, 1:2], min_val=5, max_val=MAX_PAIRS)
            with pe.Fori(1, long_pairs) as it:
                pair(it, SLOTS, SLOTS)
            with pe.Fori(long_pairs, first_short) as it:
                pair(it, MIDDLE, SLOTS)
            pair(first_short, SHORT, MIDDLE)
            with pe.Fori(more_than_short + 2, pairs) as it:
                pair(it, SHORT, SHORT)
            last = pe.value_load(n_pairs[0:1, 2:3], min_val=4, max_val=MAX_PAIRS - 1)
            down(last, 1, SHORT, SHORT)

        @block.scalar
        def _(act):
            A = nc.scalar.activation

            def root(t, round_):
                act.wait_ge(var_ready, round_ * NT + t + 1)
                s, m = (std0, mean_var0) if round_ == 0 else (std, mean_var)
                A(s[:, t:t + 1], m[:, t, 1:2], ACT.Sqrt, bias=eps[:, :]).then_inc(std_ready, 1)

            def unit_high(n):
                wait_unit_loaded(act, n)
                raw, hi, _ = unit(n)
                A(hi[:, :], raw[:, :], ACT.Copy).then_inc(unit_hi, 1)

            act.wait_ge(ident_ready, 1)
            for t in range(4):
                root(t, 0)
            act.wait_ge(cols_ready, 1)
            for n in range(2 * ND):
                half, c = divmod(n, ND)
                if half == 0 and n % 2:
                    root(4 + n // 2, 0)
                act.wait_ge(tr_ready, 4 * (half + 1))
                if n >= 2:
                    act.wait_ge(tr_taken, n - 1)
                A(x_full[:, n % 2, :], bank[c][:, :], ACT.Identity, scale=cols[:, C_G0 + c:C_G0 + c + 1],
                  bias=cols[:, C_B0 + c:C_B0 + c + 1]).then_inc(x0_full, 1)
                act.wait_ge(x0_full, n + 1)
                A(XT[:, half, 0, c, :], x_full[:, n % 2, :], ACT.Copy).then_inc(x0_hi, 1)
                if n in (ND - 1, ND + 3):
                    unit_high(n // ND)
            for n in range(NPROJ):
                if n + 2 < NPROJ + 2:
                    unit_high(n + 2)
                kind, c, col = win_k[n]
                dst = {"u": uT, "q": qT, "k": kT}[kind][:, c, :] if kind != "v" else vT[:, :]
                bcol = C_KSW if col is None else col // P
                for h in range(2):
                    k = 2 * n + h
                    act.wait_ge(proj_ready, k + 1)
                    A(dst[:, h * HALF:(h + 1) * HALF], bank[k % 4][:, :], ACT.Identity,
                      bias=cols[:, bcol:bcol + 1]).then_inc(proj_taken, 1)
            for g in range(POOL_G):
                for h in range(2):
                    m = 2 * g + h
                    act.wait_ge(mixed_ready, m + 1)
                    if m >= 2:
                        act.wait_ge(mixed_taken, m - 1)
                    A(m_full[:, m % 2, :], bank[6 + m % 2][:, :], ACT.Copy, scale=cols[:, C_PS + g:C_PS + g + 1]).then_inc(m_full_ready, 1)
                    act.wait_ge(m_full_ready, m + 1)
                    act.wait_ge(ladder_ready, g + 1)
                    A(mixT[:, 0, g, h * HALF:(h + 1) * HALF], m_full[:, m % 2, :], ACT.Copy).then_inc(m_hi_ready, 1)

            def exps(b):
                w = 2 * P if b else P
                act.wait_ge(negm_ready, b + 1)
                for h in range(HEADS):
                    A(S_sb[b % 2][:, h, 0:w], S_sb[b % 2][:, h, 0:w], ACT.Exp, scale=HD ** -0.5, bias=small[:, 32 + h:33 + h],
                      accum_out=small[:, 40 + h:41 + h]).then_inc(exp_done, 1)
                A(small[:, 56:64], small[:, 48:56], ACT.Exp).then_inc(sink_exp, 1)

            def divide(b):
                w = 2 * P if b else P
                act.wait_ge(rden_ready, b + 1)
                for h in range(HEADS):
                    A(S_sb[b % 2][:, h, 0:w], S_sb[b % 2][:, h, 0:w], ACT.Copy, scale=small[:, 24 + h:25 + h]).then_inc(scaled, 1)

            exps(0)
            divide(0)
            for b in range(NT):
                if b + 1 < NT:
                    exps(b + 1)
                    divide(b + 1)
                act.wait_ge(pv_ready, b + 1)
                A(oT[:, 0, :, b * P:(b + 1) * P], bank[6 + b % 2][:, :].rearrange("p (c q) -> p c q", c=QC), ACT.Copy).then_inc(o_hi_ready, 1)
            for c in range(ND):
                for q in range(3):
                    n = U_MERGE + 3 * c + q
                    unit_high(n + 2)
                    if q < 2:
                        for h in range(2):
                            act.wait_ge(mg_ready, MERGE_INCS * c + 2 * q + h + 1)
                            if c:
                                act.wait_ge(merged_ready, 2 * (c - 1) + h + 1)
                            A(gate_sb[:, 2 * q + h, :], bank[2 * q + h][:, :], ACT.Sigmoid,
                              bias=cols[:, GP_COL // P + q * ND + c:GP_COL // P + q * ND + c + 1]).then_inc(sg_ready, 1)

            def piece_high(half, k):
                A(XT[:, half, 0, k, :], mergedT[:, k, half * HALF:(half + 1) * HALF], ACT.Copy).then_inc(piece_hi, 1)

            act.wait_ge(mg_ready, MERGE_INCS * ND)
            act.wait_ge(merged_ready, 2 * ND)
            for k in range(ND):
                piece_high(0, k)
                if 2 <= U_OUT + k + 2 - U_OUT < ND:
                    unit_high(U_OUT + k + 2)
            for k in range(ND):
                piece_high(1, k)
            for t in range(4):
                root(t, 1)
            unit_high(U_SH)
            unit_high(U_SH + 1)
            for t in range(NT):
                for h in range(2):
                    n = 2 * t + h
                    act.wait_ge(x1T_ready, n + 1)
                    A(XT[:, t // 4, 0, 4 * h:4 * h + 4, (t % 4) * P:(t % 4 + 1) * P],
                      bank[n % 4][:, :].rearrange("p (c q) -> p c q", c=4), ACT.Copy).then_inc(x1_hi, 1)
                if t == 3:
                    unit_high(U_SH + 2)
                    unit_high(U_SH + 3)
                    act.wait_ge(wr_loaded, 32)
                    A(wr_hi[:, :, :], wr[:, :, :], ACT.Copy).then_inc(wr_ready, 1)
                    for i in range(4, NT):
                        root(i, 1)
                    for m in range(2):
                        act.wait_ge(sh_ready, m + 1)
                        if m:
                            act.wait_ge(sh_full, m)
                        A(sig_sh[:, :], bank[4 + 2 * m][:, :], ACT.Sigmoid).then_inc(sh_sig, 1)
                        act.wait_ge(sh_full, m + 1)
                        A(hsh[:, 0, m, 0:HALF], h_sh[:, :], ACT.Copy).then_inc(sh_hi, 1)
            for h in range(2):
                act.wait_ge(logits_ready, h + 1)
                A(scoresT[0:NE, h * HALF:(h + 1) * HALF], bank[h][0:NE, :], ACT.Sigmoid).then_inc(scoresT_ready, 1)
            act.wait_ge(scores_tr, 1)
            A(scores[:, :, :], bank[3][:, :].rearrange("p (t e) -> p t e", t=NT), ACT.Copy).then_inc(score_ready, 1)
            for m in range(2, 4):
                act.wait_ge(sh_ready, m + 1)
                act.wait_ge(sh_full, m)
                A(sig_sh[:, :], bank[4 + 2 * (m % 2)][:, :], ACT.Sigmoid).then_inc(sh_sig, 1)
                act.wait_ge(sh_full, m + 1)
                A(hsh[:, 0, m % 2, HALF:T], h_sh[:, :], ACT.Copy).then_inc(sh_hi, 1)
                if m == 2:
                    unit_high(U_SH + 4)
                    unit_high(U_SH + 5)

            def take_transposes(j, slots):
                for q, n in ((0, 3), (1, 3), (2, 2)):
                    A(xgT[j][:, 3 * q:3 * q + n, 0:slots], bank[q][:, 0:n * SLOTS].rearrange("p (c s) -> p c s", c=n)[:, :, 0:slots],
                      ACT.Copy).then_inc(xgT_taken, 1)

            act.wait_ge(xgT_ready, 1)
            take_transposes(0, SLOTS)
            act.wait_ge(acc_stored, 16 * NT)
            def take_y(it, j, slots, slots_before):
                wait(act, sidx_ready, it * 2 + (j + 1))
                for c, (_, size) in enumerate(CHUNKS if slots > SHORT else CHUNKS[:1]):
                    wait(act, y_ready, it * 8 + 4 * j + 2 * c + 2)
                    A(ysb[j][0:size, c, HALF:D], bank[6][0:size, :], ACT.Copy,
                      scale=sgate[j][0:size, c, :]).then_inc(y_taken_act, 1 if slots > SHORT else 2)

            def pair(it, slots, slots_before):
                for j in range(2):
                    wait(act, gu_ready, it * 2 + (j + 1))
                    wait(act, h_ready_full, it * 2 + j)
                    A(sig[:, :, 0:slots], bank[3][:, 0:NF * SLOTS].rearrange("p (f s) -> p f s", f=NF)[:, :, 0:slots], ACT.Sigmoid).then_inc(sig_ready, 1)
                    wait(act, h_ready_full, it * 2 + (j + 1))
                    A(h_hi[j][:, :, 0:slots], h_full[:, :, 0:slots], ACT.Copy).then_inc(h_hi_ready, 1)
                    wait(act, xgT_ready, it * 2 + (j + 2))
                    take_transposes(1 - j, slots)
                    behind(take_y, it, j, slots, slots_before)
                    wait(act, wd_loaded[j], it * 16 + 16)
                    wait(act, y_ready, it * 8 + 4 * j)
                    A(wd_hi[:, :, :], W[j][:, 4096:6144].rearrange("p (f d) -> p f d", f=NF), ACT.Copy).then_inc(wd_hi_ready, 1)

            pair(0, SLOTS, SLOTS)
            act.wait_ge(tables_ready, 1)
            long_pairs = act.value_load(n_pairs[0:1, 3:4], min_val=1, max_val=MAX_PAIRS - 4) + 1
            more_than_short = act.value_load(n_pairs[0:1, 0:1], min_val=2, max_val=MAX_PAIRS - 3)
            first_short = more_than_short + 1
            pairs = act.value_load(n_pairs[0:1, 1:2], min_val=5, max_val=MAX_PAIRS)
            with act.Fori(1, long_pairs) as it:
                pair(it, SLOTS, SLOTS)
            with act.Fori(long_pairs, first_short) as it:
                pair(it, MIDDLE, SLOTS)
            pair(first_short, SHORT, MIDDLE)
            with act.Fori(more_than_short + 2, pairs) as it:
                pair(it, SHORT, SHORT)
            last = act.value_load(n_pairs[0:1, 2:3], min_val=4, max_val=MAX_PAIRS - 1)
            take_y(last, 1, SHORT, SHORT)
            root(0, 2)
            for t in range(NT):
                if t + 1 < NT:
                    root(t + 1, 2)
                act.wait_ge(scale_ready, t + 1)
                A(accin[:, t, :], accin[:, t, :], ACT.Identity, scale=std[:, t:t + 1], bias=small[:, 128 + t:129 + t]).then_inc(normal_ready, 1)

        @block.vector
        def _(dve):
            v = nc.vector
            n = [0]

            def link(ins):
                n[0] += 1
                ins.then_inc(dve_chain, 1)
                dve.wait_ge(dve_chain, n[0])

            stats = small[:, 64:76].rearrange("p (a b) -> p a b", a=2)

            def statistics(src, t, round_):
                m = (mean_var0, mean_var)[round_]
                if t or round_:
                    dve.wait_ge(var_ready, NT * round_ + t)
                for h in range(2):
                    v.bn_stats(stats[:, h, :], src[:, h * HALF:(h + 1) * HALF]).then_inc(dve_chain, 1)
                n[0] += 2
                dve.wait_ge(dve_chain, n[0])
                v.bn_aggr(m[:, t, :], small[:, 64:76]).then_inc(var_ready, 1)

            def normalise(dst, src, t, round_, signal):
                m, s = ((mean_var0, std0), (mean_var, std))[round_]
                dve.wait_ge(std_ready, round_ * NT + t + 1)
                link(v.reciprocal(s[:, t:t + 1], s[:, t:t + 1]))
                v.tensor_scalar(dst, src, m[:, t, 0:1], s[:, t:t + 1], ALU.subtract, ALU.mult).then_inc(signal, 1)

            def unit_low(k):
                raw, hi, lo = unit(k)
                dve.wait_ge(unit_hi, k + 1)
                v.tensor_tensor(lo[:, :], raw[:, :], hi[:, :].bitcast(f32), ALU.subtract).then_inc(unit_split, 1)

            def x0_low(m):
                half, c = divmod(m, ND)
                dve.wait_ge(x0_hi, m + 1)
                v.tensor_tensor(XT[:, half, 1, c, :], x_full[:, m % 2, :], XT[:, half, 0, c, :].bitcast(f32),
                                ALU.subtract).then_inc(tr_taken, 1)

            for t in range(NT):
                dve.wait_ge(x_loaded[t % XBUF], 16 * (t // XBUF + 1))
                statistics(xin[:, t % XBUF, :], t, 0)
                if t >= 4:
                    x0_low(2 * (t - 4))
                    dve.wait_ge(tr_ready, t - 3)
                normalise(xhat[:, t % 4, :], xin[:, t % XBUF, :], t, 0, xhat_ready)
                if t == 0:
                    dve.wait_ge(rows_T, 1)
                    v.tensor_copy(cols[:, 0:NROWS], bank[7][:, 0:NROWS]).then_inc(cols_ready, 1)
                if t >= 4:
                    x0_low(2 * (t - 4) + 1)
            unit_low(0)
            for m in range(ND, 2 * ND):
                x0_low(m)
                if m == ND + 3:
                    unit_low(1)
            dve.wait_ge(ident_ready, 2)
            for g in range(POOL_G):
                link(v.tensor_scalar(inv[:, g, :], inv[:, g, :], float(2 << g), None, ALU.min))
                link(v.reciprocal(inv[:, g, :], inv[:, g, :]))

            def pool_difference(g):
                dve.wait_ge(ladder_ready, g + 1)
                sm = ladder[:, g % 2, :]
                link(v.tensor_tensor(pdiff[:, g, 0:16], sm[:, 0:16], inv[:, g, :], ALU.mult))
                link(v.tensor_tensor(pdiff[:, g, 0:16], pdiff[:, g, 0:16], uT[:, g, 0:16], ALU.subtract))
                v.scalar_tensor_tensor(pdiff[:, g, 16:T], sm[:, 16:T], 1.0 / (2 << g), uT[:, g, 16:T], ALU.mult,
                                       ALU.subtract).then_inc(pdiff_ready, 1)

            for k in range(NPROJ):
                unit_low(k + 2)
                if k >= 5 and (k - 5) < POOL_G:
                    pool_difference(k - 5)
            for h in range(2):
                dve.wait_ge(v_ready, h + 1)
                v.tensor_copy(v_sb[:, 4 * h:4 * h + 4, :], bank[4 + h][:, :].rearrange("p (t c) -> p t c", t=4)).then_inc(v_taken, 1)
            for m in range(2 * POOL_G):
                g, h = divmod(m, 2)
                dve.wait_ge(m_hi_ready, m + 1)
                dve.wait_ge(mixed_ready, 2 * g + 2)
                v.tensor_tensor(mixT[:, 1, g, h * HALF:(h + 1) * HALF], m_full[:, m % 2, :],
                                mixT[:, 0, g, h * HALF:(h + 1) * HALF].bitcast(f32), ALU.subtract).then_inc(mixed_taken, 1)

            def softmax_statistics(b):
                w = 2 * P if b else P
                S = S_sb[b % 2]
                if b >= 2:
                    dve.wait_ge(pt_ready, 4 * (b - 1))
                for h in range(HEADS):
                    dve.wait_ge(sc_ready, HEADS * b + (h | 2) + 1)
                    slope = 2.0 ** (-8.0 * (h + 1) / HEADS)
                    v.scalar_tensor_tensor(S[:, h, 0:w], dist[:, 2 * P - w:2 * P], -slope * HD ** 0.5,
                                           score_place(h, w), ALU.mult, ALU.add).then_inc(sc_taken, 1)
                dve.wait_ge(sc_taken, HEADS * (b + 1))
                link(v.tensor_reduce(small[:, 8:16], S[:, :, 0:w], axis=AX.X, op=ALU.max))
                link(v.scalar_tensor_tensor(small[:, 16:24], small[:, 8:16], HD ** -0.5, small[:, 0:8], ALU.mult, ALU.max))
                link(v.tensor_tensor(small[:, 48:56], small[:, 0:8], small[:, 16:24], ALU.subtract))
                v.tensor_scalar(small[:, 32:40], small[:, 16:24], -1.0, None, ALU.mult).then_inc(negm_ready, 1)

            def denominators(b):
                dve.wait_ge(sink_exp, b + 1)
                dve.wait_ge(exp_done, HEADS * (b + 1))
                if b:
                    dve.wait_ge(scaled, HEADS * b)
                link(v.tensor_tensor(small[:, 24:32], small[:, 40:48], small[:, 56:64], ALU.add))
                v.reciprocal(small[:, 24:32], small[:, 24:32]).then_inc(rden_ready, 1)

            dve.wait_ge(consts_loaded, 32)
            dve.wait_ge(mixed_taken, 2 * POOL_G)
            softmax_statistics(0)
            denominators(0)
            softmax_statistics(1)
            for b in range(NT):
                for q in range(4):
                    m = 4 * b + q
                    dve.wait_ge(pt_ready, m + 1)
                    if b and q == 0:
                        dve.wait_ge(pv_ready, b)
                    src = bank[4 + m % 2][:, :].rearrange("p (a c) -> p a c", a=4)
                    if b:
                        v.tensor_copy(PT[:, 4 * q:4 * q + 4, :], src).then_inc(pt_taken, 1)
                    else:
                        v.tensor_copy(PT[:, 4 * q + 1:4 * q + 4:2, :], src[:, 1::2, :]).then_inc(pt_taken, 1)
                if b + 1 < NT:
                    denominators(b + 1)
                if b + 2 < NT:
                    softmax_statistics(b + 2)
                dve.wait_ge(o_hi_ready, b + 1)
                v.tensor_tensor(oT[:, 1, :, b * P:(b + 1) * P], bank[6 + b % 2][:, :].rearrange("p (c q) -> p c q", c=QC),
                                oT[:, 0, :, b * P:(b + 1) * P].bitcast(f32), ALU.subtract).then_inc(o_taken, 1)
            for c in range(ND):
                for q in range(3):
                    unit_low(U_MERGE + 3 * c + q + 2)
                for h in range(2):
                    for q in range(2):
                        dve.wait_ge(mg_ready, MERGE_INCS * c + 4 + 2 * q + h + 1)
                        dve.wait_ge(sg_ready, 4 * c + 2 * q + h + 1)
                        v.tensor_tensor(gate_sb[:, 2 * q + h, :], gate_sb[:, 2 * q + h, :], bank[4 + 2 * q + h][:, :], ALU.mult).then_inc(dve_chain, 1)
                    n[0] += 2
                    dve.wait_ge(dve_chain, n[0])
                    v.tensor_tensor(mergedT[:, c, h * HALF:(h + 1) * HALF], gate_sb[:, h, :], gate_sb[:, 2 + h, :], ALU.add).then_inc(merged_ready, 1)

            def piece_low(half, k):
                dve.wait_ge(piece_hi, ND * half + k + 1)
                v.tensor_tensor(XT[:, half, 1, k, :], mergedT[:, k, half * HALF:(half + 1) * HALF],
                                XT[:, half, 0, k, :].bitcast(f32), ALU.subtract).then_inc(piece_split, 1)

            for k in range(ND):
                piece_low(0, k)
                if k + 2 < ND:
                    unit_low(U_OUT + k + 2)
            for t in range(NT):
                dve.wait_ge(xr_loaded[t], 16)
                v.tensor_scalar(xh[:, t, :], xh[:, t, :], mean_var0[:, t, 0:1], std0[:, t:t + 1], ALU.subtract, ALU.mult).then_inc(x0hat_ready, 1)
            for k in range(ND):
                piece_low(1, k)

            def residual(t):
                dve.wait_ge(x0_ready, t + 1)
                for h in range(2):
                    dve.wait_ge(mix_ready, 2 * t + h + 1)
                    v.scalar_tensor_tensor(xh[:, t, h * HALF:(h + 1) * HALF], xh[:, t, h * HALF:(h + 1) * HALF], ALPHA,
                                           bank[2 * (t % 4) + h][:, :], ALU.mult, ALU.add).then_inc(mix_taken, 1)

            def x1_low(t):
                for h in range(2):
                    m = 2 * t + h
                    dve.wait_ge(x1_hi, m + 1)
                    XTt = XT[:, t // 4, :, 4 * h:4 * h + 4, (t % 4) * P:(t % 4 + 1) * P]
                    v.tensor_tensor(XTt[:, 1], bank[m % 4][:, :].rearrange("p (c q) -> p c q", c=4),
                                    XTt[:, 0].bitcast(f32), ALU.subtract).then_inc(x1T_taken, 1)

            def shared_h(m):
                h, f = divmod(m, 2)
                g, u = bank[4 + 2 * (m % 2)], bank[5 + 2 * (m % 2)]
                dve.wait_ge(sh_sig, m + 1)
                link(v.tensor_tensor(sig_sh[:, :], sig_sh[:, :], g[:, :], ALU.mult))
                if m:
                    dve.wait_ge(sh_h, m)
                v.tensor_tensor(h_sh[:, :], sig_sh[:, :], u[:, :], ALU.mult).then_inc(sh_full, 1)
                dve.wait_ge(sh_hi, m + 1)
                v.tensor_tensor(hsh[:, 1, f, h * HALF:(h + 1) * HALF], h_sh[:, :],
                                hsh[:, 0, f, h * HALF:(h + 1) * HALF].bitcast(f32), ALU.subtract).then_inc(sh_h, 1)

            for t in range(4):
                residual(t)
            dve.wait_ge(mix_taken, NT)
            for t in range(4):
                statistics(xh[:, t, :], t, 1)
                normalise(xh[:, t, :], xh[:, t, :], t, 1, ln1_ready)
            unit_low(U_SH)
            unit_low(U_SH + 1)
            for t in range(4, NT):
                residual(t)
            for t in range(4):
                x1_low(t)
            unit_low(U_SH + 2)
            unit_low(U_SH + 3)
            dve.wait_ge(wr_ready, 1)
            v.tensor_tensor(wr_lo[:, :, :], wr[:, :, :], wr_hi[:, :, :].bitcast(f32), ALU.subtract).then_inc(wr_ready, 1)
            dve.wait_ge(mix_taken, 2 * NT)
            for t in range(4, NT):
                statistics(xh[:, t, :], t, 1)
                normalise(xh[:, t, :], xh[:, t, :], t, 1, ln1_ready)
            shared_h(0)
            shared_h(1)
            for t in range(4, NT):
                x1_low(t)
            dve.wait_ge(score_ready, 1)
            dve.wait_ge(wr_loaded, 32)
            link(v.tensor_tensor(biased[:, :, :], scores[:, :, :], rbias[:, :].rearrange("p (o e) -> p o e", o=1).to_broadcast([P, NT, NE]), ALU.add))
            for t in range(NT):
                for g in range(GROUPS):
                    v.max(top[:, t, g, :], biased[:, t, g * PER_GROUP:(g + 1) * PER_GROUP]).then_inc(dve_chain, 1)
            n[0] += NT * GROUPS
            dve.wait_ge(dve_chain, n[0])
            link(v.tensor_tensor(gs[:, :, :], top[:, :, :, 0], top[:, :, :, 1], ALU.add))
            for t in range(NT):
                v.max(gtop[:, t, :], gs[:, t, :]).then_inc(dve_chain, 1)
            n[0] += NT
            dve.wait_ge(dve_chain, n[0])
            link(v.memset(gtop[:, :, KEEP_GROUPS:8], -NEG))
            for t in range(NT):
                v.match_replace(etop[:, t, :], gtop[:, t, :], gs[:, t, :], NEG).then_inc(dve_chain, 1)
            n[0] += NT
            dve.wait_ge(dve_chain, n[0])
            link(v.tensor_tensor(gs[:, :, :], etop[:, :, :], gs[:, :, :], ALU.is_equal))
            link(v.tensor_scalar(gs[:, :, :], gs[:, :, :], NEG, None, ALU.mult))
            link(v.tensor_tensor(work[:, :, :].rearrange("p t (g k) -> p (t g) k", g=GROUPS),
                                 biased[:, :, :].rearrange("p t (g k) -> p (t g) k", g=GROUPS),
                                 gs[:, :, :].rearrange("p t (g o) -> p (t g) o", o=1).to_broadcast([P, NT * GROUPS, PER_GROUP]), ALU.add))
            for t in range(NT):
                v.max(etop[:, t, :], work[:, t, :]).then_inc(dve_chain, 1)
            n[0] += NT
            dve.wait_ge(dve_chain, n[0])
            for t in range(NT):
                v.match_replace(mask[:, t, :], etop[:, t, :], work[:, t, :], 2 * NEG).then_inc(dve_chain, 1)
            n[0] += NT
            dve.wait_ge(dve_chain, n[0])
            link(v.tensor_tensor(mask[:, :, :], mask[:, :, :], work[:, :, :], ALU.not_equal))
            v.tensor_copy(maskb[:, :, :], mask[:, :, :]).then_inc(mask_ready, 1)
            shared_h(2)
            unit_low(U_SH + 4)
            unit_low(U_SH + 5)
            link(v.tensor_tensor(gates[:, :, :], scores[:, :, :], mask[:, :, :], ALU.mult))
            link(v.tensor_reduce(gsum[:, :], gates[:, :, :], axis=AX.X, op=ALU.add))
            link(v.reciprocal(gsum[:, :], gsum[:, :]))
            link(v.tensor_tensor(gates[:, :, :], gates[:, :, :], gsum[:, :].rearrange("p (t o) -> p t o", o=1).to_broadcast([P, NT, NE]), ALU.mult))
            link(v.tensor_scalar(gates[:, :, :], gates[:, :, :], ROUTED_SCALE, None, ALU.mult))
            shared_h(3)
            dve.wait_ge(pool_consts, 11)
            for q in range(3):
                part = vlist[:, :, :, 3 + q].rearrange("p e t -> p t e")
                link(v.tensor_copy(part, gates[:, :, :]))
                if q < 2:
                    link(v.tensor_tensor(gates[:, :, :], gates[:, :, :], part, ALU.subtract))
            dve.wait_ge(pos_ready, 1)
            pt = posm[:, :, :].rearrange("p e t -> p t e")
            link(v.scalar_tensor_tensor(pt, bank[1][:, :].rearrange("p (t e) -> p t e", t=NT), 1.0, mask[:, :, :], ALU.add, ALU.mult))
            link(v.tensor_scalar(pt, pt, -1.0, None, ALU.add))
            link(v.tensor_copy(counts[:, :], bank[2][:, 0:NE]))
            link(v.memset(bank[7][:, 0:NC * LIST], 0.0))
            def make_onehot(e):
                slot, base = (posm[:, e, :], iotas) if isinstance(e, int) else (posm[:, bass.ds(e, 1), :].rearrange("p o t -> p (o t)"), iotab)
                v.tensor_tensor(onehot[:, :, :], slot.rearrange("p (t o) -> p t o", o=1).to_broadcast([P, NT, SLOTS]),
                                base[:, :].rearrange("p (o s) -> p o s", o=1).to_broadcast([P, NT, SLOTS]),
                                ALU.is_equal).then_inc(onehot_ready, 1)

            def make_index(j, chain):
                lp = bank[7][:, 0:NC * LIST].rearrange("p (c l) -> p c l", c=NC)
                lf = lst[j]
                chain(v.tensor_reduce(lf[:, :, 0], lp[:, :, 0:2], axis=AX.X, op=ALU.add), 0)
                chain(v.tensor_reduce(lf[:, :, 1], lp[:, :, 3:6], axis=AX.X, op=ALU.add), 1)
                chain(v.tensor_tensor(tmp[:, :, 0], lp[:, :, 2], trash[:, 1, :], ALU.mult), 2)
                chain(v.tensor_tensor(tmp[:, :, 0], tmp[:, :, 0], trash[:, 0, :], ALU.add), 3)
                v.tensor_tensor(gidx[j][:, :], tmp[:, :, 0], lf[:, :, 0], ALU.add).then_inc(idx_ready, 1)

            for i in range(2):
                if i:
                    dve.wait_ge(list_ready, i)
                make_onehot(i)
                dve.wait_ge(list_ready, i + 1)
                make_index(i, lambda ins, q: link(ins))
            dve.wait_ge(x1_stored, 16 * (NT + 4))
            def accumulator(pieces_):
                for m in pieces_:
                    t, h = divmod(m, 2)
                    dve.wait_ge(shd_ready, m + 1)
                    v.scalar_tensor_tensor(xh[:, t, h * HALF:(h + 1) * HALF], xh[:, t, h * HALF:(h + 1) * HALF], ALPHA,
                                           bank[(4, 5, 3, 6)[m % 4]][:, :], ALU.mult, ALU.add).then_inc(shd_taken, 1)

            accumulator(range(4))
            def row(k):
                return trow[:, k, :]

            def col(k):
                return tcol[:, k:k + 1]

            link(v.tensor_scalar(row(T_IS_LONG), counts[:, :], float(MIDDLE), None, ALU.is_gt))
            link(v.memset(trow[:, T_IS_LONG, 0:FIXED], 1.0))
            link(v.tensor_scalar(row(T_IS_MIDDLE), counts[:, :], float(SHORT), None, ALU.is_gt))
            link(v.tensor_tensor(row(T_IS_MIDDLE), row(T_IS_MIDDLE), row(T_IS_LONG), ALU.is_gt))
            link(v.tensor_scalar(row(T_OVER), counts[:, :], float(SLOTS), None, ALU.is_gt))
            for k in range(2, T // SLOTS + 1):
                link(v.tensor_scalar(row(T_TMP), counts[:, :], float(k * SLOTS), None, ALU.is_gt))
                link(v.tensor_tensor(row(T_OVER), row(T_OVER), row(T_TMP), ALU.add))
            link(v.memset(row(T_ONE), 1.0))
            link(v.tensor_tensor(row(T_TMP), row(T_ONE), row(T_IS_LONG), ALU.subtract))
            link(v.tensor_tensor(row(T_TMP), row(T_TMP), row(T_IS_MIDDLE), ALU.subtract))
            accumulator(range(4, 6))
            for q, k in ((T_LONG_SUM, T_IS_LONG), (T_MIDDLE_SUM, T_IS_MIDDLE), (T_SHORT_SUM, T_TMP), (T_OVER_SUM, T_OVER)):
                link(v.tensor_tensor_scan(row(q), row(T_ONE), row(k), 0.0, ALU.mult, ALU.add))
            n_over, n_long = trow[:, T_OVER_SUM, NE - 1:NE], trow[:, T_LONG_SUM, NE - 1:NE]
            link(v.tensor_tensor(col(C_LONG), n_long, n_over, ALU.add))
            link(v.tensor_scalar(col(C_TOTAL), n_over, float(NE), None, ALU.add))
            link(v.tensor_tensor(col(C_MIDDLE), col(C_LONG), trow[:, T_MIDDLE_SUM, NE - 1:NE], ALU.add))
            link(v.tensor_scalar(row(T_PLACE), row(T_SHORT_SUM), col(C_MIDDLE), None, ALU.add))
            link(v.tensor_scalar(row(T_MIDDLE_SUM), row(T_MIDDLE_SUM), col(C_LONG), None, ALU.add))
            link(v.tensor_tensor(row(T_TMP), row(T_MIDDLE_SUM), row(T_PLACE), ALU.subtract))
            link(v.tensor_tensor(row(T_TMP), row(T_TMP), row(T_IS_MIDDLE), ALU.mult))
            link(v.tensor_tensor(row(T_PLACE), row(T_PLACE), row(T_TMP), ALU.add))
            link(v.tensor_tensor(row(T_TMP), row(T_LONG_SUM), row(T_PLACE), ALU.subtract))
            link(v.tensor_tensor(row(T_TMP), row(T_TMP), row(T_IS_LONG), ALU.mult))
            link(v.tensor_tensor(row(T_PLACE), row(T_PLACE), row(T_TMP), ALU.add))
            link(v.tensor_scalar(row(T_PLACE), row(T_PLACE), -1.0, None, ALU.add))
            accumulator(range(6, 8))
            link(v.tensor_scalar(row(T_TMP), row(T_PLACE), block_no[:, :], None, ALU.is_equal))
            link(v.tensor_tensor(row(T_TMP), row(T_TMP), expert[:, :], ALU.mult))
            link(v.tensor_reduce(col(C_EXP), row(T_TMP), axis=AX.X, op=ALU.add))
            link(v.tensor_tensor(col(C_O), block_no[:, :], n_long, ALU.subtract))
            link(v.tensor_scalar(row(T_TMP), row(T_OVER_SUM), col(C_O), None, ALU.is_le))
            link(v.tensor_reduce(col(C_A), row(T_TMP), axis=AX.X, op=ALU.add))
            link(v.tensor_tensor(row(T_TMP), row(T_TMP), row(T_OVER), ALU.mult))
            link(v.tensor_reduce(col(C_PREV), row(T_TMP), axis=AX.X, op=ALU.add))
            link(v.tensor_scalar(col(C_IN), col(C_O), 0.0, None, ALU.is_ge))
            link(v.tensor_tensor(col(C_B), col(C_O), n_over, ALU.is_lt))
            link(v.tensor_tensor(col(C_IN), col(C_IN), col(C_B), ALU.mult))
            accumulator(range(8, 10))
            link(v.tensor_tensor(col(C_A), col(C_A), col(C_IN), ALU.mult))
            link(v.tensor_tensor(col(C_EXP), col(C_EXP), col(C_A), ALU.add))
            link(v.tensor_tensor(col(C_BASE), col(C_O), col(C_PREV), ALU.subtract))
            link(v.tensor_scalar(col(C_BASE), col(C_BASE), 1.0, float(SLOTS), ALU.add, ALU.mult))
            link(v.tensor_tensor(col(C_BASE), col(C_BASE), col(C_IN), ALU.mult))
            link(v.tensor_tensor(col(C_B), block_no[:, :], col(C_TOTAL), ALU.is_ge))
            link(v.tensor_scalar(col(C_B), col(C_B), FAR, None, ALU.mult))
            link(v.tensor_tensor(col(C_BASE), col(C_BASE), col(C_B), ALU.add))
            link(v.tensor_scalar(diag[:, 0, :], ident[:, :], col(C_EXP), None, ALU.mult))
            v.tensor_scalar(diag[:, 1, :], ident[:, :], col(C_BASE), None, ALU.mult).then_inc(diag_ready, 1)
            accumulator(range(10, 12))
            link(v.tensor_scalar(row(T_TMP), iotas[:, 0:2 * NE:2], col(C_LONG), None, ALU.is_lt))
            link(v.tensor_reduce(col(C_LONG), row(T_TMP), axis=AX.X, op=ALU.add))
            link(v.tensor_scalar(col(C_LONG), col(C_LONG), 2.0, None, ALU.max))
            accumulator(range(12, 13))
            link(v.tensor_scalar(row(T_TMP), iotas[:, 0:2 * NE:2], col(C_MIDDLE), None, ALU.is_lt))
            link(v.tensor_reduce(col(C_MIDDLE), row(T_TMP), axis=AX.X, op=ALU.add))
            link(v.tensor_scalar(col(C_A), col(C_LONG), 1.0, None, ALU.add))
            link(v.tensor_tensor(col(C_MIDDLE), col(C_MIDDLE), col(C_A), ALU.max))
            link(v.tensor_scalar(row(T_TMP), iotas[:, 0:2 * NE:2], col(C_TOTAL), None, ALU.is_lt))
            link(v.tensor_reduce(col(C_TOTAL), row(T_TMP), axis=AX.X, op=ALU.add))
            link(v.tensor_scalar(col(C_A), col(C_MIDDLE), 2.0, None, ALU.add))
            link(v.tensor_tensor(col(C_TOTAL), col(C_TOTAL), col(C_A), ALU.max))
            link(v.tensor_scalar(n_pairs[:, 3:4], col(C_LONG), -1.0, None, ALU.add))
            link(v.tensor_scalar(n_pairs[:, 0:1], col(C_MIDDLE), -1.0, None, ALU.add))
            link(v.tensor_copy(n_pairs[:, 1:2], col(C_TOTAL)))
            link(v.tensor_scalar(n_pairs[:, 2:3], col(C_TOTAL), -1.0, None, ALU.add))
            accumulator(range(13, 16))
            dve.wait_ge(rows_of_table, 1)
            link(v.tensor_copy(etab[:, :], bank[7][:, 2 * P:2 * P + NTAB]))
            v.tensor_copy(btab[:, :], bank[7][:, 3 * P:3 * P + NTAB]).then_inc(tables_ready, 1)
            dve.wait_ge(tables_ready, 1)
            dve.wait_ge(acc_stored, 16 * NT)
            n0 = n[0]
            STEPS = 7
            def take_y(it, j, slots, chunks=range(NC)):
                for c in chunks:
                    if c and slots == SHORT:
                        continue
                    size = CHUNKS[c][1]
                    wait(dve, y_ready, it * 8 + 4 * j + 2 * c + 1)
                    v.tensor_scalar(ysb[j][0:size, c, 0:HALF], bank[5][0:size, :], sgate[j][0:size, c, :], None,
                                    ALU.mult).then_inc(y_taken_dve, 1 if slots > SHORT else 2)

            def pair(it, slots, slots_before):
                for j in range(2):
                    def chain(ins, q):
                        ins.then_inc(dve_chain, 1)
                        dve.wait_ge(dve_chain, it * (2 * STEPS) + (n0 + j * STEPS + q + 1))

                    e2 = j + 2 if isinstance(it, int) else dve.value_load(etab[0:1, bass.ds(it * 2 + (j + 2), 1)], min_val=0, max_val=NE - 1)
                    wait(dve, list_ready, it * 2 + (j + 2))
                    chain(v.tensor_scalar(iotab[:, :], iotas[:, :], btab[:, bass.ds(it * 2 + (j + 2), 1)], None, ALU.add), 0)
                    make_onehot(e2)
                    wait(dve, sig_ready, it * 2 + (j + 1))
                    chain(v.tensor_tensor(sig[:, :, 0:slots], sig[:, :, 0:slots], bank[3][:, 0:NF * SLOTS].rearrange("p (f s) -> p f s", f=NF)[:, :, 0:slots], ALU.mult), 1)
                    wait(dve, h_ready, it * 2 + j)
                    v.tensor_tensor(h_full[:, :, 0:slots], sig[:, :, 0:slots], bank[4][:, 0:NF * SLOTS].rearrange("p (f s) -> p f s", f=NF)[:, :, 0:slots], ALU.mult).then_inc(h_ready_full, 1)
                    wait(dve, h_hi_ready, it * 2 + (j + 1))
                    v.tensor_tensor(h_lo[j][:, :, 0:slots], h_full[:, :, 0:slots], h_hi[j][:, :, 0:slots].bitcast(f32), ALU.subtract).then_inc(h_ready, 1)
                    behind(lambda it, j, slots, _: take_y(it, j, slots, (0,)), it, j, slots, slots_before)
                    wait(dve, scattered[j], it * 16)
                    if slots_before > SHORT:
                        wait(dve, scattered_rest[j], it * 16)
                    wait(dve, idx_ready, it * 2 + (j + 2))
                    chain(v.tensor_copy(sidx[j][:, :], gidx[j][:, :]), 2)
                    v.tensor_copy(sgate[j][:, :, 0], lst[j][:, :, 1]).then_inc(sidx_ready, 1)
                    wait(dve, list_ready, it * 2 + (j + 3))
                    wait(dve, sidx_ready, it * 2 + (j + 1))
                    wait(dve, gathered[j], it * 16 + 16)
                    if slots_before > SHORT:
                        wait(dve, gathered_rest[j], it * 16 + 16)
                    make_index(j, lambda ins, q: chain(ins, 3 + q))
                    behind(lambda it, j, slots, _: take_y(it, j, slots, (1,)), it, j, slots, slots_before)
                    wait(dve, wd_hi_ready, it * 2 + (j + 1))
                    v.tensor_tensor(wd_lo[:, :, :], W[j][:, 4096:6144].rearrange("p (f d) -> p f d", f=NF),
                                    wd_hi[:, :, :].bitcast(f32), ALU.subtract).then_inc(wd_split, 1)

            pair(0, SLOTS, SLOTS)
            dve.wait_ge(tables_ready, 1)
            long_pairs = dve.value_load(n_pairs[0:1, 3:4], min_val=1, max_val=MAX_PAIRS - 4) + 1
            more_than_short = dve.value_load(n_pairs[0:1, 0:1], min_val=2, max_val=MAX_PAIRS - 3)
            first_short = more_than_short + 1
            pairs = dve.value_load(n_pairs[0:1, 1:2], min_val=5, max_val=MAX_PAIRS)
            with dve.Fori(1, long_pairs) as it:
                pair(it, SLOTS, SLOTS)
            with dve.Fori(long_pairs, first_short) as it:
                pair(it, MIDDLE, SLOTS)
            pair(first_short, SHORT, MIDDLE)
            with dve.Fori(more_than_short + 2, pairs) as it:
                pair(it, SHORT, SHORT)
            last = dve.value_load(n_pairs[0:1, 2:3], min_val=4, max_val=MAX_PAIRS - 1)
            take_y(last, 1, SHORT)
            def affine(t):
                dve.wait_ge(normal_ready, t + 1)
                if t == 0:
                    dve.wait_ge(g2_loaded, 32)
                v.tensor_tensor(accin[:, t, :], accin[:, t, :], g2b[:, :], ALU.mult).then_inc(out_ready, 1)

            for t in range(NT):
                src = accin[:, t, :]
                dve.wait_ge(acc_loaded[t], 16)
                if t:
                    dve.wait_ge(var_ready, 2 * NT + t)
                for h in range(2):
                    v.bn_stats(stats[:, h, :], src[:, h * HALF:(h + 1) * HALF]).then_inc(last_chain, 1)
                dve.wait_ge(last_chain, 3 * t + 2)
                v.bn_aggr(mean_var[:, t, :], small[:, 64:76]).then_inc(var_ready, 1)
                dve.wait_ge(std_ready, 2 * NT + t + 1)
                v.reciprocal(std[:, t:t + 1], std[:, t:t + 1]).then_inc(last_chain, 1)
                dve.wait_ge(last_chain, 3 * t + 3)
                v.scalar_tensor_tensor(small[:, 128 + t:129 + t], mean_var[:, t, 0:1], -1.0, std[:, t:t + 1], ALU.mult, ALU.mult).then_inc(scale_ready, 1)
                if t > 1:
                    affine(t - 2)
            affine(NT - 2)
            affine(NT - 1)
            dve.wait_ge(out_ready, NT)
            v.tensor_tensor(accin[:, NT - 1, :], accin[:, NT - 1, :], b2b[:, :], ALU.add).then_inc(last_scaled, 1)


_INS = ['x', 'ln0_g', 'ln0_b', 'w_in', 'b_in', 'w_pool', 'pool_scale', 'attn_sinks', 'w_br_pool', 'w_br_attn', 'w_out',
        'ln1_g', 'ln1_b', 'w_router', 'router_bias', 'w_exp_gate', 'w_exp_up', 'w_exp_down', 'w_sh_gate', 'w_sh_up',
        'w_sh_down', 'ln2_g', 'ln2_b']


def kernel(**inputs):
    import numpy as _np
    import concourse.bacc as _bacc
    from concourse import mybir as _mybir
    from concourse.bass_utils import run_bass_kernel_spmd as _run

    nc = _bacc.Bacc("TRN2", target_bir_lowering=False, num_devices=1)
    arrays, args = {}, []
    for name in _INS:
        a = _np.ascontiguousarray(inputs[name])
        arrays[f"in_{name}_dram"] = a
        args.append(nc.dram_tensor(f"in_{name}_dram", a.shape, _mybir.dt.from_np(a.dtype), kind="ExternalInput").ap())
    args.append(nc.dram_tensor("out_dram", (1, 1024, 1024), _mybir.dt.float32, kind="ExternalOutput").ap())
    build(nc, *args)
    r = _run(nc, [arrays], core_ids=[0])
    return r.results[0]["out_dram"]
```
